# Optimizing a Trainium2 kernel written in Bass

```python
import math
import jax
import jax.numpy as jnp
from jax import lax
import numpy as np

D_MODEL = 1024
BATCH = 1
SEQ = 512
DEPTH = 1

GRID_W = 64
CTX_LEN = 256

D_SSM = 1024
SSM_HEAD_DIM = 64
SSM_HEADS = D_SSM // SSM_HEAD_DIM
SSM_GROUPS = 2
SSM_STATE = 128
SSM_CONV = 3
SSD_CHUNK = 128

D_HYENA = 1024
HY_ORDER = 2
HY_SHORT = 3
HY_EMB = 33
HY_BANDS = (HY_EMB - 1) // 2
HY_FILTER_WIDTH = 64
HY_DECAY_TARGET = 1e-2
HY_FAST_DECAY = 0.3
HY_SLOW_DECAY = 1.5

N_EXPERTS = 64
TOP_K = 6
N_EXPERT_GROUPS = 8
TOPK_GROUPS = 4
D_EXPERT = 256
D_SHARED = 256
ROUTED_SCALE = 2.5
EXPERT_BLOCK = 128

NORM_EPS = 1e-6
N_ADA = 6

N_XB = D_SSM + SSM_GROUPS * SSM_STATE
N_XBC = D_SSM + 2 * SSM_GROUPS * SSM_STATE
N_DT = 2 * SSM_HEADS
N_Z = D_SSM
N_HY = (HY_ORDER + 1) * D_HYENA
N_GATE = 2 * D_MODEL
N_IN = N_XBC + N_DT + N_Z + N_HY + N_GATE
IN_SPLITS = (N_XBC, N_XBC + N_DT, N_XBC + N_DT + N_Z, N_XBC + N_DT + N_Z + N_HY)

kernel_name = 'hyena_ssd_moe_prefix_dit_block'

F32 = jnp.float32

def rmsnorm(x, g):
    xf = x.astype(F32)
    y = xf * lax.rsqrt(jnp.mean(xf * xf, axis=-1, keepdims=True) + NORM_EPS)
    return (y * g.astype(F32)).astype(x.dtype)

def modulate(h, shift, scale):
    return h * (1 + scale) + shift

def seq_flip(a):
    return jnp.flip(a, axis=1)

def dwconv(u, w, b):
    k = w.shape[0]
    y = lax.conv_general_dilated(u, w[:, None, :].astype(u.dtype), window_strides=(1,),
                                 padding=[(k // 2, k // 2)], dimension_numbers=('NWC', 'WIO', 'NWC'),
                                 feature_group_count=u.shape[-1])
    return y + b.astype(u.dtype)

def gated_rmsnorm(y, z, g):
    v = y.astype(F32) * jax.nn.silu(z.astype(F32))
    shp = v.shape
    v = v.reshape(shp[:-1] + (SSM_GROUPS, shp[-1] // SSM_GROUPS))
    v = v * lax.rsqrt(jnp.mean(v * v, axis=-1, keepdims=True) + NORM_EPS)
    return v.reshape(shp) * g.astype(F32)

def swiglu(x, wg, wu, wd):
    return (jax.nn.silu(x @ wg) * (x @ wu)) @ wd

def ssd_dt(dt_raw, dt_bias):
    b, l, _ = dt_raw.shape
    return jax.nn.softplus(dt_raw.astype(F32).reshape(b, l, 2, SSM_HEADS) + dt_bias.astype(F32))

def _ssd_prep(x, dt, A, B):
    b, l, h, p = x.shape
    g, n = B.shape[-2:]
    c = l // SSD_CHUNK
    xdt = (x.astype(F32) * dt[..., None]).reshape(b, c, SSD_CHUNK, g, h // g, p)
    a_cs = jnp.cumsum((dt * A).reshape(b, c, SSD_CHUNK, g, h // g), axis=2)
    Bc = B.astype(F32).reshape(b, c, SSD_CHUNK, g, n)
    return xdt, a_cs, Bc

def ssd_scan(x, dt, A, B, C, h0):
    b, l, h, p = x.shape
    g, n = B.shape[-2:]
    c = l // SSD_CHUNK
    xdt, a_cs, Bc = _ssd_prep(x, dt, A, B)
    Cc = C.astype(F32).reshape(b, c, SSD_CHUNK, g, n)
    to_end = jnp.exp(a_cs[:, :, -1:] - a_cs)
    chunk_states = jnp.einsum('bcsgn,bcsghp->bcghpn', Bc, xdt * to_end[..., None])
    chunk_decay = jnp.exp(a_cs[:, :, -1])

    def carry_state(state, inp):
        st, dec = inp
        return state * dec[..., None, None] + st, state

    final, s_in = lax.scan(carry_state, h0.astype(F32).reshape(b, g, h // g, p, n),
                           (jnp.moveaxis(chunk_states, 1, 0), jnp.moveaxis(chunk_decay, 1, 0)))
    s_in = jnp.moveaxis(s_in, 0, 1)
    lower = jnp.tril(jnp.ones((SSD_CHUNK, SSD_CHUNK), bool))[:, :, None, None]
    seg = a_cs[:, :, :, None] - a_cs[:, :, None, :]
    decay = jnp.exp(jnp.where(lower, seg, -jnp.inf))
    cb = jnp.einsum('bclgn,bcsgn->bclsg', Cc, Bc)
    y_diag = jnp.einsum('bclsgh,bcsghp->bclghp', cb[..., None] * decay, xdt)
    y_off = jnp.einsum('bclgn,bcghpn->bclghp', Cc, s_in) * jnp.exp(a_cs)[..., None]
    return (y_diag + y_off).reshape(b, l, h, p), final.reshape(b, h, p, n)

def ssd_final_state(x, dt, A, B, h0):
    b, l, h, p = x.shape
    g, n = B.shape[-2:]
    xdt, a_cs, Bc = _ssd_prep(x, dt, A, B)
    la = a_cs[:, :, -1]
    total = jnp.sum(la, axis=1)
    later = total[:, None] - jnp.cumsum(la, axis=1)
    to_end = jnp.exp(a_cs[:, :, -1:] - a_cs + later[:, :, None])
    contrib = jnp.einsum('bcsgn,bcsghp->bghpn', Bc, xdt * to_end[..., None])
    final = jnp.exp(total)[..., None, None] * h0.astype(F32).reshape(b, g, h // g, p, n) + contrib
    return final.reshape(b, h, p, n)

def implicit_filters(L, p):
    pos = jnp.arange(L, dtype=F32)
    t = pos / max(L - 1, 1)
    bands = jnp.linspace(1e-4, HY_BANDS - 1, HY_BANDS, dtype=F32)
    ang = (2.0 * math.pi / L) * pos[:, None] * bands[None, :]
    z = jnp.concatenate([t[:, None], jnp.cos(ang), -jnp.sin(ang)], axis=-1)
    freq = p['hy_freq'].astype(F32)
    hdn = jnp.sin(freq[0] * (z @ p['hy_w1'].astype(F32) + p['hy_b1'].astype(F32)))
    hdn = jnp.sin(freq[1] * (hdn @ p['hy_w2'].astype(F32) + p['hy_b2'].astype(F32)))
    hdn = jnp.sin(freq[2] * (hdn @ p['hy_w3'].astype(F32) + p['hy_b3'].astype(F32)))
    h = (hdn @ p['hy_w_out'].astype(F32)).reshape(L, 2, HY_ORDER, D_HYENA)
    window = jnp.exp(-t[:, None, None] * jnp.abs(p['hy_decay'].astype(F32)))
    return h * window[:, None]

def long_conv(u, h_fwd, h_bwd, skip):
    L = u.shape[1]
    k = jnp.concatenate([h_fwd, jnp.zeros_like(h_fwd[:1]), h_bwd[:0:-1]], axis=0)
    uf = jnp.fft.rfft(u.astype(F32), n=2 * L, axis=1)
    kf = jnp.fft.rfft(k, axis=0)
    y = jnp.fft.irfft(uf * kf[None], n=2 * L, axis=1)[:, :L]
    return (y + u.astype(F32) * skip.astype(F32)).astype(u.dtype)

def hyena(u, p):
    L = u.shape[1]
    u = dwconv(u, p['hy_conv_w'], p['hy_conv_b'])
    parts = jnp.split(u, HY_ORDER + 1, axis=-1)
    z = parts[-1]
    h = implicit_filters(L, p)
    for k in range(HY_ORDER):
        z = parts[k] * long_conv(z, h[:, 0, k], h[:, 1, k], p['hy_bias'][k])
    return z

def mixer(h, p, init_f, init_b):
    b, l, _ = h.shape
    proj = h @ p['w_in']
    xbc, dt_raw, z, hy, gate_logits = jnp.split(proj, IN_SPLITS, axis=-1)
    xbc = jax.nn.silu(dwconv(xbc, p['ssm_conv_w'], p['ssm_conv_b']))
    xs, Bm, Cm = jnp.split(xbc, [D_SSM, N_XB], axis=-1)
    xs = xs.reshape(b, l, SSM_HEADS, SSM_HEAD_DIM)
    Bm = Bm.reshape(b, l, SSM_GROUPS, SSM_STATE)
    Cm = Cm.reshape(b, l, SSM_GROUPS, SSM_STATE)
    dt = ssd_dt(dt_raw, p['ssm_dt_bias'])
    A = -jnp.exp(p['ssm_a_log'].astype(F32))
    y_f, s_f = ssd_scan(xs, dt[:, :, 0], A[0], Bm, Cm, init_f)
    y_b, s_b = ssd_scan(seq_flip(xs), seq_flip(dt[:, :, 1]), A[1], seq_flip(Bm), seq_flip(Cm), init_b)
    y = y_f + seq_flip(y_b) + xs.astype(F32) * p['ssm_d'].astype(F32)[:, None]
    y = gated_rmsnorm(y.reshape(b, l, D_SSM), z, p['ssm_norm_g']).astype(h.dtype)
    ssd_out = y @ p['w_ssm_out']
    hy_out = hyena(hy, p) @ p['w_hy_out']
    g = jax.nn.sigmoid(gate_logits.astype(F32)).astype(h.dtype)
    merged = g[..., :D_MODEL] * hy_out + g[..., D_MODEL:] * ssd_out
    return merged @ p['w_o'], s_f, s_b

def context_states(hc, p, init):
    b, l, _ = hc.shape
    w = jnp.concatenate([p['w_in'][:, :N_XB], p['w_in'][:, N_XBC:N_XBC + N_DT]], axis=1)
    xb, dt_raw = jnp.split(hc @ w, [N_XB], axis=-1)
    xb = jax.nn.silu(dwconv(xb, p['ssm_conv_w'][:, :N_XB], p['ssm_conv_b'][:N_XB]))
    xs = xb[..., :D_SSM].reshape(b, l, SSM_HEADS, SSM_HEAD_DIM)
    Bm = xb[..., D_SSM:].reshape(b, l, SSM_GROUPS, SSM_STATE)
    dt = ssd_dt(dt_raw, p['ssm_dt_bias'])
    A = -jnp.exp(p['ssm_a_log'].astype(F32))
    s_f = ssd_final_state(xs, dt[:, :, 0], A[0], Bm, init)
    s_b = ssd_final_state(seq_flip(xs), seq_flip(dt[:, :, 1]), A[1], seq_flip(Bm), init)
    return s_f, s_b

def route(xf, router_w, router_bias):
    t = xf.shape[0]
    per_group = N_EXPERTS // N_EXPERT_GROUPS
    scores = jax.nn.sigmoid((xf @ router_w).astype(F32))
    sel = scores + router_bias.astype(F32)
    grp_score = jnp.sum(lax.top_k(sel.reshape(t, N_EXPERT_GROUPS, per_group), 2)[0], axis=-1)
    top_groups = lax.top_k(grp_score, TOPK_GROUPS)[1]
    keep = jnp.any(top_groups[:, :, None] == jnp.arange(N_EXPERT_GROUPS)[None, None, :], axis=1)
    sel = jnp.where(jnp.repeat(keep, per_group, axis=1), sel, -jnp.inf)
    idx = lax.top_k(sel, TOP_K)[1]
    w = jnp.take_along_axis(scores, idx, axis=1)
    w = w / jnp.sum(w, axis=-1, keepdims=True) * ROUTED_SCALE
    return idx, w

def routed_experts(xf, idx, w, e_gate, e_up, e_down):
    t, d = xf.shape
    k = idx.shape[1]
    s = t * k
    flat_e = idx.reshape(-1)
    order = jnp.argsort(flat_e)
    sorted_e = flat_e[order]
    counts = jnp.zeros((N_EXPERTS,), jnp.int32).at[flat_e].add(1)
    padded = (counts + EXPERT_BLOCK - 1) // EXPERT_BLOCK * EXPERT_BLOCK
    pad_end = jnp.cumsum(padded)
    pad_start = pad_end - padded
    start = jnp.cumsum(counts) - counts
    dest = pad_start[sorted_e] + jnp.arange(s, dtype=jnp.int32) - start[sorted_e]
    n_rows = -(-s // EXPERT_BLOCK) * EXPERT_BLOCK + N_EXPERTS * EXPERT_BLOCK
    nb = n_rows // EXPERT_BLOCK
    row_tok = jnp.zeros((n_rows,), jnp.int32).at[dest].set((order // k).astype(jnp.int32))
    row_w = jnp.zeros((n_rows,), xf.dtype).at[dest].set(w.reshape(-1)[order].astype(xf.dtype))
    block_e = jnp.minimum(jnp.searchsorted(pad_end, jnp.arange(nb, dtype=jnp.int32) * EXPERT_BLOCK, side='right'),
                          N_EXPERTS - 1)

    def expert_block(acc, blk):
        tok, wt, e = blk
        y = swiglu(xf[tok], e_gate[e], e_up[e], e_down[e])
        return acc.at[tok].add(y * wt[:, None]), None

    out, _ = lax.scan(expert_block, jnp.zeros_like(xf),
                      (row_tok.reshape(nb, EXPERT_BLOCK), row_w.reshape(nb, EXPERT_BLOCK), block_e))
    return out

def moe(h, p):
    b, l, d = h.shape
    xf = h.reshape(b * l, d)
    idx, w = route(xf, p['router_w'], p['router_bias'])
    routed = routed_experts(xf, idx, w, p['e_w_gate'], p['e_w_up'], p['e_w_down'])
    shared = swiglu(xf, p['sh_w_gate'], p['sh_w_up'], p['sh_w_down'])
    return (routed + shared).reshape(b, l, d)

def setup_inputs(seed: int = 0) -> dict:
    key = jax.random.key(seed)
    ks = iter(jax.random.split(key, 48))

    def nrm(shape, scale):
        return jax.random.normal(next(ks), shape, F32) * scale

    nl = DEPTH
    dt0 = jnp.exp(jax.random.uniform(next(ks), (nl, 2, SSM_HEADS), F32, math.log(1e-3), math.log(1e-1)))
    a0 = jax.random.uniform(next(ks), (nl, 2, SSM_HEADS), F32, 1.0, 16.0)
    decay_base = jnp.linspace(math.log(1.0 / HY_DECAY_TARGET) / HY_SLOW_DECAY,
                              math.log(1.0 / HY_DECAY_TARGET) / HY_FAST_DECAY, D_HYENA, dtype=F32)
    return {
        'x': nrm((BATCH, SEQ, D_MODEL), 1.0),
        'c': nrm((BATCH, D_MODEL), 1.0),
        'ctx': nrm((BATCH, CTX_LEN, D_MODEL), 1.0),
        'c_ctx': nrm((D_MODEL,), 1.0),
        'ada_w': nrm((nl, D_MODEL, N_ADA * D_MODEL), 0.5 * D_MODEL ** -0.5),
        'ada_b': nrm((nl, N_ADA * D_MODEL), 0.02),
        'norm1_g': 1.0 + nrm((nl, D_MODEL), 0.02),
        'norm2_g': 1.0 + nrm((nl, D_MODEL), 0.02),
        'w_in': nrm((nl, D_MODEL, N_IN), D_MODEL ** -0.5),
        'ssm_conv_w': nrm((nl, SSM_CONV, N_XBC), SSM_CONV ** -0.5),
        'ssm_conv_b': nrm((nl, N_XBC), 0.02),
        'ssm_dt_bias': dt0 + jnp.log(-jnp.expm1(-dt0)),
        'ssm_a_log': jnp.log(a0),
        'ssm_d': 1.0 + nrm((nl, SSM_HEADS), 0.1),
        'ssm_norm_g': 1.0 + nrm((nl, D_SSM), 0.02),
        'w_ssm_out': nrm((nl, D_SSM, D_MODEL), D_SSM ** -0.5),
        'hy_conv_w': nrm((nl, HY_SHORT, N_HY), HY_SHORT ** -0.5),
        'hy_conv_b': nrm((nl, N_HY), 0.02),
        'hy_w1': nrm((nl, HY_EMB, HY_FILTER_WIDTH), HY_EMB ** -0.5),
        'hy_b1': nrm((nl, HY_FILTER_WIDTH), 0.1),
        'hy_w2': nrm((nl, HY_FILTER_WIDTH, HY_FILTER_WIDTH), HY_FILTER_WIDTH ** -0.5),
        'hy_b2': nrm((nl, HY_FILTER_WIDTH), 0.1),
        'hy_w3': nrm((nl, HY_FILTER_WIDTH, HY_FILTER_WIDTH), HY_FILTER_WIDTH ** -0.5),
        'hy_b3': nrm((nl, HY_FILTER_WIDTH), 0.1),
        'hy_freq': 1.0 + nrm((nl, 3, HY_FILTER_WIDTH), 0.01),
        'hy_w_out': nrm((nl, HY_FILTER_WIDTH, 2 * HY_ORDER * D_HYENA), 0.01),
        'hy_decay': decay_base * (1.0 + nrm((nl, HY_ORDER, D_HYENA), 0.05)),
        'hy_bias': nrm((nl, HY_ORDER, D_HYENA), 0.5),
        'w_hy_out': nrm((nl, D_HYENA, D_MODEL), D_HYENA ** -0.5),
        'w_o': nrm((nl, D_MODEL, D_MODEL), D_MODEL ** -0.5),
        'router_w': nrm((nl, D_MODEL, N_EXPERTS), D_MODEL ** -0.5),
        'router_bias': nrm((nl, N_EXPERTS), 0.01),
        'e_w_gate': nrm((nl, N_EXPERTS, D_MODEL, D_EXPERT), D_MODEL ** -0.5),
        'e_w_up': nrm((nl, N_EXPERTS, D_MODEL, D_EXPERT), D_MODEL ** -0.5),
        'e_w_down': nrm((nl, N_EXPERTS, D_EXPERT, D_MODEL), D_EXPERT ** -0.5),
        'sh_w_gate': nrm((nl, D_MODEL, D_SHARED), D_MODEL ** -0.5),
        'sh_w_up': nrm((nl, D_MODEL, D_SHARED), D_MODEL ** -0.5),
        'sh_w_down': nrm((nl, D_SHARED, D_MODEL), D_SHARED ** -0.5),
        'final_g': 1.0 + nrm((D_MODEL,), 0.02),
    }

def reference(x, c, ctx, c_ctx, ada_w, ada_b, norm1_g, norm2_g, w_in, ssm_conv_w, ssm_conv_b,
              ssm_dt_bias, ssm_a_log, ssm_d, ssm_norm_g, w_ssm_out, hy_conv_w, hy_conv_b,
              hy_w1, hy_b1, hy_w2, hy_b2, hy_w3, hy_b3, hy_freq, hy_w_out, hy_decay, hy_bias,
              w_hy_out, w_o, router_w, router_bias, e_w_gate, e_w_up, e_w_down,
              sh_w_gate, sh_w_up, sh_w_down, final_g):
    bsz = x.shape[0]
    for i in range(DEPTH):
        p = dict(w_in=w_in[i], ssm_conv_w=ssm_conv_w[i], ssm_conv_b=ssm_conv_b[i],
                 ssm_dt_bias=ssm_dt_bias[i], ssm_a_log=ssm_a_log[i], ssm_d=ssm_d[i],
                 ssm_norm_g=ssm_norm_g[i], w_ssm_out=w_ssm_out[i], hy_conv_w=hy_conv_w[i],
                 hy_conv_b=hy_conv_b[i], hy_w1=hy_w1[i], hy_b1=hy_b1[i], hy_w2=hy_w2[i],
                 hy_b2=hy_b2[i], hy_w3=hy_w3[i], hy_b3=hy_b3[i], hy_freq=hy_freq[i],
                 hy_w_out=hy_w_out[i], hy_decay=hy_decay[i], hy_bias=hy_bias[i],
                 w_hy_out=w_hy_out[i], w_o=w_o[i], router_w=router_w[i], router_bias=router_bias[i],
                 e_w_gate=e_w_gate[i], e_w_up=e_w_up[i], e_w_down=e_w_down[i],
                 sh_w_gate=sh_w_gate[i], sh_w_up=sh_w_up[i], sh_w_down=sh_w_down[i])
        mod = (jax.nn.silu(c) @ ada_w[i] + ada_b[i]).reshape(bsz, N_ADA, 1, D_MODEL)
        mod_c = (jax.nn.silu(c_ctx) @ ada_w[i] + ada_b[i]).reshape(N_ADA, D_MODEL)
        hx = modulate(rmsnorm(x, norm1_g[i]), mod[:, 0], mod[:, 1])
        hc = modulate(rmsnorm(ctx, norm1_g[i]), mod_c[0], mod_c[1])
        zero_state = jnp.zeros((bsz, SSM_HEADS, SSM_HEAD_DIM, SSM_STATE), F32)
        if i == DEPTH - 1:
            s_f, s_b = context_states(hc, p, zero_state)
        else:
            ctx_mix, s_f, s_b = mixer(hc, p, zero_state, zero_state)
            ctx = ctx + mod_c[2] * ctx_mix
            ctx = ctx + mod_c[5] * moe(modulate(rmsnorm(ctx, norm2_g[i]), mod_c[3], mod_c[4]), p)
        x_mix, _, _ = mixer(hx, p, s_f, s_b)
        x = x + mod[:, 2] * x_mix
        x = x + mod[:, 5] * moe(modulate(rmsnorm(x, norm2_g[i]), mod[:, 3], mod[:, 4]), p)
    return rmsnorm(x, final_g)


_drawn_inputs = setup_inputs


def setup_inputs(seed=0):
    import zlib

    import numpy as np

    out = dict(_drawn_inputs(seed))
    spreads = {}
    factors = {'norm1_g': 3.4,
     'ssm_conv_b': 25.752,
     'ssm_d': 22.176,
     'ssm_norm_g': 30.8,
     'hy_conv_b': 2.963,
     'hy_freq': 7.753,
     'final_g': 8.211,
     'ctx': 3.654,
     'c_ctx': 6.293,
     'norm2_g': 5.095,
     'router_bias': 3.473}
    for name, (base, spread) in spreads.items():
        noise = np.random.default_rng([zlib.crc32(name.encode()), seed]).standard_normal(out[name].shape)
        drawn = base * np.exp(spread * noise) if base else spread * noise
        out[name] = jnp.asarray(drawn.astype(out[name].dtype))
    for name, factor in factors.items():
        out[name] = (out[name] * factor).astype(out[name].dtype)
    return out
```

```python
from contextlib import ExitStack

import concourse.bass as bass
from concourse import mybir

ALU = mybir.AluOpType
ACT = mybir.ActivationFunctionType
AX = mybir.AxisListType
F32 = mybir.dt.float32
I32 = mybir.dt.int32
U32 = mybir.dt.uint32

P = 128
D = 1024
KD = D // P
L = 512
LT_ = L // P
LC = 256
CT_ = LC // P
TA = LT_ + CT_
HEADS, HD, GROUPS, NS = 16, 64, 2, 128
D_XBC = D + 2 * GROUPS * NS
N_HY = 3 * D
EPS = 1e-6
W_CHUNK = 256
RING = 4
E, TOPK, DE = 64, 6, 256
EG, TOPG = 8, 4
SCALE_R = 2.5
PAIR_STRIDE = 8
PAD_PAIR = L * PAIR_STRIDE
MAX_BLOCKS = E + (L * TOPK - E) // P
NPAIR_IT = (MAX_BLOCKS + 1) // 2
NBLK = 2 * NPAIR_IT + 2
TWO_PI = 6.283185307179586
TP_HI = 6.28125
TP_LO = TWO_PI - TP_HI
ROUND_MAGIC = 12582912.0
PI_SAFE = 3.1415925

COLS = {}
_at = 0
for _n, _w in (("c", 8), ("c_ctx", 8), ("norm1_g", 8), ("norm2_g", 8), ("ada_b", 48), ("ssm_norm_g", 8),
               ("ssm_w", 36), ("ssm_b", 12), ("hy_w", 72), ("hy_b", 24), ("neg_t", 4), ("not_t0", 4),
               ("mlp", 6), ("jcol", 1)):
    COLS[_n] = (_at, _at + _w)
    _at += _w
N_COLS = _at
ADA_EARLY = [("ada", j) for j in range(8)]
XBC_CHUNKS = [("w_in", j) for j in range(6)]
Z_CHUNKS = [("w_in", j) for j in range(6, 10)]
HY_CHUNKS = [("w_in", 10 + j) for j in (8, 9, 10, 11, 0, 1, 2, 3, 4, 5, 6, 7)]
GATE_CHUNKS = [("w_in", 22 + j) for j in range(8)]
HYO_CHUNKS = [("w_hy_out", j) for j in range(4)]
SSO_CHUNKS = [("w_ssm_out", j) for j in range(4)]
ADA_LATE = [("ada", j) for j in range(8, 24)]
WO_CHUNKS = [("w_o", j) for j in range(4)]
RING_ITEMS = (ADA_EARLY + XBC_CHUNKS + Z_CHUNKS + HY_CHUNKS + GATE_CHUNKS + HYO_CHUNKS + SSO_CHUNKS
              + ADA_LATE + WO_CHUNKS)
AT_ADA1 = 0
AT_XBC = AT_ADA1 + 8
AT_Z = AT_XBC + 6
AT_HY = AT_Z + 4
AT_GATE = AT_HY + 12
AT_HYO = AT_GATE + 8
AT_SSO = AT_HYO + 4
AT_ADA2 = AT_SSO + 4
AT_WO = AT_ADA2 + 16
N_RING = AT_WO + 4
assert N_RING == len(RING_ITEMS)

SSM_TILES = []
for _m in range(12):
    _kind = ("xs", _m) if _m < 8 else ("B", _m - 8) if _m < 10 else ("C", _m - 10)
    SSM_TILES.append((AT_XBC + _m // 2, _m % 2, "ssm", _m, False) + _kind)
    if _m < 10:
        SSM_TILES.append((AT_XBC + _m // 2, _m % 2, "ssm", _m, True) + _kind)
HY_TILES = []
for _i in range(24):
    _part, _m = ("v", _i) if _i < 8 else ("p0", _i - 8) if _i < 16 else ("p1", _i - 16)
    _conv = {"v": 16, "p0": 0, "p1": 8}[_part] + _m
    HY_TILES.append((AT_HY + _i // 2, _i % 2, "hy", _conv, False, _part, _m))


def col(cols, name, i=0, n=1):
    at = COLS[name][0] + i
    return cols[:, at:at + n]


def over(ap, n):
    return ap.unsqueeze(2).to_broadcast([ap.shape[0], ap.shape[1], n])


def each(ap, n):
    return ap.unsqueeze(1).to_broadcast([ap.shape[0], n, ap.shape[1]])


def build(nc, d):
    with ExitStack() as ctx:
        arena_len = 53200
        arena = ctx.enter_context(nc.sbuf_tensor("arena", [P, arena_len], F32))
        ps = ctx.enter_context(nc.psum_tensor("ps", [P, 8, 512], F32))

        class Region:

            def __init__(self, at):
                self.at = at

            def take(self, *shape, parts=P, dtype=F32):
                n = 1
                for s in shape:
                    n *= s
                v = arena[0:parts, self.at:self.at + n]
                self.at += n
                assert self.at <= arena_len, self.at
                if dtype is not F32:
                    v = v.bitcast(dtype)
                if len(shape) == 1:
                    return v
                names = "abcd"[:len(shape)]
                sizes = {k: s for k, s in zip(names, shape)}
                return v.rearrange(f"p ({' '.join(names)}) -> p {' '.join(names)}", **sizes)

        fixed = Region(0)
        ident = fixed.take(P)
        tri_le, tri_gt, tri_ge, tri_lt = (fixed.take(P) for _ in range(4))
        ones = fixed.take(P)
        cols = fixed.take(N_COLS + N_COLS % 2)
        silu_c = fixed.take(KD, 2)
        mod = fixed.take(48, 2)
        scale1 = fixed.take(KD, 2)
        scale2 = fixed.take(KD)
        small = fixed.take(64)
        ring_at = fixed.at
        ring = fixed.take(RING, KD, W_CHUNK)
        yT = fixed.take(KD, L)
        hT = fixed.take(KD, L + LC)
        phase_at = fixed.at

        r = Region(phase_at)
        xin = r.take(TA, D)
        junk = r.take(D)
        modrow = r.take(2, W_CHUNK, parts=2)

        r = Region(phase_at)
        xs_tok = r.take(TA, D)
        BT = r.take(GROUPS, L)
        CT = r.take(GROUPS, L)
        B_tok = r.take(TA, GROUPS * NS)
        zs = r.take(LT_, D)
        xdt = r.take(2, 2, D)
        xdte = r.take(D)
        sb_in = r.take(LT_, D)
        sf_in = r.take(D)
        seg_rhs = r.take(2, 4, P)
        decay = r.take(2, 2, 4, P)
        cbm = r.take(2, LT_, GROUPS, P)
        acc = decay.rearrange("p a b c e -> p (a b c e)")[:, 0:3 * L].rearrange("p (a b) -> p a b", a=3)
        squares = r.take(512)
        y1 = r.take(D)
        y2 = r.take(D)
        w_dt = y1[:, 0:KD * 32].rearrange("p (k n) -> p k n", k=KD)
        dtw = xdte[:, 0:5 * 192].rearrange("p (w t n) -> p w t n", w=5, t=TA)
        dt_tok = r.take(TA, 32)
        a_tok = r.take(TA, 32)
        ecs = r.take(TA, 96)
        dte = r.take(TA, 32)
        rows_ssd = r.take(80)
        v_ss = small[:, 0:8]
        v_rstd = small[:, 8:16]
        ssd_end = r.at

        r = Region(phase_at)
        dft = r.take(2, 2, LT_, L)
        v_tok = r.take(LT_, D)
        p0_tok = r.take(LT_, D)
        p1T = r.take(KD, L)
        filt = r.take(2, LT_, 512)
        spec = r.take(2, LT_, 512)
        w_f = r.take(2, 512, parts=64)
        hdnT = r.take(L, parts=64)
        hy_w1 = r.take(64, parts=33)
        hy_w23 = r.take(2, 64, parts=64)
        decay_row = r.take(512)
        skip_row = r.take(512, parts=1)
        window = r.take(2, 512)
        h_bwd = r.take(2, 512)
        acc_hy = spec[:, 0, 0:3, :]
        zpos = filt[0:33, 0, 0, :]
        sin_arg, sin_n, sin_r = (filt[0:64, 0, 1 + i, :] for i in range(3))
        prod = h_bwd

        r = Region(phase_at)
        gates = r.take(2, KD, L)
        mergedT = r.take(KD, L)
        x1 = r.take(LT_, D)
        after_x1 = r.at
        r.take(KD, L)
        rows = r.take(4, D)
        h2 = r.take(LT_, D)
        squares2 = r.take(D)
        modrow_late = r.take(2, W_CHUNK, parts=2)
        xmix = r.take(2, W_CHUNK)
        router_w = r.take(KD, E)
        bias_row = r.take(E)
        iota_row = r.take(E)
        pair_ids = r.take(LT_ * TOPK, dtype=I32)

        r = Region(ring_at)
        gu_w = r.take(3, KD, 2 * DE)
        down_w = r.take(3, 2, D)
        assert r.at <= phase_at
        h2T = r.take(KD, L)
        shg = r.take(2, L)
        sg = r.take(2, DE)
        hh = r.take(2, DE)
        hhT = r.take(2, 2, P)
        yo = r.take(2, D)
        scores = r.take(LT_, E)
        sel = r.take(LT_, E + 8)
        grp8 = r.take(EG, 8)
        grp = r.take(16)
        grp_top = r.take(8)
        grp_rep = r.take(8)
        grp_mark = r.take(16)
        keep = r.take(8)
        drop = r.take(8)
        top8 = r.take(LT_, 8)
        top_rep = r.take(8)
        marked = r.take(E + 8)
        mask = r.take(LT_, E)
        idx_u = r.take(LT_, 8, dtype=U32)
        idx_f = r.take(LT_, 8)
        w_tok = r.take(LT_, TOPK)
        w_sum = r.take(LT_)
        counts = r.take(E)
        nblk = r.take(E)
        cend = r.take(E)
        base = r.take(E)
        rank = r.take(LT_, E)
        over_b = r.take(LT_, E)
        dest = r.take(LT_, E)
        picked = r.take(E)
        dest_k = r.take(LT_, TOPK)
        dest_i = r.take(LT_ * TOPK, dtype=I32)
        ecol = r.take(2)
        erow = r.take(P, dtype=I32, parts=1)
        nstep = r.take(4, dtype=I32, parts=1)
        nstep_f = r.take(4, parts=1)
        pad_tab = r.take(NBLK, dtype=I32)
        slots = r.take(NBLK, dtype=I32)
        tokens = r.take(NBLK, dtype=I32)
        idx_g = r.take(2, 1, dtype=I32)
        idx_s = r.take(2, 1, dtype=I32)
        onehot = r.take(TOPK, E)
        assert r.at <= phase_at + 3 * KD * L, r.at
        r = Region(after_x1)
        xg = r.take(2, D)
        xgT = r.take(2, KD, P)
        chosen = xgT[:, 0].rearrange("p k n -> p (k n)")[:, 0:2 * TOPK * E].rearrange(
            "p (a k e) -> p a k e", a=2, k=TOPK)
        y_in = Region(ring_at).take(2, TOPK, D)
        acc2 = Region(phase_at).take(2, D)
        fin_row = h2[:, 0]
        x_out = [h2[:, 1], h2[:, 2], h2[:, 3], rows[:, 0]]

        def sem(name):
            return ctx.enter_context(nc.semaphore(name))

        s_const = sem("constants_loaded")
        s_x = sem("x_loaded")
        s_ring = [sem(f"ring_loaded_{i}") for i in range(RING)]
        s_pe = sem("phases_ended")
        s_silu_c = sem("silu_c_ready")
        s_modmm = sem("mod_rows_summed")
        s_modrow = sem("mod_row_copied")
        s_modtr = sem("mod_rows_turned")
        s_mod = sem("mod_columns_ready")
        s_ss = sem("x_squares_summed")
        s_rs = sem("x_rstd_step")
        s_xn = sem("x_normalised")
        s_htr = sem("h_turned")
        s_hT = sem("hT_written")
        s_proj = sem("tile_projected")
        s_cva = sem("conv_centre_done")
        s_cvm = sem("conv_left_done")
        s_cv = sem("conv_done")
        s_sl = sem("silu_done")
        s_tr = sem("tile_turned")
        s_te = sem("turned_tile_copied")
        s_w_dt = sem("w_dt_loaded")
        s_dtmm = sem("dt_projected")
        s_dt = sem("dt_steps")
        s_dta = sem("dt_act_steps")
        s_zmm = sem("z_projected")
        s_z = sem("z_silu_done")
        s_cs = sem("cumulative_sums_done")
        s_ecs = sem("decays_ready")
        s_cb = sem("cb_done")
        s_cbm = sem("cb_masked")
        s_dte = sem("dt_to_end_ready")
        s_xe = sem("xdte_ready")
        s_st = sem("chunk_state_done")
        s_stu = sem("state_updated")
        s_xdt = sem("xdt_ready")
        s_rhs = sem("segment_rhs_ready")
        s_seg = sem("segments_summed")
        s_exp = sem("segments_exponentiated")
        s_msk = sem("decay_masked")
        s_y = sem("y_quad_done")
        s_off = sem("y_off_done")
        s_offr = sem("y_off_read")
        s_dve = sem("vector_steps")
        s_yc = sem("chunk_gated")
        s_vss = sem("gated_squares_summed")
        s_vr = sem("gated_rstd_ready")
        s_vn = sem("gated_normalised")
        s_ytr = sem("y_turned")
        s_yT = sem("yT_written")
        s_hyin = sem("filter_network_loaded")
        s_fb = sem("freq_bias_ready")
        s_mlp = sem("filter_layer_summed")
        s_arg = sem("sine_argument_ready")
        s_red = sem("sine_argument_reduced")
        s_sin = sem("sine_done")
        s_dft = sem("dft_tables_loaded")
        s_rows = sem("filter_rows_loaded")
        s_drow = sem("decay_row_positive")
        s_fmm = sem("filter_tile_summed")
        s_win = sem("window_ready")
        s_hb = sem("backward_filter_copied")
        s_fd = sem("filter_parts_ready")
        s_fp = sem("filter_windowed")
        s_kmm = sem("filter_spectrum_summed")
        s_kev = sem("filter_spectrum_copied")
        s_umm = sem("signal_spectrum_summed")
        s_um = sem("spectra_multiplied")
        s_ua = sem("product_ready")
        s_imm = sem("time_tile_summed")
        s_iv = sem("time_tile_gated")
        s_mp = sem("merge_tile_summed")
        s_gt = sem("gate_ready")
        s_mg = sem("merge_tile_gated")
        s_mga = sem("merged_ready")
        s_x1l = sem("residual_loaded")
        s_mod2 = sem("late_modulation_ready")
        s_rowmm = sem("modulation_row_spread")
        s_row = sem("modulation_row_copied")
        s_xmm = sem("mixer_output_summed")
        s_x1 = sem("residual_updated")
        s_ss2 = sem("residual_squares_summed")
        s_rs2 = sem("residual_rstd_step")
        s_h2 = sem("h2_ready")
        s_h2st = sem("h2_stored")
        s_h2t = sem("h2_turned")
        s_h2T = sem("h2T_written")
        s_rw = sem("router_loaded")
        s_lg = sem("logits_summed")
        s_sc0 = sem("scores_ready")
        s_msk2 = sem("expert_mask_ready")
        s_rk = sem("ranks_summed")
        s_be = sem("block_experts_ready")
        s_bt = sem("block_experts_turned")
        s_brow = sem("block_row_ready")
        s_dst = sem("slots_ready")
        s_pad = sem("slot_table_padded")
        s_scat = sem("pairs_scattered")
        s_slot = sem("slot_table_loaded")
        s_tok = sem("token_table_ready")
        s_shl = sem("shared_weights_loaded")
        s_shm = sem("shared_hidden_summed")
        s_sha = sem("shared_silu_done")
        s_shh = sem("shared_hidden_ready")
        s_shy = sem("shared_output_summed")
        s_shx = sem("shared_output_added")
        s_pi = sem("pool_index_ready")
        s_pseen = sem("pool_waits_met")
        s_gu = sem("block_hidden_summed")
        s_sg = sem("block_silu_done")
        s_h = sem("block_hidden_ready")
        s_th = sem("hidden_turned")
        s_hte = sem("hiddenT_copied")
        s_xt = sem("rows_turned")
        s_xea = sem("rowsT_low_copied")
        s_xeb = sem("rowsT_high_copied")
        s_ym = sem("block_output_summed")
        s_yea = sem("output_low_copied")
        s_yeb = sem("output_high_copied")
        s_fl = sem("final_gain_loaded")
        s_cmb = sem("token_sum_ready")
        s_ss3 = sem("final_squares_summed")
        s_rs3 = sem("final_rstd_step")
        s_fo = sem("output_tile_ready")
        s_xz = sem("rows_cleared")
        s_gul = [sem(f"gate_up_loaded_{u}") for u in range(2)]
        s_dnl = [sem(f"down_loaded_{u}") for u in range(2)]
        s_xg = [sem(f"rows_gathered_{u}") for u in range(2)]
        s_sca = [sem(f"outputs_scattered_{u}") for u in range(2)]
        s_yl = [sem(f"token_outputs_loaded_{u}") for u in range(2)]
        s_out = sem("stores_done")

        def bank(b):
            return ps[:, b, :]

        h2_dram = nc.dram_tensor("h2_rows", (L, D), F32, kind="Internal").ap()
        y_dram = nc.dram_tensor("pair_outputs", (L * PAIR_STRIDE, D), F32, kind="Internal").ap()
        slot_dram = nc.dram_tensor("slot_table", (P * NBLK, 1), I32, kind="Internal").ap()

        freed = {}
        for j in range(8):
            freed[AT_ADA1 + j] = (s_modmm, j + 1)
        for g, t in enumerate(SSM_TILES):
            freed[t[0]] = (s_proj, g + 1)
        for j in range(4):
            freed[AT_Z + j] = (s_zmm, LT_ * (j + 1))
        for g, t in enumerate(HY_TILES):
            freed[t[0]] = (s_proj, len(SSM_TILES) + g + 1)

        for n in range(32):
            freed[AT_GATE + n // 2] = (s_mp, n + 1)
        for n in range(8, 24):
            freed[AT_ADA2 + n - 8] = (s_modmm, n + 1)
        tiles = SSM_TILES + HY_TILES

        def ring_wait(eng, item):
            eng.wait_ge(s_ring[item % RING], 16 * (item // RING + 1))

        def phase_end(eng, n):
            eng.sem_inc(s_pe, 1)
            eng.wait_ge(s_pe, 4 * n)

        SSM_TURNED = sum(t[5] != "C" for t in SSM_TILES)
        DT_READY = 4
        STATE_UPDATES = [(0, 4), (0, 5), (1, 5), (1, 4), (1, 3), (1, 2), (1, 1), (0, 0), (0, 1), (0, 2)]

        def turned_before(g):
            return sum(t[5] in ("xs", "B", "v", "p0") for t in tiles[:g])

        def silu_before(g):
            return sum(t[2] == "ssm" for t in tiles[:g])

        def in_ring(t):
            return t[5] in ("xs", "v", "p0") or (t[5] == "B" and t[4])

        def conv_out(g):
            item, c, conv, ct, is_ctx, what, m = tiles[g]
            n = LC if is_ctx else L
            if in_ring(tiles[g]):
                return (acc if conv == "ssm" else acc_hy)[:, sum(map(in_ring, tiles[:g])) % 3, 0:n]
            return {"B": BT, "C": CT, "p1": p1T}[what][:, m, :]

        def conv_pe(pe, g0, g1, first):
            for g in range(g0, g1):
                item, c, conv, ct, is_ctx, what, m = tiles[g]
                n, t0 = (LC, L) if is_ctx else (L, 0)
                ring_wait(pe, item)
                if g >= first + 4:
                    pe.wait_ge(s_cv, g - 3)
                for k in range(KD):
                    mm = nc.tensor.matmul(bank(g % 4)[:, 0:n], ring[:, item % RING, k, c * P:(c + 1) * P],
                                          hT[:, k, t0:t0 + n], start=(k == 0), stop=(k == KD - 1))
                mm.then_inc(s_proj, 1)
                if g > g0:
                    turn_pe(pe, g - 1, first)
            turn_pe(pe, g1 - 1, first)

        def turn_pe(pe, g, first):
            t = tiles[g]
            if t[5] not in ("xs", "B", "v", "p0"):
                return
            j = turned_before(g)
            if t[2] == "ssm":
                pe.wait_ge(s_sl, silu_before(g) + 1)
            else:
                pe.wait_ge(s_cv, g + 1)
            if j >= turned_before(first) + 2:
                pe.wait_ge(s_te, j - 1)
            for i in range(CT_ if t[4] else LT_):
                mm = nc.tensor.transpose(bank(4 + j % 2)[:, i * P:(i + 1) * P],
                                         conv_out(g)[:, i * P:(i + 1) * P], ident)
            mm.then_inc(s_tr, 1)

        def conv_act(act, g0, g1, first):
            for g in range(g0, g1):
                item, c, conv, ct, is_ctx, what, m = tiles[g]
                out = conv_out(g)
                act.wait_ge(s_proj, g + 1)
                if in_ring(tiles[g]):
                    before = [h for h in range(first, g) if in_ring(tiles[h])]
                    if len(before) >= 3:
                        act.wait_ge(s_tr, turned_before(before[-3]) + 1)
                ctn = 12 if conv == "ssm" else 24
                nc.scalar.activation(out, bank(g % 4)[:, 0:out.shape[1]], ACT.Identity,
                                     scale=col(cols, conv + "_w", ctn + ct),
                                     bias=col(cols, conv + "_b", ct)).then_inc(s_cva, 1)
                if conv == "ssm":
                    act.wait_ge(s_cv, g + 1)
                    nc.scalar.activation(out, out, ACT.Silu).then_inc(s_sl, 1)
                if g > g0:
                    turned_act(act, g - 1)
            turned_act(act, g1 - 1)

        def turned_act(act, g):
            t = tiles[g]
            if t[5] not in ("xs", "B", "v", "p0"):
                return
            j = turned_before(g)
            n, t0 = (CT_, LT_) if t[4] else (LT_, 0)
            dst = {"xs": xs_tok, "B": B_tok, "v": v_tok, "p0": p0_tok}[t[5]]
            act.wait_ge(s_tr, j + 1)
            nc.scalar.copy(dst[:, t0:t0 + n, t[6] * P:(t[6] + 1) * P],
                           bank(4 + j % 2)[:, 0:n * P].rearrange("p (t c) -> p t c", c=P)).then_inc(s_te, 1)

        def conv_dve(dve, g0, g1):
            for g in range(g0, g1):
                item, c, conv, ct, is_ctx, what, m = tiles[g]
                out, ctn = conv_out(g), 12 if conv == "ssm" else 24
                n = out.shape[1]
                dve.wait_ge(s_cva, g + 1)
                nc.vector.scalar_tensor_tensor(out[:, 1:n], bank(g % 4)[:, 0:n - 1], col(cols, conv + "_w", ct),
                                               out[:, 1:n], ALU.mult, ALU.add).then_inc(s_cvm, 1)
                dve.wait_ge(s_cvm, g + 1)
                nc.vector.scalar_tensor_tensor(out[:, 0:n - 1], bank(g % 4)[:, 1:n],
                                               col(cols, conv + "_w", 2 * ctn + ct), out[:, 0:n - 1],
                                               ALU.mult, ALU.add).then_inc(s_cv, 1)

        def row_buf(n):
            return modrow if n < 8 else modrow_late

        def mod_chunk(pe, n, item):
            ring_wait(pe, item)
            if n == 0:
                pe.wait_ge(s_silu_c, 2)
            if n >= 2:
                pe.wait_ge(s_modrow, n - 1)
            for k in range(KD):
                mm = nc.tensor.matmul(bank(n % 2)[0:2, 0:W_CHUNK], silu_c[:, k, :], ring[:, item % RING, k, :],
                                      start=(k == 0), stop=(k == KD - 1))
            mm.then_inc(s_modmm, 1)
            if n >= 1 and n != 8:
                mod_turn(pe, n - 1)
            if n in (7, 23):
                mod_turn(pe, n)

        def mod_turn(pe, n):
            pe.wait_ge(s_modrow, n + 1)
            for i in range(2):
                mm = nc.tensor.transpose(bank(2)[:, 2 * (2 * n + i):2 * (2 * n + i) + 2],
                                         row_buf(n)[0:2, n % 2, i * P:(i + 1) * P], ident[0:2, 0:2])
            mm.then_inc(s_modtr, 1)

        def mod_rows_act(act, n0, n1):
            for n in range(n0, n1):
                act.wait_ge(s_modmm, n + 1)
                if n >= n0 + 2:
                    act.wait_ge(s_modtr, n - 1)
                nc.scalar.copy(row_buf(n)[0:2, n % 2, :], bank(n % 2)[0:2, 0:W_CHUNK]).then_inc(s_modrow, 1)

        def pool_xdte(pool, u, dirn, c):
            if u == 0:
                pool.wait_ge(s_dte, 1)
                pool.wait_ge(s_te, SSM_TURNED)
            else:
                pool.wait_ge(s_st, u)
            nc.gpsimd.tensor_tensor(xdte.rearrange("p (h e) -> p h e", e=HD),
                                    xs_tok[:, c].rearrange("p (h e) -> p h e", e=HD),
                                    over(dte[:, c, 16 * dirn:16 * dirn + 16], HD), ALU.mult).then_inc(s_xe, 1)

        def state_pe(pe, u):
            dirn, c = STATE_UPDATES[u]
            pe.wait_ge(s_xe, u + 1)
            if u < 7:
                if u >= 1:
                    pe.wait_ge(s_stu, u)
            else:
                pe.wait_ge(s_offr, 2 * (u - 7) + 2)
            for g in range(GROUPS):
                mm = nc.tensor.matmul(bank(4 + g), B_tok[:, c, g * NS:(g + 1) * NS],
                                      xdte[:, g * 512:(g + 1) * 512], start=True, stop=True)
            mm.then_inc(s_st, 1)

        def state_dve(dve, link, u):
            dirn, c = STATE_UPDATES[u]
            new = ps[:, 4:6, :].rearrange("p b (h e) -> p (b h) e", e=HD)
            heads = lambda ap: ap.rearrange("p (h e) -> p h e", e=HD)
            src, dst = {0: (None, sf_in), 1: (sf_in, sf_in), 2: (None, sb_in[:, 3]),
                        3: (sb_in[:, 3], sb_in[:, 3]), 4: (sb_in[:, 3], sb_in[:, 2]),
                        5: (sb_in[:, 2], sb_in[:, 1]), 6: (sb_in[:, 1], sb_in[:, 0])}.get(u, (sf_in, sf_in))
            dve.wait_ge(s_st, u + 1)
            if src is None:
                nc.vector.tensor_copy(heads(dst), new).then_inc(s_stu, 1)
            else:
                link(nc.vector.tensor_tensor(heads(dst), heads(src),
                                             over(ecs[:, c, 64 + 16 * dirn:80 + 16 * dirn], HD), ALU.mult))
                nc.vector.tensor_tensor(heads(dst), new, heads(dst), ALU.add).then_inc(s_stu, 1)
            dve.wait_ge(s_stu, u + 1)

        def off_pe(pe, c, dirn):
            if dirn == 0:
                pe.wait_ge(s_stu, 7 + c)
            else:
                pe.wait_ge(s_offr, 2 * c + 1)
            state = sb_in[:, c] if dirn else sf_in
            for g in range(GROUPS):
                mm = nc.tensor.matmul(bank(4 + g), CT[:, g, c * P:(c + 1) * P],
                                      state[:, g * 512:(g + 1) * 512], start=True, stop=True)
            mm.then_inc(s_off, 1)

        def quad_pe(pe, n):
            c, q = n // 4, n % 4
            pe.wait_ge(s_msk, 2 * n + 2)
            if q == 0:
                pe.wait_ge(s_xdt, 2 * c + 2)
                if c >= 1:
                    pe.wait_ge(s_yc, c)
            for i in range(4):
                h = 4 * q + i
                for dirn in range(2):
                    mm = nc.tensor.matmul(bank(6 + h // 8)[:, (h % 8) * HD:(h % 8 + 1) * HD],
                                          decay[:, n % 2, dirn, i, :], xdt[:, c % 2, dirn, h * HD:(h + 1) * HD],
                                          start=(dirn == 0), stop=(dirn == 1))
            mm.then_inc(s_y, 1)

        def gate_squares(act, c):
            act.wait_ge(s_yc, c + 1)
            for g in range(GROUPS):
                if 2 * c + g >= 1:
                    act.wait_ge(s_vss, 2 * c + g)
                nc.scalar.activation(squares, zs[:, c, g * 512:(g + 1) * 512], ACT.Square,
                                     accum_out=v_ss[:, 2 * c + g:2 * c + g + 1]).then_inc(s_vss, 1)

        HY_STEPS = [(half, o) for half in range(2) for o in range(2)]
        N_SSM, N_ALL = len(SSM_TILES), len(tiles)

        def mlp_pe(pe, layer):
            if layer == 0:
                pe.wait_ge(s_hyin, 48)
                nc.tensor.matmul(bank(6)[0:64, :], hy_w1, zpos, start=True, stop=True).then_inc(s_mlp, 1)
            else:
                pe.wait_ge(s_sin, layer)
                nc.tensor.matmul(bank(6)[0:64, :], hy_w23[:, layer - 1, :], hdnT, start=True,
                                 stop=True).then_inc(s_mlp, 1)

        def mlp_act(act, layer):
            if layer == 0:
                act.wait_ge(s_fb, 1)
            act.wait_ge(s_mlp, layer + 1)
            nc.scalar.activation(sin_arg, bank(6)[0:64, :], ACT.Identity, scale=col(cols, "mlp", 3 + layer)[0:64],
                                 bias=small[0:64, 48 + layer:49 + layer]).then_inc(s_arg, 1)
            act.wait_ge(s_red, layer + 1)
            nc.scalar.activation(hdnT, sin_r, ACT.Sin).then_inc(s_sin, 1)

        def mlp_dve(dve, link, layer):
            dve.wait_ge(s_arg, layer + 1)
            link(nc.vector.tensor_scalar(sin_n, sin_arg, 1.0 / TWO_PI, ROUND_MAGIC, ALU.mult, ALU.add))
            link(nc.vector.tensor_scalar(sin_n, sin_n, ROUND_MAGIC, None, ALU.subtract))
            link(nc.vector.scalar_tensor_tensor(sin_r, sin_n, -TP_HI, sin_arg, ALU.mult, ALU.add))
            link(nc.vector.scalar_tensor_tensor(sin_r, sin_n, -TP_LO, sin_r, ALU.mult, ALU.add))
            nc.vector.tensor_scalar(sin_r, sin_r, PI_SAFE, -PI_SAFE, ALU.min, ALU.max).then_inc(s_red, 1)

        def rows_dma(act, s):
            half, o = HY_STEPS[s]
            c0 = o * D + half * 512
            if s >= 1:
                act.wait_ge(s_fmm, 4 * s)
                act.wait_ge(s_fd, 4 * s)
                act.wait_ge(s_win, 4 * s)
            src = d["hy_w_out"].rearrange("p (a n) -> p a n", a=2)[:, :, c0:c0 + 512]
            act.dma_start(w_f, src).then_inc(s_rows, 16)
            act.dma_start(decay_row, d["hy_decay"][c0:c0 + 512].partition_broadcast(P)).then_inc(s_rows, 16)
            act.dma_start(skip_row, d["hy_bias"][c0:c0 + 512].partition_broadcast(1)).then_inc(s_rows, 16)

        def filter_pe(pe, s):
            pe.wait_ge(s_rows, 48 * (s + 1))
            for ti in range(LT_):
                i = 4 * s + ti
                if i >= 2:
                    pe.wait_ge(s_fd, i - 1)
                if ti == 0 and s >= 1:
                    pe.wait_ge(s_um, 4 * s)
                for a in range(2):
                    mm = nc.tensor.matmul(bank(2 * (i % 2) + a), hdnT[:, ti * P:(ti + 1) * P], w_f[:, a, :],
                                          start=True, stop=True)
                mm.then_inc(s_fmm, 1)

        def filter_act(act, s):
            for ti in range(LT_):
                i = 4 * s + ti
                if ti == 0:
                    act.wait_ge(s_drow, s + 1)
                if i >= 2:
                    act.wait_ge(s_fp, i - 1)
                nc.scalar.activation(window[:, i % 2, :], decay_row, ACT.Exp,
                                     scale=col(cols, "neg_t", ti)).then_inc(s_win, 1)
                act.wait_ge(s_fmm, i + 1)
                if i >= 2:
                    act.wait_ge(s_fd, i - 1)
                if ti == 0 and s >= 1:
                    act.wait_ge(s_ua, 4 * s)
                nc.scalar.activation(h_bwd[:, i % 2, :], bank(2 * (i % 2) + 1), ACT.Identity,
                                     scale=col(cols, "not_t0", ti)).then_inc(s_hb, 1)
            if s < 3:
                rows_dma(act, s + 1)

        def filter_dve(dve, link, s):
            dve.wait_ge(s_rows, 48 * (s + 1))
            nc.vector.scalar_tensor_tensor(decay_row, decay_row, -1.0, decay_row, ALU.mult,
                                           ALU.max).then_inc(s_drow, 1)
            for ti in range(LT_):
                i = 4 * s + ti
                dve.wait_ge(s_hb, i + 1)
                if ti == 0 and s >= 1:
                    dve.wait_ge(s_imm, 4 * s)
                f = bank(2 * (i % 2))
                if ti == 0:
                    link(nc.vector.tensor_tensor(filt[:, 0, ti, :], f, h_bwd[:, i % 2, :], ALU.add))
                    nc.vector.tensor_tensor(filt[0:1, 0, 0, :], filt[0:1, 0, 0, :], skip_row, ALU.add)
                else:
                    nc.vector.tensor_tensor(filt[:, 0, ti, :], f, h_bwd[:, i % 2, :], ALU.add)
                nc.vector.tensor_tensor(filt[:, 1, ti, :], f, h_bwd[:, i % 2, :], ALU.subtract).then_inc(s_fd, 1)

        def filter_pool(pool, s):
            for ti in range(LT_):
                i = 4 * s + ti
                pool.wait_ge(s_fd, i + 1)
                pool.wait_ge(s_win, i + 1)
                nc.gpsimd.tensor_tensor(filt[:, :, ti, :], filt[:, :, ti, :], each(window[:, i % 2, :], 2),
                                        ALU.mult).then_inc(s_fp, 1)

        def spectrum_pe(pe, s):
            pe.wait_ge(s_fp, 4 * (s + 1))
            for ft in range(LT_):
                j = 4 * s + ft
                if ft == 0 and s >= 1:
                    pe.wait_ge(s_iv, 4 * s)
                if j >= 2:
                    pe.wait_ge(s_kev, j - 1)
                for a in range(2):
                    for ti in range(LT_):
                        mm = nc.tensor.matmul(bank(4 + 2 * (j % 2) + a), dft[:, 0, a, ti, ft * P:(ft + 1) * P],
                                              filt[:, a, ti, :], start=(ti == 0), stop=(ti == LT_ - 1))
                mm.then_inc(s_kmm, 1)

        def spectrum_act(act, s):
            for ft in range(LT_):
                j = 4 * s + ft
                if ft == 0 and s >= 1:
                    act.wait_ge(s_um, 4 * s)
                act.wait_ge(s_kmm, j + 1)
                nc.scalar.copy(spec[:, :, ft, :], ps[:, 4 + 2 * (j % 2):6 + 2 * (j % 2), :]).then_inc(s_kev, 1)

        def signal_pe(pe, s):
            half, o = HY_STEPS[s]
            pe.wait_ge(s_fd, 4 * (s + 1))
            for ft in range(LT_):
                j = 4 * s + ft
                if j >= 2:
                    pe.wait_ge(s_um, j - 1)
                for a in range(2):
                    for ti in range(LT_):
                        mm = nc.tensor.matmul(bank(2 * (j % 2) + a), dft[:, 0, a, ti, ft * P:(ft + 1) * P],
                                              v_tok[:, ti, half * 512:(half + 1) * 512],
                                              start=(ti == 0), stop=(ti == LT_ - 1))
                mm.then_inc(s_umm, 1)

        def product_dve(dve, s):
            for ft in range(LT_):
                j = 4 * s + ft
                uc, us = bank(2 * (j % 2)), bank(2 * (j % 2) + 1)
                dve.wait_ge(s_umm, j + 1)
                dve.wait_ge(s_kev, j + 1)
                if j >= 1:
                    dve.wait_ge(s_ua, j)
                for dst, u, k in ((prod[:, 0, :], us, 1), (filt[:, 0, ft, :], uc, 0),
                                  (prod[:, 1, :], us, 0), (filt[:, 1, ft, :], uc, 1)):
                    last = nc.vector.tensor_tensor(dst, u, spec[:, k, ft, :], ALU.mult)
                last.then_inc(s_um, 1)

        def product_pool(pool, s):
            for ft in range(LT_):
                j = 4 * s + ft
                pool.wait_ge(s_um, j + 1)
                nc.gpsimd.tensor_tensor(filt[:, 0, ft, :], filt[:, 0, ft, :], prod[:, 0, :], ALU.subtract)
                nc.gpsimd.tensor_tensor(filt[:, 1, ft, :], filt[:, 1, ft, :], prod[:, 1, :],
                                        ALU.add).then_inc(s_ua, 1)

        def inverse_pe(pe, s):
            half, o = HY_STEPS[s]
            pe.wait_ge(s_ua, 4 * (s + 1))
            for i in range(LT_):
                for a in range(2):
                    for ft in range(LT_):
                        y, w = filt[:, a, ft, :], dft[:, 1, a, ft, :]
                        lhsT, rhs = (y[:, i * P:(i + 1) * P], w) if o else (w[:, i * P:(i + 1) * P], y)
                        mm = nc.tensor.matmul(bank(4 + i), lhsT, rhs, start=(a == 0 and ft == 0),
                                              stop=(a == 1 and ft == LT_ - 1))
                mm.then_inc(s_imm, 1)

        def inverse_dve(dve, s):
            half, o = HY_STEPS[s]
            for i in range(LT_):
                dve.wait_ge(s_imm, 4 * s + i + 1)
                if o == 0:
                    v = v_tok[:, i, half * 512:(half + 1) * 512]
                    nc.vector.tensor_tensor(v, bank(4 + i), p0_tok[:, i, half * 512:(half + 1) * 512],
                                            ALU.mult).then_inc(s_iv, 1)
                else:
                    m = 4 * half + i
                    nc.vector.tensor_tensor(p1T[:, m, :], bank(4 + i), p1T[:, m, :], ALU.mult).then_inc(s_iv, 1)

        LATE_ROWS = [(mod[:, 16:24, :], 0), (mod[:, 24:32, :], 0), (scale2.unsqueeze(2), 0), (mod[:, 40:48, :], 0)]

        SENTINEL, MARK, FAR = -3.0e38, 3.0e38, 1.0e30

        def turn_rows(pe, u):
            for k in range(KD):
                mm = nc.tensor.transpose(bank(3 + k // 4)[:, (k % 4) * P:(k % 4 + 1) * P],
                                         xg[:, u, k * P:(k + 1) * P], ident)
            mm.then_inc(s_xt, 1)

        def gate_up(pe, u):
            for k in range(KD):
                mm = nc.tensor.matmul(bank(u), xgT[:, u, k, :], gu_w[:, u, k, :], start=(k == 0), stop=(k == KD - 1))
            mm.then_inc(s_gu, 1)

        def turn_hidden(pe, u):
            for f in range(2):
                mm = nc.tensor.transpose(bank(2)[:, (2 * u + f) * P:(2 * u + f + 1) * P],
                                         hh[:, u, f * P:(f + 1) * P], ident)
            mm.then_inc(s_th, 1)

        def down(pe, u, half):
            for f in range(2):
                mm = nc.tensor.matmul(bank(5 + half), hhT[:, u, f, :], down_w[:, u, f, half * 512:(half + 1) * 512],
                                      start=(f == 0), stop=(f == 1))
            mm.then_inc(s_ym, 1)

        def rowsT_low(u):
            return nc.scalar.copy(xgT[:, u, 0:4, :], bank(3).rearrange("p (k n) -> p k n", k=4))

        def rowsT_high(u):
            return nc.vector.tensor_copy(xgT[:, u, 4:8, :], bank(4).rearrange("p (k n) -> p k n", k=4))
        block = ctx.enter_context(nc.Block())

        @block.sync
        def _(sp):
            for dst, src in ((ident, d["ident"]), (tri_le, d["tri_le"]), (tri_gt, d["tri_gt"]),
                             (tri_ge, d["tri_ge"]), (tri_lt, d["tri_lt"]), (cols[:, 0:N_COLS], d["cols"])):
                sp.dma_start(dst, src).then_inc(s_const, 16)
            for i in range(2):
                item = i
                sp.dma_start(ring[:, item % RING], d["ada"][item]).then_inc(s_ring[item % RING], 16)
            for t in range(TA):
                src = d["x"][t * P:(t + 1) * P, :] if t < LT_ else d["ctx"][(t - LT_) * P:(t - LT_ + 1) * P, :]
                sp.dma_start(xin[:, t], src).then_inc(s_x, 16)
            for item in range(2, N_RING):
                name, chunk = RING_ITEMS[item]
                if item >= RING:
                    sp.wait_ge(*freed[item - RING])
                sp.dma_start(ring[:, item % RING], d[name][chunk]).then_inc(s_ring[item % RING], 16)
                if item == AT_XBC + 1:
                    sp.wait_ge(s_pe, 4)
                    sp.dma_start(w_dt, d["w_dt"]).then_inc(s_w_dt, 16)
                    sp.dma_start(rows_ssd, d["rows_ssd"].partition_broadcast(P)).then_inc(s_w_dt, 16)
                if item == AT_Z + 3:
                    sp.wait_ge(s_pe, 8)
                    sp.dma_start(zpos, d["zpos"]).then_inc(s_hyin, 16)
                    sp.dma_start(hy_w1, d["hy_w1"]).then_inc(s_hyin, 16)
                    sp.dma_start(hy_w23, d["hy_w23"]).then_inc(s_hyin, 16)
                if item == AT_HY + 5:
                    sp.dma_start(dft, d["dft"]).then_inc(s_dft, 16)
                if item == AT_HYO:
                    sp.wait_ge(s_pe, 12)
                    sp.dma_start(x1, d["x"].rearrange("(t p) c -> p t c", p=P)).then_inc(s_x1l, 16)
                    sp.dma_start(router_w, d["router_w"]).then_inc(s_rw, 16)
                    sp.dma_start(bias_row, d["router_bias"].partition_broadcast(P)).then_inc(s_rw, 16)
                    sp.dma_start(iota_row, d["iota64"]).then_inc(s_rw, 16)
                    sp.dma_start(pair_ids, d["pair_ids"]).then_inc(s_rw, 16)
            sp.wait_ge(s_pe, 16)
            sp.dma_start(h2_dram.rearrange("(t p) c -> p t c", p=P), h2).then_inc(s_h2st, 16)
            sp.dma_start(gu_w[:, 2], d["sh_gu"]).then_inc(s_shl, 16)
            sp.dma_start(down_w[:, 2], d["sh_down"]).then_inc(s_shl, 16)
            sp.wait_ge(s_brow, 2)
            for u in range(2):
                e = nc.sync.value_load(erow[0:1, u:u + 1], min_val=0, max_val=E - 1)
                sp.dma_start(gu_w[:, u], d["w_gu"][bass.ds(e, 1)].rearrange("a p k n -> p (a k) n")).then_inc(s_gul[u], 16)
                sp.dma_start(down_w[:, u], d["w_down"][bass.ds(e, 1)].rearrange("a p k n -> p (a k) n")).then_inc(s_dnl[u], 16)
            steps_n = nc.sync.value_load(nstep[0:1, 0:1], min_val=1, max_val=NPAIR_IT)
            with sp.Fori(1, NPAIR_IT) as i:
                with sp.If(i < steps_n):
                    for u in range(2):
                        e = nc.sync.value_load(erow[0:1, bass.ds(i * 2 + u, 1)], min_val=0, max_val=E - 1)
                        sp.wait_ge(s_gu, i * 2 + u - 1)
                        sp.wait_ge(s_brow, 2)
                        sp.dma_start(gu_w[:, u], d["w_gu"][bass.ds(e, 1)].rearrange("a p k n -> p (a k) n")).then_inc(s_gul[u], 16)
                        sp.wait_ge(s_ym, i * 4 + 2 * u - 2)
                        sp.wait_ge(s_brow, 2)
                        sp.dma_start(down_w[:, u], d["w_down"][bass.ds(e, 1)].rearrange("a p k n -> p (a k) n")).then_inc(s_dnl[u], 16)
            for u in range(2):
                sp.wait_ge(s_sca[u], steps_n * 16)
            sp.dma_start(fin_row, d["final_g"].partition_broadcast(P)).then_inc(s_fl, 16)
            for t in range(LT_):
                if t >= 2:
                    sp.wait_ge(s_cmb, t - 1)
                src = y_dram.rearrange("(t p k) c -> t p k c", p=P, k=PAIR_STRIDE)[t, :, 0:TOPK, :]
                sp.dma_start(y_in[:, t % 2], src).then_inc(s_yl[t % 2], 16)
            for t in range(LT_):
                sp.wait_ge(s_fo, t + 1)
                sp.dma_start(d["out"][t * P:(t + 1) * P, :], x_out[t]).then_inc(s_out, 16)
            sp.wait_ge(s_out, 16 * LT_)

        @block.gpsimd
        def _(pool):
            nc.gpsimd.memset(ones[:, :], 1.0).then_inc(s_const, 16)
            pool.wait_ge(s_const, 16 * 7)
            phase_end(pool, 1)
            for u, (dirn, c) in enumerate(STATE_UPDATES[:7]):
                pool_xdte(pool, u, dirn, c)
            for c in range(LT_):
                pool.wait_ge(s_te, SSM_TURNED)
                for dirn in range(2):
                    if c >= 2:
                        pool.wait_ge(s_y, 4 * (c - 1))
                    nc.gpsimd.tensor_tensor(
                        xdt[:, c % 2, dirn].rearrange("p (h e) -> p h e", e=HD),
                        xs_tok[:, c].rearrange("p (h e) -> p h e", e=HD),
                        over(dt_tok[:, c, 16 * dirn:16 * dirn + 16], HD), ALU.mult).then_inc(s_xdt, 1)
                for q in range(4):
                    n = 4 * c + q
                    if n >= 1:
                        pool.wait_ge(s_seg, 2 * n)
                    for dirn in range(2):
                        nc.gpsimd.tensor_tensor(
                            seg_rhs[:, dirn], each(tri_ge if dirn else tri_le, 4),
                            over(a_tok[:, c, 16 * dirn + 4 * q:16 * dirn + 4 * q + 4], P),
                            ALU.mult).then_inc(s_rhs, 1)
                if c < LT_ - 1:
                    pool_xdte(pool, 7 + c, 0, c)
            pool.wait_ge(s_xe, 10)
            pool.wait_ge(s_rhs, 2 * 16)
            phase_end(pool, 2)
            for s in range(4):
                filter_pool(pool, s)
                product_pool(pool, s)
            pool.wait_ge(s_ua, 16)
            phase_end(pool, 3)
            for m in range(8):
                pool.wait_ge(s_mg, 8 + m + 1)
                nc.gpsimd.tensor_tensor(mergedT[:, m, :], mergedT[:, m, :], gates[:, 1, m, :], ALU.add).then_inc(s_mga, 1)
            pool.wait_ge(s_mga, 8)
            phase_end(pool, 4)
            nc.gpsimd.memset(xg, 0.0).then_inc(s_xz, 1)
            nc.gpsimd.memset(pad_tab, PAD_PAIR).then_inc(s_xz, 1)
            pool.wait_ge(s_xz, 2)
            pool.dma_start(slot_dram.rearrange("(p j) a -> p (j a)", p=P), pad_tab).then_inc(s_pad, 16)
            pool.wait_ge(s_pad, 16)
            pool.wait_ge(s_dst, 1)
            for c in range(LT_ * TOPK):
                nc.gpsimd.indirect_dma_start(
                    out=slot_dram, out_offset=bass.IndirectOffsetOnAxis(ap=dest_i[:, c:c + 1], axis=0),
                    in_=pair_ids[:, c:c + 1], in_offset=None).then_inc(s_scat, 16)
            pool.wait_ge(s_scat, 16 * LT_ * TOPK)
            pool.dma_start(slots, slot_dram.rearrange("(p j) a -> p (j a)", p=P)).then_inc(s_slot, 16)
            pool.wait_ge(s_tok, 1)
            pool.wait_ge(s_h2st, 16)

            def gather_rows(u, j):
                return nc.gpsimd.indirect_dma_start(
                    out=xg[:, u], out_offset=None, in_=h2_dram,
                    in_offset=bass.IndirectOffsetOnAxis(ap=idx_g[:, u], axis=0), bounds_check=L - 1,
                    oob_is_err=False)

            for u in range(2):
                nc.gpsimd.tensor_copy(idx_g[:, u], tokens[:, u:u + 1]).then_inc(s_pi, 1)
                pool.wait_ge(s_pi, u + 1)
                gather_rows(u, u).then_inc(s_xg[u], 16)
            pool.wait_ge(s_brow, 2)
            steps_n = nc.gpsimd.value_load(nstep[0:1, 0:1], min_val=1, max_val=NPAIR_IT)
            with pool.Fori(0, NPAIR_IT) as i:
                with pool.If(i < steps_n):
                    for u in range(2):
                        pool.wait_ge(s_xt, i * 2 + u + 1)
                        pool.wait_ge(s_xg[u], i * 16 + 16)
                        pool.wait_ge(s_tok, 1)
                        nc.gpsimd.tensor_copy(idx_g[:, u], tokens[:, bass.ds(i * 2 + 2 + u, 1)]).then_inc(s_pi, 1)
                        pool.wait_ge(s_pi, i * 4 + u + 3)
                        pool.sem_inc(s_pseen, 1)
                        gather_rows(u, None).then_inc(s_xg[u], 16)
                    for u in range(2):
                        pool.wait_ge(s_sca[u], i * 16)
                        pool.wait_ge(s_slot, 16)
                        nc.gpsimd.tensor_copy(idx_s[:, u], slots[:, bass.ds(i * 2 + u, 1)]).then_inc(s_pi, 1)
                        pool.wait_ge(s_pi, i * 4 + u + 5)
                        pool.wait_ge(s_yea, i * 2 + u + 1)
                        pool.wait_ge(s_yeb, i * 2 + u + 1)
                        pool.sem_inc(s_pseen, 1)
                        nc.gpsimd.indirect_dma_start(
                            out=y_dram, out_offset=bass.IndirectOffsetOnAxis(ap=idx_s[:, u], axis=0),
                            in_=yo[:, u], in_offset=None, bounds_check=PAD_PAIR - 1,
                            oob_is_err=False).then_inc(s_sca[u], 16)

        @block.tensor
        def _(pe):
            pe.wait_ge(s_const, 16 * 7)
            for j in range(8):
                mod_chunk(pe, j, AT_ADA1 + j)
            for k in range(KD):
                for part, (t0, n) in enumerate(((0, LT_), (LT_, CT_))):
                    g = 2 * k + part
                    if k == 0:
                        pe.wait_ge(s_xn, t0 + n)
                    if g >= 4:
                        pe.wait_ge(s_hT, g - 3)
                    for t in range(n):
                        mm = nc.tensor.transpose(bank(4 + g % 4)[:, t * P:(t + 1) * P],
                                                 xin[:, t0 + t, k * P:(k + 1) * P], ident)
                    mm.then_inc(s_htr, 1)
            pe.wait_ge(s_htr, 2 * KD)
            phase_end(pe, 1)
            pe.wait_ge(s_hT, 2 * KD)
            conv_pe(pe, 0, len(SSM_TILES), 0)
            pe.wait_ge(s_w_dt, 32)
            for t in range(TA):
                for k in range(KD):
                    mm = nc.tensor.matmul(bank(6)[:, t * 32:(t + 1) * 32], hT[:, k, t * P:(t + 1) * P],
                                          w_dt[:, k, :], start=(k == 0), stop=(k == KD - 1))
            mm.then_inc(s_dtmm, 1)
            for j in range(4):
                ring_wait(pe, AT_Z + j)
                for t in range(LT_):
                    n = LT_ * j + t
                    if n == 0:
                        pe.wait_ge(s_cv, len(SSM_TILES))
                    if n >= 2:
                        pe.wait_ge(s_z, n - 1)
                    for k in range(KD):
                        mm = nc.tensor.matmul(bank(n % 2)[:, 0:W_CHUNK], hT[:, k, t * P:(t + 1) * P],
                                              ring[:, (AT_Z + j) % RING, k, :], start=(k == 0), stop=(k == KD - 1))
                    mm.then_inc(s_zmm, 1)
            pe.wait_ge(s_dt, DT_READY)
            for t in range(TA):
                b = bank(2 + t // 3)[:, 96 * (t % 3):96 * (t % 3) + 96]
                af, ab, a2 = a_tok[:, t, 0:16], a_tok[:, t, 16:32], a_tok[:, t, :]
                for at, tri, rhs in ((0, tri_le, af), (16, tri_ge, ab), (32, tri_gt, af), (48, tri_lt, ab),
                                     (64, ones, a2)):
                    mm = nc.tensor.matmul(b[:, at:at + rhs.shape[1]], tri, rhs, start=True, stop=True)
            mm.then_inc(s_cs, 1)
            pe.wait_ge(s_te, SSM_TURNED)
            for c in range(LT_):
                if c >= 2:
                    pe.wait_ge(s_cbm, 2 * (c - 1))
                for g in range(GROUPS):
                    mm = nc.tensor.matmul(bank(4 + c % 2)[:, g * P:(g + 1) * P], BT[:, g, c * P:(c + 1) * P],
                                          CT[:, g, c * P:(c + 1) * P], start=True, stop=True)
                mm.then_inc(s_cb, 1)
            pe.wait_ge(s_z, 4 * LT_)
            for u in range(7):
                if u == 0:
                    pe.wait_ge(s_cbm, 2 * LT_)
                state_pe(pe, u)
            for c in range(LT_):
                pe.wait_ge(s_ecs, 2)
                for q in range(4):
                    n = 4 * c + q
                    pe.wait_ge(s_rhs, 2 * n + 2)
                    for dirn in range(2):
                        if n >= 2:
                            pe.wait_ge(s_exp, 2 * (n - 2) + dirn + 1)
                        nc.tensor.matmul(bank(2 * (n % 2) + dirn), tri_lt if dirn else tri_gt,
                                         seg_rhs[:, dirn].rearrange("p a b -> p (a b)"),
                                         start=True, stop=True).then_inc(s_seg, 1)
                    if q in (1, 2):
                        off_pe(pe, c, q - 1)
                    if q == 3 and c < LT_ - 1:
                        state_pe(pe, 7 + c)
                    if n >= 1:
                        quad_pe(pe, n - 1)
                if c == LT_ - 1:
                    quad_pe(pe, 4 * c + 3)
            pe.wait_ge(s_yc, LT_)
            for m in range(KD):
                if m == 0:
                    pe.wait_ge(s_vn, 2 * LT_)
                if m >= 4:
                    pe.wait_ge(s_yT, m - 3)
                for t in range(LT_):
                    mm = nc.tensor.transpose(bank(m % 4)[:, t * P:(t + 1) * P], zs[:, t, m * P:(m + 1) * P], ident)
                mm.then_inc(s_ytr, 1)
            pe.wait_ge(s_ytr, KD)
            phase_end(pe, 2)
            mlp_pe(pe, 0)
            conv_pe(pe, N_SSM, N_SSM + 2, N_SSM)
            mlp_pe(pe, 1)
            conv_pe(pe, N_SSM + 2, N_SSM + 4, N_SSM)
            mlp_pe(pe, 2)
            conv_pe(pe, N_SSM + 4, N_ALL, N_SSM)
            pe.wait_ge(s_te, turned_before(N_ALL))
            pe.wait_ge(s_cv, N_ALL)
            pe.wait_ge(s_sin, 3)
            pe.wait_ge(s_dft, 16)
            for s in range(4):
                filter_pe(pe, s)
                spectrum_pe(pe, s)
                signal_pe(pe, s)
                inverse_pe(pe, s)
            pe.wait_ge(s_imm, 16)
            phase_end(pe, 3)
            for n in range(32):
                item, c = AT_GATE + n // 2, n % 2
                src = hT[:, :, 0:L] if n < 16 else p1T if n < 24 else yT
                ring_wait(pe, item)
                if 4 <= n < 20:
                    pe.wait_ge(s_gt, n - 3)
                elif n >= 20:
                    pe.wait_ge(s_mg, n - 19)
                for k in range(KD):
                    mm = nc.tensor.matmul(bank(n % 4), ring[:, item % RING, k, c * P:(c + 1) * P], src[:, k, :],
                                          start=(k == 0), stop=(k == KD - 1))
                mm.then_inc(s_mp, 1)
            pe.wait_ge(s_mg, 16)
            for n in range(8, 24):
                mod_chunk(pe, n, AT_ADA2 + n - 8)
            pe.wait_ge(s_mod2, 1)
            for i, (v, w) in enumerate(LATE_ROWS):
                for half in range(2):
                    if 2 * i + half >= 4:
                        pe.wait_ge(s_row, 2 * i + half - 3)
                    for k in range(4):
                        kk = 4 * half + k
                        mm = nc.tensor.matmul(bank(4 + (2 * i + half) % 4)[:, k * P:(k + 1) * P],
                                              v[:, kk, w:w + 1].to_broadcast([P, P]), ident, start=True, stop=True)
                    mm.then_inc(s_rowmm, 1)
            pe.wait_ge(s_mga, 8)
            for j in range(4):
                ring_wait(pe, AT_WO + j)
                for t in range(LT_):
                    n = 4 * j + t
                    if n >= 4:
                        pe.wait_ge(s_x1, n - 3)
                    for k in range(KD):
                        mm = nc.tensor.matmul(bank(n % 4)[:, 0:W_CHUNK], mergedT[:, k, t * P:(t + 1) * P],
                                              ring[:, (AT_WO + j) % RING, k, :], start=(k == 0), stop=(k == KD - 1))
                    mm.then_inc(s_xmm, 1)
            pe.wait_ge(s_xmm, 16)
            phase_end(pe, 4)
            for m in range(KD):
                if m >= 4:
                    pe.wait_ge(s_h2T, m - 3)
                for t in range(LT_):
                    mm = nc.tensor.transpose(bank(m % 4)[:, t * P:(t + 1) * P], h2[:, t, m * P:(m + 1) * P], ident)
                mm.then_inc(s_h2t, 1)
            pe.wait_ge(s_rw, 64)
            pe.wait_ge(s_h2T, KD)
            for t in range(LT_):
                for k in range(KD):
                    mm = nc.tensor.matmul(bank(4)[:, t * E:(t + 1) * E], h2T[:, k, t * P:(t + 1) * P],
                                          router_w[:, k, :], start=(k == 0), stop=(k == KD - 1))
            mm.then_inc(s_lg, 1)
            pe.wait_ge(s_shl, 32)
            for f in range(4):
                for k in range(KD):
                    mm = nc.tensor.matmul(bank(f), gu_w[:, 2, k, f * P:(f + 1) * P], h2T[:, k, :],
                                          start=(k == 0), stop=(k == KD - 1))
                mm.then_inc(s_shm, 1)
            pe.wait_ge(s_msk2, LT_)
            for t in range(LT_):
                for b in range(t + 1):
                    mm = nc.tensor.matmul(bank(5)[:, t * E:(t + 1) * E], tri_lt if b == t else ones, mask[:, b, :],
                                          start=(b == 0), stop=(b == t))
            for b in range(LT_):
                mm = nc.tensor.matmul(bank(5)[:, LT_ * E:(LT_ + 1) * E], ones, mask[:, b, :], start=(b == 0),
                                      stop=(b == LT_ - 1))
            mm.then_inc(s_rk, 1)
            pe.wait_ge(s_shh, 2)
            for t in range(LT_):
                for half in range(2):
                    n = 2 * t + half
                    if n == 2:
                        pe.wait_ge(s_be, 1)
                        nc.tensor.transpose(bank(4)[0:1, 0:P], ecol[:, 0:1], ident).then_inc(s_bt, 1)
                    if n >= 2:
                        pe.wait_ge(s_shx, n - 1)
                    for f in range(2):
                        mm = nc.tensor.matmul(bank(6 + half), shg[:, f, t * P:(t + 1) * P],
                                              down_w[:, 2, f, half * 512:(half + 1) * 512], start=(f == 0), stop=(f == 1))
                    mm.then_inc(s_shy, 1)
            pe.wait_ge(s_shx, 8)
            pe.wait_ge(s_brow, 2)
            for u in range(2):
                pe.wait_ge(s_xg[u], 16)
                if u:
                    pe.wait_ge(s_xea, 1)
                    pe.wait_ge(s_xeb, 1)
                turn_rows(pe, u)
            steps_n = nc.tensor.value_load(nstep[0:1, 0:1], min_val=1, max_val=NPAIR_IT)
            with pe.Fori(0, NPAIR_IT) as i:
                with pe.If(i < steps_n):
                    for u in range(2):
                        pe.wait_ge(s_gul[u], i * 16 + 16)
                        pe.wait_ge(s_xea, i * 2 + u + 1)
                        pe.wait_ge(s_xeb, i * 2 + u + 1)
                        gate_up(pe, u)
                    for u in range(2):
                        pe.wait_ge(s_h, i * 2 + u + 1)
                        turn_hidden(pe, u)
                        pe.wait_ge(s_xg[u], i * 16 + 32)
                        pe.wait_ge(s_xea, i * 2 + u + 2)
                        pe.wait_ge(s_xeb, i * 2 + u + 2)
                        turn_rows(pe, u)
                        pe.wait_ge(s_hte, i * 2 + u + 1)
                        pe.wait_ge(s_dnl[u], i * 16 + 16)
                        pe.wait_ge(s_yea, i * 2 + u)
                        down(pe, u, 0)
                        pe.wait_ge(s_yeb, i * 2 + u)
                        down(pe, u, 1)

        @block.scalar
        def _(act):
            act.wait_ge(s_const, 16 * 7)
            for i, name in enumerate(("c", "c_ctx")):
                nc.scalar.activation(silu_c[:, :, i], col(cols, name, 0, KD), ACT.Silu).then_inc(s_silu_c, 1)
            for t in range(TA):
                act.wait_ge(s_x, 16 * TA)
                if t >= 1:
                    act.wait_ge(s_ss, t)
                nc.scalar.activation(junk, xin[:, t], ACT.Square,
                                     accum_out=small[:, 16 + t:17 + t]).then_inc(s_ss, 1)
            act.wait_ge(s_rs, 1)
            nc.scalar.activation(small[:, 32:32 + TA], small[:, 24:24 + TA], ACT.Sqrt).then_inc(s_rs, 1)
            mod_rows_act(act, 0, 8)
            act.wait_ge(s_mod, 4)
            for k in range(KD):
                for part, (t0, n) in enumerate(((0, L), (L, LC))):
                    g = 2 * k + part
                    act.wait_ge(s_htr, g + 1)
                    nc.scalar.activation(hT[:, k, t0:t0 + n], bank(4 + g % 4)[:, 0:n], ACT.Identity,
                                         scale=scale1[:, k, part:part + 1],
                                         bias=mod[:, k, part:part + 1]).then_inc(s_hT, 1)
            act.wait_ge(s_hT, 2 * KD)
            phase_end(act, 1)
            conv_act(act, 0, len(SSM_TILES), 0)
            act.wait_ge(s_w_dt, 32)
            act.wait_ge(s_dt, 2)
            nc.scalar.activation(dtw[:, 2], dtw[:, 1], ACT.Exp, scale=-1.0).then_inc(s_dta, 1)
            nc.scalar.activation(rows_ssd[:, 32:64], rows_ssd[:, 32:64], ACT.Exp).then_inc(s_dta, 1)
            act.wait_ge(s_dt, 3)
            nc.scalar.activation(dtw[:, 4], dtw[:, 3], ACT.Ln).then_inc(s_dta, 1)
            for j in range(4):
                for t in range(LT_):
                    n = LT_ * j + t
                    act.wait_ge(s_zmm, n + 1)
                    nc.scalar.activation(zs[:, t, j * W_CHUNK:(j + 1) * W_CHUNK], bank(n % 2)[:, 0:W_CHUNK],
                                         ACT.Silu).then_inc(s_z, 1)
            act.wait_ge(s_cs, 1)
            for i in range(2):
                nc.scalar.activation(ecs[:, 3 * i:3 * i + 3, :],
                                     bank(2 + i)[:, 0:288].rearrange("p (a b) -> p a b", a=3),
                                     ACT.Exp).then_inc(s_ecs, 1)
            for n in range(4 * LT_):
                for dirn in range(2):
                    act.wait_ge(s_seg, 2 * n + dirn + 1)
                    if n >= 2:
                        act.wait_ge(s_y, n - 1)
                    nc.scalar.activation(decay[:, n % 2, dirn].rearrange("p a b -> p (a b)"),
                                         bank(2 * (n % 2) + dirn), ACT.Exp).then_inc(s_exp, 1)
                if n % 4 == 1 and n >= 5:
                    gate_squares(act, n // 4 - 1)
            gate_squares(act, LT_ - 1)
            act.wait_ge(s_vr, 1)
            nc.scalar.activation(v_rstd, v_rstd, ACT.Sqrt).then_inc(s_vr, 1)
            for m in range(KD):
                act.wait_ge(s_ytr, m + 1)
                nc.scalar.activation(yT[:, m, :], bank(m % 4), ACT.Identity,
                                     scale=col(cols, "ssm_norm_g", m)).then_inc(s_yT, 1)
            act.wait_ge(s_yT, KD)
            phase_end(act, 2)
            mlp_act(act, 0)
            conv_act(act, N_SSM, N_SSM + 2, N_SSM)
            mlp_act(act, 1)
            conv_act(act, N_SSM + 2, N_SSM + 4, N_SSM)
            mlp_act(act, 2)
            conv_act(act, N_SSM + 4, N_ALL, N_SSM)
            act.wait_ge(s_cv, N_ALL)
            rows_dma(act, 0)
            for s in range(4):
                filter_act(act, s)
                spectrum_act(act, s)
            act.wait_ge(s_kev, 16)
            phase_end(act, 3)
            for n in range(16):
                act.wait_ge(s_mp, n + 1)
                nc.scalar.activation(gates[:, n // 8, n % 8, :], bank(n % 4), ACT.Sigmoid).then_inc(s_gt, 1)
            mod_rows_act(act, 8, 24)
            for n in range(8):
                act.wait_ge(s_rowmm, n + 1)
                nc.scalar.copy(rows[:, n // 2, (n % 2) * 512:(n % 2 + 1) * 512], bank(4 + n % 4)).then_inc(s_row, 1)
            act.wait_ge(s_row, 8)
            for t in range(LT_):
                act.wait_ge(s_x1, 16)
                if t >= 1:
                    act.wait_ge(s_ss2, t)
                nc.scalar.activation(squares2, x1[:, t], ACT.Square, accum_out=small[:, 16 + t:17 + t]).then_inc(s_ss2, 1)
            act.wait_ge(s_rs2, 1)
            nc.scalar.activation(small[:, 32:32 + LT_], small[:, 24:24 + LT_], ACT.Sqrt).then_inc(s_rs2, 1)
            act.wait_ge(s_rs2, 2)
            phase_end(act, 4)
            for m in range(KD):
                act.wait_ge(s_h2t, m + 1)
                nc.scalar.copy(h2T[:, m, :], bank(m % 4)).then_inc(s_h2T, 1)
            act.wait_ge(s_lg, 1)
            for t in range(LT_):
                nc.scalar.activation(scores[:, t], bank(4)[:, t * E:(t + 1) * E], ACT.Sigmoid).then_inc(s_sc0, 1)
            for f in range(2):
                act.wait_ge(s_shm, f + 1)
                nc.scalar.activation(shg[:, f, :], bank(f), ACT.Silu).then_inc(s_sha, 1)
            act.wait_ge(s_xt, 1)
            rowsT_low(0).then_inc(s_xea, 1)
            act.wait_ge(s_xt, 2)
            rowsT_low(1).then_inc(s_xea, 1)
            steps_n = nc.scalar.value_load(nstep[0:1, 0:1], min_val=1, max_val=NPAIR_IT)
            with act.Fori(0, NPAIR_IT) as i:
                with act.If(i < steps_n):
                    for u in range(2):
                        act.wait_ge(s_gu, i * 2 + u + 1)
                        nc.scalar.activation(sg[:, u, :], bank(u)[:, 0:DE], ACT.Silu).then_inc(s_sg, 1)
                    for u in range(2):
                        act.wait_ge(s_xt, i * 2 + u + 3)
                        rowsT_low(u).then_inc(s_xea, 1)
                        act.wait_ge(s_ym, i * 4 + 2 * u + 1)
                        act.wait_ge(s_sca[u], i * 16)
                        nc.scalar.copy(yo[:, u, 0:512], bank(5)).then_inc(s_yea, 1)
            for t in range(LT_):
                act.wait_ge(s_cmb, t + 1)
                if t >= 1:
                    act.wait_ge(s_ss3, t)
                nc.scalar.activation(squares2, x1[:, t], ACT.Square, accum_out=small[:, 16 + t:17 + t]).then_inc(s_ss3, 1)
                act.wait_ge(s_rs3, 2 * t + 1)
                nc.scalar.activation(small[:, 32 + t:33 + t], small[:, 24 + t:25 + t], ACT.Sqrt).then_inc(s_rs3, 1)

        @block.vector
        def _(dve):
            steps = [0]

            def link(ins):
                steps[0] += 1
                ins.then_inc(s_dve, 1)
                dve.wait_ge(s_dve, steps[0])

            V = nc.vector
            dve.wait_ge(s_const, 16 * 7)
            dve.wait_ge(s_ss, TA)
            V.tensor_scalar(small[:, 24:24 + TA], small[:, 16:16 + TA], 1.0 / D, EPS, ALU.mult,
                            ALU.add).then_inc(s_rs, 1)
            dve.wait_ge(s_rs, 2)
            link(V.reciprocal(small[:, 40:40 + TA], small[:, 32:32 + TA]))
            for t in range(TA):
                V.tensor_scalar(xin[:, t], xin[:, t], small[:, 40 + t:41 + t], None, ALU.mult).then_inc(s_xn, 1)
            dve.wait_ge(s_modtr, 8)
            link(V.tensor_tensor(mod[:, 0:16, :], bank(2)[:, 0:32].rearrange("p (a b) -> p a b", b=2),
                                 over(col(cols, "ada_b", 0, 16), 2), ALU.add))
            link(V.tensor_scalar(scale1[:, :, :], mod[:, 8:16, :], 1.0, None, ALU.add))
            V.tensor_tensor(scale1[:, :, :], scale1[:, :, :], over(col(cols, "norm1_g", 0, 8), 2),
                            ALU.mult).then_inc(s_mod, 4)
            dve.wait_ge(s_mod, 4)
            dve.wait_ge(s_xn, TA)
            phase_end(dve, 1)
            conv_dve(dve, 0, len(SSM_TILES))
            dve.wait_ge(s_dtmm, 1)
            dve.wait_ge(s_w_dt, 32)
            V.tensor_tensor(dtw[:, 0], bank(6)[:, 0:192].rearrange("p (t n) -> p t n", t=TA),
                            each(rows_ssd[:, 0:32], TA), ALU.add).then_inc(s_dt, 1)
            dve.wait_ge(s_dt, 1)
            V.scalar_tensor_tensor(dtw[:, 1], dtw[:, 0], -1.0, dtw[:, 0], ALU.mult, ALU.max).then_inc(s_dt, 1)
            dve.wait_ge(s_dta, 2)
            V.tensor_scalar(dtw[:, 3], dtw[:, 2], 1.0, None, ALU.add).then_inc(s_dt, 1)
            dve.wait_ge(s_dt, 3)
            link(V.reciprocal(dtw[:, 1], dtw[:, 3]))
            link(V.scalar_tensor_tensor(dt_tok[:, :, :], dtw[:, 3], -1.0, dtw[:, 2], ALU.add, ALU.subtract))
            link(V.tensor_tensor(dt_tok[:, :, :], dt_tok[:, :, :], dtw[:, 1], ALU.mult))
            dve.wait_ge(s_dta, 3)
            link(V.tensor_tensor(dt_tok[:, :, :], dtw[:, 4], dt_tok[:, :, :], ALU.subtract))
            link(V.scalar_tensor_tensor(dt_tok[:, :, :], dtw[:, 0], 0.0, dt_tok[:, :, :], ALU.max, ALU.add))
            V.scalar_tensor_tensor(a_tok[:, :, :], dt_tok[:, :, :], -1.0, each(rows_ssd[:, 32:64], TA),
                                   ALU.mult, ALU.mult).then_inc(s_dt, 1)
            dve.wait_ge(s_ecs, 2)
            V.tensor_tensor(dte[:, :, :], dt_tok[:, :, :], ecs[:, :, 32:64], ALU.mult).then_inc(s_dte, 1)
            for c in range(LT_):
                dve.wait_ge(s_cb, c + 1)
                for dirn in range(2):
                    V.tensor_tensor(cbm[:, dirn, c], bank(4 + c % 2)[:, 0:GROUPS * P].rearrange(
                        "p (g l) -> p g l", g=GROUPS), each(tri_ge if dirn else tri_le, GROUPS),
                        ALU.mult).then_inc(s_cbm, 1)
            dve.wait_ge(s_cbm, 2 * LT_)
            for u in range(7):
                state_dve(dve, link, u)
            for c in range(LT_):
                for q in range(4):
                    n = 4 * c + q
                    for dirn in range(2):
                        dve.wait_ge(s_exp, 2 * n + dirn + 1)
                        V.tensor_tensor(decay[:, n % 2, dirn], decay[:, n % 2, dirn],
                                        each(cbm[:, dirn, c, q // 2], 4), ALU.mult).then_inc(s_msk, 1)
                    if q in (1, 2):
                        dve.wait_ge(s_off, 2 * c + q)
                        dst = y1 if q == 1 else y2
                        V.tensor_tensor(dst.rearrange("p (h e) -> p h e", e=HD),
                                        ps[:, 4:6, :].rearrange("p b (h e) -> p (b h) e", e=HD),
                                        over(ecs[:, c, 16 * (q - 1):16 * q], HD), ALU.mult).then_inc(s_offr, 1)
                dve.wait_ge(s_offr, 2 * c + 2)
                link(V.tensor_tensor(y1, y1, y2, ALU.add))
                if c < LT_ - 1:
                    state_dve(dve, link, 7 + c)
                link(V.tensor_tensor(y2.rearrange("p (h e) -> p h e", e=HD),
                                     xs_tok[:, c].rearrange("p (h e) -> p h e", e=HD),
                                     over(rows_ssd[:, 64:80], HD), ALU.mult))
                link(V.tensor_tensor(y1, y1, y2, ALU.add))
                dve.wait_ge(s_y, 4 * c + 4)
                link(V.tensor_tensor(y1, ps[:, 6:8, :].rearrange("p b e -> p (b e)"), y1, ALU.add))
                V.tensor_tensor(zs[:, c], y1, zs[:, c], ALU.mult).then_inc(s_yc, 1)
                dve.wait_ge(s_yc, c + 1)
            dve.wait_ge(s_vss, 2 * LT_)
            V.tensor_scalar(v_rstd, v_ss, 1.0 / 512, EPS, ALU.mult, ALU.add).then_inc(s_vr, 1)
            dve.wait_ge(s_vr, 2)
            link(V.reciprocal(v_rstd, v_rstd))
            for c in range(LT_):
                for g in range(GROUPS):
                    V.tensor_scalar(zs[:, c, g * 512:(g + 1) * 512], zs[:, c, g * 512:(g + 1) * 512],
                                    v_rstd[:, 2 * c + g:2 * c + g + 1], None, ALU.mult).then_inc(s_vn, 1)
            dve.wait_ge(s_vn, 2 * LT_)
            phase_end(dve, 2)
            V.tensor_tensor(small[0:64, 48:51], col(cols, "mlp", 0, 3)[0:64], col(cols, "mlp", 3, 3)[0:64],
                            ALU.mult).then_inc(s_fb, 1)
            mlp_dve(dve, link, 0)
            conv_dve(dve, N_SSM, N_SSM + 2)
            mlp_dve(dve, link, 1)
            conv_dve(dve, N_SSM + 2, N_SSM + 4)
            mlp_dve(dve, link, 2)
            conv_dve(dve, N_SSM + 4, N_ALL)
            for s in range(4):
                filter_dve(dve, link, s)
                product_dve(dve, s)
                inverse_dve(dve, s)
            dve.wait_ge(s_iv, 16)
            phase_end(dve, 3)
            for n in range(16):
                dve.wait_ge(s_mp, 16 + n + 1)
                dst = mergedT[:, n, :] if n < 8 else gates[:, 1, n - 8, :]
                if n == 0:
                    dve.wait_ge(s_gt, 16)
                V.tensor_tensor(dst, bank(n % 4), gates[:, n // 8, n % 8, :], ALU.mult).then_inc(s_mg, 1)
            dve.wait_ge(s_modtr, 24)
            link(V.tensor_tensor(mod[:, 16:48, :], bank(2)[:, 32:96].rearrange("p (a b) -> p a b", b=2),
                                 over(col(cols, "ada_b", 16, 32), 2), ALU.add))
            V.scalar_tensor_tensor(scale2.unsqueeze(2), mod[:, 32:40, 0:1], 1.0,
                                   col(cols, "norm2_g", 0, 8).unsqueeze(2), ALU.add, ALU.mult).then_inc(s_mod2, 1)
            dve.wait_ge(s_row, 8)
            dve.wait_ge(s_x1l, 16)
            for j in range(4):
                for t in range(LT_):
                    n = 4 * j + t
                    cs = slice(j * W_CHUNK, (j + 1) * W_CHUNK)
                    dve.wait_ge(s_xmm, n + 1)
                    link(V.tensor_tensor(xmix[:, n % 2, :], bank(n % 4)[:, 0:W_CHUNK], rows[:, 0, cs], ALU.mult))
                    V.tensor_tensor(x1[:, t, cs], x1[:, t, cs], xmix[:, n % 2, :], ALU.add).then_inc(s_x1, 1)
            dve.wait_ge(s_ss2, LT_)
            V.tensor_scalar(small[:, 24:24 + LT_], small[:, 16:16 + LT_], 1.0 / D, EPS, ALU.mult,
                            ALU.add).then_inc(s_rs2, 1)
            dve.wait_ge(s_rs2, 2)
            link(V.reciprocal(small[:, 40:40 + LT_], small[:, 32:32 + LT_]))
            for t in range(LT_):
                link(V.scalar_tensor_tensor(h2[:, t], x1[:, t], small[:, 40 + t:41 + t], rows[:, 2],
                                            ALU.mult, ALU.mult))
                V.tensor_tensor(h2[:, t], h2[:, t], rows[:, 1], ALU.add).then_inc(s_h2, 1)
            dve.wait_ge(s_h2, LT_)
            phase_end(dve, 4)
            V.memset(grp[:, 8:16], SENTINEL)
            V.memset(grp_rep, SENTINEL)
            V.memset(top_rep, SENTINEL)
            link(V.memset(sel[:, :, E:E + 8], SENTINEL))
            for t in range(LT_):
                dve.wait_ge(s_sc0, t + 1)
                link(V.tensor_tensor(sel[:, t, 0:E], scores[:, t], bias_row, ALU.add))
                for g in range(EG):
                    last = V.max(grp8[:, g, :], sel[:, t, g * 8:(g + 1) * 8])
                link(last)
                link(V.tensor_tensor(grp[:, 0:EG].unsqueeze(2), grp8[:, :, 0:1], grp8[:, :, 1:2], ALU.add))
                link(V.max(grp_top, grp[:, 0:EG]))
                link(V.tensor_copy(grp_rep[:, 0:TOPG], grp_top[:, 0:TOPG]))
                link(V.match_replace(grp_mark[:, 0:12], grp_rep, grp[:, 0:12], MARK))
                link(V.tensor_scalar(keep, grp_mark[:, 0:EG], MARK, None, ALU.is_equal))
                link(V.tensor_scalar(drop, keep, FAR, -FAR, ALU.mult, ALU.add))
                s3 = sel[:, t, 0:E].rearrange("p (g e) -> p g e", g=EG)
                link(V.tensor_tensor(s3, s3, over(keep, 8), ALU.mult))
                link(V.tensor_tensor(s3, s3, over(drop, 8), ALU.add))
                link(V.max(top8[:, t, :], sel[:, t, 0:E]))
                V.tensor_copy(top_rep[:, 0:TOPK], top8[:, t, 0:TOPK])
                link(V.max_index(idx_u[:, t, :], top8[:, t, :], sel[:, t, 0:E]))
                link(V.match_replace(marked, top_rep, sel[:, t, :], MARK))
                V.tensor_scalar(mask[:, t, :], marked[:, 0:E], MARK, None, ALU.is_equal).then_inc(s_msk2, 1)
            link(V.tensor_copy(idx_f, idx_u))
            for f in range(2):
                dve.wait_ge(s_sha, f + 1)
                dve.wait_ge(s_shm, f + 3)
                V.tensor_tensor(shg[:, f, :], bank(2 + f), shg[:, f, :], ALU.mult).then_inc(s_shh, 1)
            dve.wait_ge(s_rk, 1)
            V.tensor_copy(rank, bank(5)[:, 0:LT_ * E].rearrange("p (t e) -> p t e", e=E))
            link(V.tensor_copy(counts, bank(5)[:, LT_ * E:(LT_ + 1) * E]))
            link(V.tensor_scalar(nblk, counts, 0.0, None, ALU.is_gt))
            for b in range(1, LT_):
                link(V.scalar_tensor_tensor(nblk, counts, float(b * P), nblk, ALU.is_gt, ALU.add))
            link(V.tensor_tensor_scan(cend, ones[:, 0:E], nblk, 0.0, ALU.mult, ALU.add))
            link(V.tensor_scalar(picked, cend, col(cols, "jcol"), None, ALU.is_le))
            link(V.tensor_reduce(ecol[:, 0:1], picked, AX.X, ALU.add))
            V.tensor_scalar(ecol[:, 0:1], ecol[:, 0:1], float(E - 1), None, ALU.min).then_inc(s_be, 1)
            link(V.tensor_scalar(nstep_f[:, 0:1], cend[0:1, E - 1:E], 0.5, 0.25, ALU.mult, ALU.add))
            link(V.tensor_scalar(nstep_f[:, 0:1], nstep_f[:, 0:1], ROUND_MAGIC, None, ALU.add))
            link(V.tensor_scalar(nstep_f[:, 0:1], nstep_f[:, 0:1], ROUND_MAGIC, None, ALU.subtract))
            V.tensor_copy(nstep[:, 0:1], nstep_f[:, 0:1]).then_inc(s_brow, 1)
            link(V.tensor_tensor(base, cend, nblk, ALU.subtract))
            link(V.tensor_scalar(over_b, rank, float(P), None, ALU.is_ge))
            for b in range(2, LT_):
                link(V.scalar_tensor_tensor(over_b, rank, float(b * P), over_b, ALU.is_ge, ALU.add))
            link(V.scalar_tensor_tensor(dest, over_b, float(-P), rank, ALU.mult, ALU.add))
            link(V.scalar_tensor_tensor(dest, dest, float(NBLK), over_b, ALU.mult, ALU.add))
            link(V.tensor_tensor(dest, dest, each(base, LT_), ALU.add))
            for t in range(LT_):
                link(V.tensor_tensor(onehot, each(iota_row, TOPK), over(idx_f[:, t, 0:TOPK], E), ALU.is_equal))
                V.tensor_tensor(chosen[:, 0], onehot, each(dest[:, t], TOPK), ALU.mult)
                link(V.tensor_tensor(chosen[:, 1], onehot, each(scores[:, t], TOPK), ALU.mult))
                V.tensor_reduce(dest_k[:, t], chosen[:, 0], AX.X, ALU.add)
                link(V.tensor_reduce(w_tok[:, t], chosen[:, 1], AX.X, ALU.add))
            V.tensor_copy(dest_i, dest_k.rearrange("p t k -> p (t k)")).then_inc(s_dst, 1)
            link(V.tensor_reduce(w_sum, w_tok, AX.X, ALU.add))
            link(V.reciprocal(w_sum, w_sum))
            link(V.scalar_tensor_tensor(w_tok, w_tok, SCALE_R, over(w_sum, TOPK), ALU.mult, ALU.mult))
            dve.wait_ge(s_bt, 1)
            V.tensor_copy(erow, bank(4)[0:1, 0:P]).then_inc(s_brow, 1)
            for t in range(LT_):
                for half in range(2):
                    n = 2 * t + half
                    cs = slice(half * 512, (half + 1) * 512)
                    dve.wait_ge(s_shy, n + 1)
                    link(V.tensor_tensor(acc2[:, 0, cs], bank(6 + half), rows[:, 3, cs], ALU.mult))
                    V.tensor_tensor(x1[:, t, cs], x1[:, t, cs], acc2[:, 0, cs], ALU.add).then_inc(s_shx, 1)
            dve.wait_ge(s_slot, 16)
            V.tensor_scalar(tokens, slots, 3, None, ALU.logical_shift_right).then_inc(s_tok, 1)
            for u in range(2):
                dve.wait_ge(s_xt, u + 1)
                rowsT_high(u).then_inc(s_xeb, 1)
            dve.wait_ge(s_brow, 2)
            steps_n = nc.vector.value_load(nstep[0:1, 0:1], min_val=1, max_val=NPAIR_IT)
            with dve.Fori(0, NPAIR_IT) as i:
                with dve.If(i < steps_n):
                    for u in range(2):
                        dve.wait_ge(s_sg, i * 2 + u + 1)
                        V.tensor_tensor(hh[:, u, :], bank(u)[:, DE:2 * DE], sg[:, u, :], ALU.mult).then_inc(s_h, 1)
                    for u in range(2):
                        dve.wait_ge(s_th, i * 2 + u + 1)
                        V.tensor_copy(hhT[:, u], bank(2)[:, 2 * u * P:(2 * u + 2) * P].rearrange(
                            "p (f n) -> p f n", f=2)).then_inc(s_hte, 1)
                        dve.wait_ge(s_xt, i * 2 + u + 3)
                        rowsT_high(u).then_inc(s_xeb, 1)
                        dve.wait_ge(s_ym, i * 4 + 2 * u + 2)
                        dve.wait_ge(s_sca[u], i * 16)
                        V.tensor_copy(yo[:, u, 512:1024], bank(6)).then_inc(s_yeb, 1)
            dve.wait_ge(s_fl, 16)
            for t in range(LT_):
                a, b = acc2[:, 0], acc2[:, 1]
                dve.wait_ge(s_yl[t % 2], 16 * (t // 2 + 1))
                link(V.tensor_scalar(a, y_in[:, t % 2, 0, :], w_tok[:, t, 0:1], None, ALU.mult))
                for k in range(1, TOPK):
                    link(V.scalar_tensor_tensor(a, y_in[:, t % 2, k, :], w_tok[:, t, k:k + 1], a, ALU.mult, ALU.add))
                link(V.tensor_tensor(b, a, rows[:, 3], ALU.mult))
                V.tensor_tensor(x1[:, t], x1[:, t], b, ALU.add).then_inc(s_cmb, 1)
                dve.wait_ge(s_ss3, t + 1)
                V.tensor_scalar(small[:, 24 + t:25 + t], small[:, 16 + t:17 + t], 1.0 / D, EPS, ALU.mult,
                                ALU.add).then_inc(s_rs3, 1)
                dve.wait_ge(s_rs3, 2 * t + 2)
                link(V.reciprocal(small[:, 40 + t:41 + t], small[:, 32 + t:33 + t]))
                V.scalar_tensor_tensor(x_out[t], x1[:, t], small[:, 40 + t:41 + t], fin_row, ALU.mult,
                                       ALU.mult).then_inc(s_fo, 1)


def kernel(**inputs):
    import numpy as np
    import concourse.bacc as bacc
    from concourse.bass_utils import run_bass_kernel_spmd

    arrays = host_arrays(inputs, np)
    nc = bacc.Bacc("TRN2", target_bir_lowering=False, num_devices=1)
    d = {n: nc.dram_tensor("in_" + n, a.shape, mybir.dt.from_np(a.dtype), kind="ExternalInput").ap()
         for n, a in arrays.items()}
    d["out"] = nc.dram_tensor("out_x", (L, D), F32, kind="ExternalOutput").ap()
    build(nc, d)
    r = run_bass_kernel_spmd(nc, [{"in_" + n: a for n, a in arrays.items()}], core_ids=[0])
    return r.results[0]["out_x"].reshape(1, L, D)


def host_arrays(inputs, np):
    x = {k: np.asarray(v) for k, v in inputs.items()}

    def chunks(w, n):
        k = w.shape[0] // P
        return np.ascontiguousarray(
            w.reshape(k, P, w.shape[1] // n, n).transpose(2, 1, 0, 3)).reshape(w.shape[1] // n, P, k, n)

    def columns(v):
        return np.ascontiguousarray(v.reshape(-1, P).T)

    w_in = x["w_in"][0]
    n_x, n_dt = D_XBC, 2 * HEADS
    pos = np.arange(L, dtype=np.float64)
    mlp = np.zeros((P, 6), np.float32)
    for i, n in enumerate(("hy_b1", "hy_b2", "hy_b3")):
        mlp[0:64, i] = x[n][0]
    mlp[0:64, 3:6] = x["hy_freq"][0].T
    consts = {"neg_t": columns((-(pos / (L - 1))).astype(np.float32)),
              "not_t0": columns((pos > 0).astype(np.float32)),
              "mlp": mlp, "jcol": np.arange(P, dtype=np.float32)[:, None]}
    named = {"c": x["c"], "c_ctx": x["c_ctx"], "norm1_g": x["norm1_g"], "norm2_g": x["norm2_g"],
             "ada_b": x["ada_b"], "ssm_norm_g": x["ssm_norm_g"], "ssm_w": x["ssm_conv_w"],
             "ssm_b": x["ssm_conv_b"], "hy_w": x["hy_conv_w"], "hy_b": x["hy_conv_b"]}
    cols = np.concatenate([consts[n] if n in consts else columns(named[n]) for n in COLS], axis=1)
    j, i = np.arange(P)[:, None], np.arange(P)[None, :]
    f32 = lambda a: np.ascontiguousarray(a, dtype=np.float32)
    omega = np.pi * (2 * pos + 1) / (2 * L)
    ang = pos[:, None] * omega[None, :]
    fwd = np.stack([np.cos(ang), np.sin(ang)])
    inv = np.stack([np.cos(ang).T, np.sin(ang).T]) / L
    tables = np.stack([fwd, inv]).reshape(2, 2, LT_, P, L).transpose(3, 0, 1, 2, 4)
    bands = np.linspace(1e-4, 15, 16)
    pa = (2.0 * np.pi / L) * pos[:, None] * bands[None, :]
    zpos = np.concatenate([(pos / (L - 1))[:, None], np.cos(pa), -np.sin(pa)], axis=-1)
    out = {
        "x": x["x"][0], "ctx": x["ctx"][0], "cols": cols,
        "ident": f32(j == i), "tri_le": f32(j <= i), "tri_gt": f32(j > i), "tri_ge": f32(j >= i),
        "tri_lt": f32(j < i),
        "ada": chunks(x["ada_w"][0], W_CHUNK),
        "w_in": chunks(np.concatenate([w_in[:, 0:n_x], w_in[:, n_x + n_dt:]], axis=1), W_CHUNK),
        "w_dt": chunks(w_in[:, n_x:n_x + n_dt], n_dt)[0],
        "rows_ssd": np.concatenate([x["ssm_dt_bias"].reshape(-1), x["ssm_a_log"].reshape(-1),
                                    x["ssm_d"].reshape(-1)]),
        "w_hy_out": chunks(x["w_hy_out"][0], W_CHUNK), "w_ssm_out": chunks(x["w_ssm_out"][0], W_CHUNK),
        "w_o": chunks(x["w_o"][0], W_CHUNK),
        "dft": f32(tables),
        "zpos": f32(zpos.T), "hy_w1": x["hy_w1"][0],
        "hy_w23": np.ascontiguousarray(np.stack([x["hy_w2"][0], x["hy_w3"][0]], axis=1)),
        "hy_w_out": x["hy_w_out"][0], "hy_decay": x["hy_decay"].reshape(-1), "hy_bias": x["hy_bias"].reshape(-1),
        "router_w": np.ascontiguousarray(x["router_w"][0].reshape(KD, P, E).transpose(1, 0, 2)),
        "router_bias": x["router_bias"][0], "final_g": x["final_g"],
        "w_gu": np.ascontiguousarray(
            np.stack([x["e_w_gate"][0], x["e_w_up"][0]], axis=2).reshape(E, KD, P, 2 * DE).transpose(0, 2, 1, 3)),
        "w_down": np.ascontiguousarray(x["e_w_down"][0].reshape(E, 2, P, D).transpose(0, 2, 1, 3)),
        "sh_gu": np.ascontiguousarray(
            np.stack([x["sh_w_gate"][0], x["sh_w_up"][0]], axis=1).reshape(KD, P, 2 * DE).transpose(1, 0, 2)),
        "sh_down": np.ascontiguousarray(x["sh_w_down"][0].reshape(2, P, D).transpose(1, 0, 2)),
        "pair_ids": ((np.arange(LT_)[None, :, None] * P + np.arange(P)[:, None, None]) * PAIR_STRIDE
                     + np.arange(TOPK)[None, None, :]).reshape(P, LT_ * TOPK).astype(np.int32),
        "iota64": np.tile(np.arange(E, dtype=np.float32), (P, 1)),
    }
    return {n: np.ascontiguousarray(a) for n, a in out.items()}
```

```python
from contextlib import ExitStack

import concourse.bass as bass
from concourse import mybir

ALU = mybir.AluOpType
ACT = mybir.ActivationFunctionType
AX = mybir.AxisListType
F32 = mybir.dt.float32
I32 = mybir.dt.int32
U32 = mybir.dt.uint32

P = 128
D = 1024
KD = D // P
L = 512
LT_ = L // P
LC = 256
CT_ = LC // P
TA = LT_ + CT_
HEADS, HD, GROUPS, NS = 16, 64, 2, 128
D_XBC = D + 2 * GROUPS * NS
N_HY = 3 * D
EPS = 1e-6
HQ = 256
W_CHUNK = 256
RING = 4
E, TOPK, DE = 64, 6, 256
EG, TOPG = 8, 4
SCALE_R = 2.5
PAIR_STRIDE = 8
PAD_PAIR = L * PAIR_STRIDE
MAX_BLOCKS = E + (L * TOPK - E) // P
NPAIR_IT = (MAX_BLOCKS + 1) // 2
NBLK = 2 * NPAIR_IT + 2
TWO_PI = 6.283185307179586
TP_HI = 6.28125
TP_LO = TWO_PI - TP_HI
ROUND_MAGIC = 12582912.0
PI_SAFE = 3.1415925

COLS = {}
_at = 0
for _n, _w in (("c", 8), ("c_ctx", 8), ("norm1_g", 8), ("norm2_g", 8), ("ada_b", 48), ("ssm_norm_g", 8),
               ("ssm_w", 36), ("ssm_b", 12), ("hy_w", 72), ("hy_b", 24), ("neg_t", 4), ("not_t0", 4),
               ("mlp", 6), ("jcol", 1)):
    COLS[_n] = (_at, _at + _w)
    _at += _w
N_COLS = _at
ADA_EARLY = [("ada", j) for j in range(8)]
XBC_CHUNKS = [("w_in", j) for j in range(6)]
Z_CHUNKS = [("w_in", j) for j in range(6, 10)]
HY_CHUNKS = [("w_in", 10 + j) for j in (8, 9, 10, 11, 0, 1, 2, 3, 4, 5, 6, 7)]
GATE_CHUNKS = [("w_in", 22 + j) for j in range(8)]
HYO_CHUNKS = [("w_hy_out", j) for j in range(4)]
SSO_CHUNKS = [("w_ssm_out", j) for j in range(4)]
ADA_LATE = [("ada", j) for j in range(8, 24)]
WO_CHUNKS = [("w_o", j) for j in range(4)]
RING_ITEMS = (ADA_EARLY + XBC_CHUNKS + Z_CHUNKS + HY_CHUNKS + GATE_CHUNKS + HYO_CHUNKS + SSO_CHUNKS
              + ADA_LATE + WO_CHUNKS)
AT_ADA1 = 0
AT_XBC = AT_ADA1 + 8
AT_Z = AT_XBC + 6
AT_HY = AT_Z + 4
AT_GATE = AT_HY + 12
AT_HYO = AT_GATE + 8
AT_SSO = AT_HYO + 4
AT_ADA2 = AT_SSO + 4
AT_WO = AT_ADA2 + 16
N_RING = AT_WO + 4
assert N_RING == len(RING_ITEMS)

SSM_TILES = []
for _m in range(12):
    _kind = ("xs", _m) if _m < 8 else ("B", _m - 8) if _m < 10 else ("C", _m - 10)
    SSM_TILES.append((AT_XBC + _m // 2, _m % 2, "ssm", _m, False) + _kind)
    if _m < 10:
        SSM_TILES.append((AT_XBC + _m // 2, _m % 2, "ssm", _m, True) + _kind)
HY_TILES = []
for _i in range(24):
    _part, _m = ("v", _i) if _i < 8 else ("p0", _i - 8) if _i < 16 else ("p1", _i - 16)
    _conv = {"v": 16, "p0": 0, "p1": 8}[_part] + _m
    HY_TILES.append((AT_HY + _i // 2, _i % 2, "hy", _conv, False, _part, _m))


def col(cols, name, i=0, n=1):
    at = COLS[name][0] + i
    return cols[:, at:at + n]


def over(ap, n):
    return ap.unsqueeze(2).to_broadcast([ap.shape[0], ap.shape[1], n])


def each(ap, n):
    return ap.unsqueeze(1).to_broadcast([ap.shape[0], n, ap.shape[1]])


def build(nc, d):
    with ExitStack() as ctx:
        arena_len = 53200
        arena = ctx.enter_context(nc.sbuf_tensor("arena", [P, arena_len], F32))
        ps = ctx.enter_context(nc.psum_tensor("ps", [P, 8, 512], F32))

        class Region:

            def __init__(self, at):
                self.at = at

            def take(self, *shape, parts=P, dtype=F32):
                n = 1
                for s in shape:
                    n *= s
                v = arena[0:parts, self.at:self.at + n]
                self.at += n
                assert self.at <= arena_len, self.at
                if dtype is not F32:
                    v = v.bitcast(dtype)
                if len(shape) == 1:
                    return v
                names = "abcd"[:len(shape)]
                sizes = {k: s for k, s in zip(names, shape)}
                return v.rearrange(f"p ({' '.join(names)}) -> p {' '.join(names)}", **sizes)

        fixed = Region(0)
        ident = fixed.take(P)
        tri_le, tri_gt, tri_ge, tri_lt = (fixed.take(P) for _ in range(4))
        ones = fixed.take(P)
        cols = fixed.take(N_COLS + N_COLS % 2)
        silu_c = fixed.take(KD, 2)
        mod = fixed.take(48, 2)
        scale1 = fixed.take(KD, 2)
        scale2 = fixed.take(KD)
        small = fixed.take(64)
        ring_at = fixed.at
        ring = fixed.take(RING, KD, W_CHUNK)
        yT = fixed.take(KD, L)
        hT = fixed.take(KD, L + LC)
        phase_at = fixed.at

        r = Region(phase_at)
        xin = r.take(TA, D)
        junk = r.take(D)
        modrow = r.take(2, W_CHUNK, parts=2)

        r = Region(phase_at)
        xs_tok = r.take(TA, D)
        BT = r.take(GROUPS, L)
        CT = r.take(GROUPS, L)
        B_tok = r.take(TA, GROUPS * NS)
        zs = r.take(LT_, D)
        xdt = r.take(2, 2, D)
        xdte = r.take(D)
        sb_in = r.take(LT_, D)
        sf_in = r.take(D)
        seg_rhs = r.take(2, 4, P)
        decay = r.take(2, 2, 4, P)
        cbm = r.take(2, LT_, GROUPS, P)
        acc = decay.rearrange("p a b c e -> p (a b c e)")[:, 0:3 * L].rearrange("p (a b) -> p a b", a=3)
        squares = r.take(512)
        y1 = r.take(D)
        y2 = r.take(D)
        w_dt = y1[:, 0:KD * 32].rearrange("p (k n) -> p k n", k=KD)
        dtw = xdte[:, 0:5 * 192].rearrange("p (w t n) -> p w t n", w=5, t=TA)
        dt_tok = r.take(TA, 32)
        a_tok = r.take(TA, 32)
        ecs = r.take(TA, 96)
        dte = r.take(TA, 32)
        rows_ssd = r.take(80)
        v_ss = small[:, 0:8]
        v_rstd = small[:, 8:16]
        ssd_end = r.at

        r = Region(phase_at)
        dft_f = r.take(2, LT_, 256)
        dft_i = r.take(2, 2, 512)
        filt = r.take(2, LT_, HQ)
        y4 = r.take(2, 2, 2 * HQ)
        v_tok = r.take(LT_, D)
        p0_tok = r.take(LT_, D)
        p1T = r.take(KD, L)
        spec = r.take(2, 2, 2 * HQ)
        u4 = r.take(2, 2, 2 * HQ)
        prod_a = r.take(2, 2, 2 * HQ)
        prod_b = r.take(2, 2, 2 * HQ)
        odd = r.take(2, 2 * HQ)
        w_f = r.take(2, HQ, parts=64)
        hdnT = r.take(L, parts=64)
        hy_w1 = r.take(64, parts=33)
        hy_w23 = r.take(2, 64, parts=64)
        decay_row = r.take(HQ)
        skip_row = r.take(HQ, parts=1)
        window = r.take(LT_, HQ)
        h_bwd = r.take(LT_, HQ)
        acc_hy = u4.rearrange("p a b c -> p (a b c)")[:, 0:3 * L].rearrange("p (a b) -> p a b", a=3)
        zpos = prod_a.rearrange("p a b c -> p (a b c)")[0:33, 0:L]
        sin_arg, sin_n, sin_r = (prod_a.rearrange("p a b c -> p (a b c)")[0:64, (1 + i) * L:(2 + i) * L]
                                 for i in range(3))

        r = Region(phase_at)
        gates = r.take(2, KD, L)
        mergedT = r.take(KD, L)
        x1 = r.take(LT_, D)
        after_x1 = r.at
        r.take(KD, L)
        rows = r.take(4, D)
        h2 = r.take(LT_, D)
        squares2 = r.take(D)
        modrow_late = r.take(2, W_CHUNK, parts=2)
        xmix = r.take(2, W_CHUNK)
        router_w = r.take(KD, E)
        bias_row = r.take(E)
        iota_row = r.take(E)
        pair_ids = r.take(LT_ * TOPK, dtype=I32)

        r = Region(ring_at)
        gu_w = r.take(3, KD, 2 * DE)
        down_w = r.take(3, 2, D)
        assert r.at <= phase_at
        h2T = r.take(KD, L)
        shg = r.take(2, L)
        sg = r.take(2, DE)
        hh = r.take(2, DE)
        hhT = r.take(2, 2, P)
        yo = r.take(2, D)
        scores = r.take(LT_, E)
        sel = r.take(LT_, E + 8)
        grp8 = r.take(EG, 8)
        grp = r.take(16)
        grp_top = r.take(8)
        grp_rep = r.take(8)
        grp_mark = r.take(16)
        keep = r.take(8)
        drop = r.take(8)
        top8 = r.take(LT_, 8)
        top_rep = r.take(8)
        marked = r.take(E + 8)
        mask = r.take(LT_, E)
        idx_u = r.take(LT_, 8, dtype=U32)
        idx_f = r.take(LT_, 8)
        w_tok = r.take(LT_, TOPK)
        w_sum = r.take(LT_)
        counts = r.take(E)
        nblk = r.take(E)
        cend = r.take(E)
        base = r.take(E)
        rank = r.take(LT_, E)
        over_b = r.take(LT_, E)
        dest = r.take(LT_, E)
        picked = r.take(E)
        dest_k = r.take(LT_, TOPK)
        dest_i = r.take(LT_ * TOPK, dtype=I32)
        ecol = r.take(2)
        erow = r.take(P, dtype=I32, parts=1)
        nstep = r.take(4, dtype=I32, parts=1)
        nstep_f = r.take(4, parts=1)
        pad_tab = r.take(NBLK, dtype=I32)
        slots = r.take(NBLK, dtype=I32)
        tokens = r.take(NBLK, dtype=I32)
        idx_g = r.take(2, 1, dtype=I32)
        idx_s = r.take(2, 1, dtype=I32)
        onehot = r.take(TOPK, E)
        assert r.at <= phase_at + 3 * KD * L, r.at
        r = Region(after_x1)
        xg = r.take(2, D)
        xgT = r.take(2, KD, P)
        chosen = xgT[:, 0].rearrange("p k n -> p (k n)")[:, 0:2 * TOPK * E].rearrange(
            "p (a k e) -> p a k e", a=2, k=TOPK)
        y_in = Region(ring_at).take(2, TOPK, D)
        acc2 = Region(phase_at).take(2, D)
        fin_row = h2[:, 0]
        x_out = [h2[:, 1], h2[:, 2], h2[:, 3], rows[:, 0]]

        def sem(name):
            return ctx.enter_context(nc.semaphore(name))

        s_const = sem("constants_loaded")
        s_x = sem("x_loaded")
        s_ring = [sem(f"ring_loaded_{i}") for i in range(RING)]
        s_pe = sem("phases_ended")
        s_silu_c = sem("silu_c_ready")
        s_modmm = sem("mod_rows_summed")
        s_modrow = sem("mod_row_copied")
        s_modtr = sem("mod_rows_turned")
        s_mod = sem("mod_columns_ready")
        s_ss = sem("x_squares_summed")
        s_rs = sem("x_rstd_step")
        s_xn = sem("x_normalised")
        s_htr = sem("h_turned")
        s_hT = sem("hT_written")
        s_proj = sem("tile_projected")
        s_cva = sem("conv_centre_done")
        s_cvm = sem("conv_left_done")
        s_cv = sem("conv_done")
        s_sl = sem("silu_done")
        s_tr = sem("tile_turned")
        s_te = sem("turned_tile_copied")
        s_w_dt = sem("w_dt_loaded")
        s_dtmm = sem("dt_projected")
        s_dt = sem("dt_steps")
        s_dta = sem("dt_act_steps")
        s_zmm = sem("z_projected")
        s_z = sem("z_silu_done")
        s_cs = sem("cumulative_sums_done")
        s_ecs = sem("decays_ready")
        s_cb = sem("cb_done")
        s_cbm = sem("cb_masked")
        s_dte = sem("dt_to_end_ready")
        s_xe = sem("xdte_ready")
        s_st = sem("chunk_state_done")
        s_stu = sem("state_updated")
        s_xdt = sem("xdt_ready")
        s_rhs = sem("segment_rhs_ready")
        s_seg = sem("segments_summed")
        s_exp = sem("segments_exponentiated")
        s_msk = sem("decay_masked")
        s_y = sem("y_quad_done")
        s_off = sem("y_off_done")
        s_offr = sem("y_off_read")
        s_dve = sem("vector_steps")
        s_yc = sem("chunk_gated")
        s_vss = sem("gated_squares_summed")
        s_vr = sem("gated_rstd_ready")
        s_vn = sem("gated_normalised")
        s_ytr = sem("y_turned")
        s_yT = sem("yT_written")
        s_hyin = sem("filter_network_loaded")
        s_fb = sem("freq_bias_ready")
        s_mlp = sem("filter_layer_summed")
        s_arg = sem("sine_argument_ready")
        s_red = sem("sine_argument_reduced")
        s_sin = sem("sine_done")
        s_dft = sem("dft_tables_loaded")
        s_rows = sem("filter_rows_loaded")
        s_drow = sem("decay_row_positive")
        s_fmm = sem("filter_summed")
        s_win = sem("window_ready")
        s_hb = sem("backward_filter_copied")
        s_fd = sem("filter_parts_ready")
        s_fp = sem("filter_windowed")
        s_kmm = sem("filter_spectrum_summed")
        s_kod = sem("filter_odd_part_copied")
        s_kb = sem("filter_spectrum_ready")
        s_umm = sem("signal_spectrum_summed")
        s_uod = sem("signal_odd_part_copied")
        s_ub = sem("signal_spectrum_ready")
        s_pa = sem("like_products_ready")
        s_pb = sem("cross_products_ready")
        s_yq = sem("product_spectrum_ready")
        s_ua = sem("product_transforms_ready")
        s_imm = sem("output_in_time_summed")
        s_iv = sem("output_in_time_gated")
        s_mp = sem("merge_tile_summed")
        s_gt = sem("gate_ready")
        s_mg = sem("merge_tile_gated")
        s_mga = sem("merged_ready")
        s_x1l = sem("residual_loaded")
        s_mod2 = sem("late_modulation_ready")
        s_rowmm = sem("modulation_row_spread")
        s_row = sem("modulation_row_copied")
        s_xmm = sem("mixer_output_summed")
        s_x1 = sem("residual_updated")
        s_ss2 = sem("residual_squares_summed")
        s_rs2 = sem("residual_rstd_step")
        s_h2 = sem("h2_ready")
        s_h2st = sem("h2_stored")
        s_h2t = sem("h2_turned")
        s_h2T = sem("h2T_written")
        s_rw = sem("router_loaded")
        s_lg = sem("logits_summed")
        s_sc0 = sem("scores_ready")
        s_msk2 = sem("expert_mask_ready")
        s_rk = sem("ranks_summed")
        s_be = sem("block_experts_ready")
        s_bt = sem("block_experts_turned")
        s_brow = sem("block_row_ready")
        s_dst = sem("slots_ready")
        s_pad = sem("slot_table_padded")
        s_scat = sem("pairs_scattered")
        s_slot = sem("slot_table_loaded")
        s_tok = sem("token_table_ready")
        s_shl = sem("shared_weights_loaded")
        s_shm = sem("shared_hidden_summed")
        s_sha = sem("shared_silu_done")
        s_shh = sem("shared_hidden_ready")
        s_shy = sem("shared_output_summed")
        s_shx = sem("shared_output_added")
        s_pi = sem("pool_index_ready")
        s_pseen = sem("pool_waits_met")
        s_gu = sem("block_hidden_summed")
        s_sg = sem("block_silu_done")
        s_h = sem("block_hidden_ready")
        s_th = sem("hidden_turned")
        s_hte = sem("hiddenT_copied")
        s_xt = sem("rows_turned")
        s_xea = sem("rowsT_low_copied")
        s_xeb = sem("rowsT_high_copied")
        s_ym = sem("block_output_summed")
        s_yea = sem("output_low_copied")
        s_yeb = sem("output_high_copied")
        s_fl = sem("final_gain_loaded")
        s_cmb = sem("token_sum_ready")
        s_ss3 = sem("final_squares_summed")
        s_rs3 = sem("final_rstd_step")
        s_fo = sem("output_tile_ready")
        s_xz = sem("rows_cleared")
        s_gul = [sem(f"gate_up_loaded_{u}") for u in range(2)]
        s_dnl = [sem(f"down_loaded_{u}") for u in range(2)]
        s_xg = [sem(f"rows_gathered_{u}") for u in range(2)]
        s_sca = [sem(f"outputs_scattered_{u}") for u in range(2)]
        s_yl = [sem(f"token_outputs_loaded_{u}") for u in range(2)]
        s_out = sem("stores_done")

        def bank(b):
            return ps[:, b, :]

        h2_dram = nc.dram_tensor("h2_rows", (L, D), F32, kind="Internal").ap()
        y_dram = nc.dram_tensor("pair_outputs", (L * PAIR_STRIDE, D), F32, kind="Internal").ap()
        slot_dram = nc.dram_tensor("slot_table", (P * NBLK, 1), I32, kind="Internal").ap()

        freed = {}
        for j in range(8):
            freed[AT_ADA1 + j] = (s_modmm, j + 1)
        for g, t in enumerate(SSM_TILES):
            freed[t[0]] = (s_proj, g + 1)
        for j in range(4):
            freed[AT_Z + j] = (s_zmm, LT_ * (j + 1))
        for g, t in enumerate(HY_TILES):
            freed[t[0]] = (s_proj, len(SSM_TILES) + g + 1)

        for n in range(32):
            freed[AT_GATE + n // 2] = (s_mp, n + 1)
        for n in range(8, 24):
            freed[AT_ADA2 + n - 8] = (s_modmm, n + 1)
        tiles = SSM_TILES + HY_TILES

        def ring_wait(eng, item):
            eng.wait_ge(s_ring[item % RING], 16 * (item // RING + 1))

        def phase_end(eng, n):
            eng.sem_inc(s_pe, 1)
            eng.wait_ge(s_pe, 4 * n)

        SSM_TURNED = sum(t[5] != "C" for t in SSM_TILES)
        DT_READY = 4
        STATE_UPDATES = [(0, 4), (0, 5), (1, 5), (1, 4), (1, 3), (1, 2), (1, 1), (0, 0), (0, 1), (0, 2)]

        def turned_before(g):
            return sum(t[5] in ("xs", "B", "v", "p0") for t in tiles[:g])

        def silu_before(g):
            return sum(t[2] == "ssm" for t in tiles[:g])

        def in_ring(t):
            return t[5] in ("xs", "v", "p0") or (t[5] == "B" and t[4])

        def conv_out(g):
            item, c, conv, ct, is_ctx, what, m = tiles[g]
            n = LC if is_ctx else L
            if in_ring(tiles[g]):
                return (acc if conv == "ssm" else acc_hy)[:, sum(map(in_ring, tiles[:g])) % 3, 0:n]
            return {"B": BT, "C": CT, "p1": p1T}[what][:, m, :]

        def conv_pe(pe, g0, g1, first):
            for g in range(g0, g1):
                item, c, conv, ct, is_ctx, what, m = tiles[g]
                n, t0 = (LC, L) if is_ctx else (L, 0)
                ring_wait(pe, item)
                if g >= first + 4:
                    pe.wait_ge(s_cv, g - 3)
                for k in range(KD):
                    mm = nc.tensor.matmul(bank(g % 4)[:, 0:n], ring[:, item % RING, k, c * P:(c + 1) * P],
                                          hT[:, k, t0:t0 + n], start=(k == 0), stop=(k == KD - 1))
                mm.then_inc(s_proj, 1)
                if g > g0:
                    turn_pe(pe, g - 1, first)
            turn_pe(pe, g1 - 1, first)

        def turn_pe(pe, g, first):
            t = tiles[g]
            if t[5] not in ("xs", "B", "v", "p0"):
                return
            j = turned_before(g)
            if t[2] == "ssm":
                pe.wait_ge(s_sl, silu_before(g) + 1)
            else:
                pe.wait_ge(s_cv, g + 1)
            if j >= turned_before(first) + 2:
                pe.wait_ge(s_te, j - 1)
            for i in range(CT_ if t[4] else LT_):
                src = conv_out(g)[:, i * P:(i + 1) * P]
                if t[2] == "hy":
                    src = conv_out(g).rearrange("p (h t a) -> p a h t", a=2, h=2)[:, i // 2, i % 2]
                mm = nc.tensor.transpose(bank(4 + j % 2)[:, i * P:(i + 1) * P], src, ident)
            mm.then_inc(s_tr, 1)

        def conv_act(act, g0, g1, first):
            for g in range(g0, g1):
                item, c, conv, ct, is_ctx, what, m = tiles[g]
                out = conv_out(g)
                act.wait_ge(s_proj, g + 1)
                if in_ring(tiles[g]):
                    before = [h for h in range(first, g) if in_ring(tiles[h])]
                    if len(before) >= 3:
                        act.wait_ge(s_tr, turned_before(before[-3]) + 1)
                ctn = 12 if conv == "ssm" else 24
                nc.scalar.activation(out, bank(g % 4)[:, 0:out.shape[1]], ACT.Identity,
                                     scale=col(cols, conv + "_w", ctn + ct),
                                     bias=col(cols, conv + "_b", ct)).then_inc(s_cva, 1)
                if conv == "ssm":
                    act.wait_ge(s_cv, g + 1)
                    nc.scalar.activation(out, out, ACT.Silu).then_inc(s_sl, 1)
                if g > g0:
                    turned_act(act, g - 1)
            turned_act(act, g1 - 1)

        def turned_act(act, g):
            t = tiles[g]
            if t[5] not in ("xs", "B", "v", "p0"):
                return
            j = turned_before(g)
            n, t0 = (CT_, LT_) if t[4] else (LT_, 0)
            dst = {"xs": xs_tok, "B": B_tok, "v": v_tok, "p0": p0_tok}[t[5]]
            act.wait_ge(s_tr, j + 1)
            nc.scalar.copy(dst[:, t0:t0 + n, t[6] * P:(t[6] + 1) * P],
                           bank(4 + j % 2)[:, 0:n * P].rearrange("p (t c) -> p t c", c=P)).then_inc(s_te, 1)

        def conv_dve(dve, g0, g1):
            for g in range(g0, g1):
                item, c, conv, ct, is_ctx, what, m = tiles[g]
                out, ctn = conv_out(g), 12 if conv == "ssm" else 24
                n = out.shape[1]
                dve.wait_ge(s_cva, g + 1)
                nc.vector.scalar_tensor_tensor(out[:, 1:n], bank(g % 4)[:, 0:n - 1], col(cols, conv + "_w", ct),
                                               out[:, 1:n], ALU.mult, ALU.add).then_inc(s_cvm, 1)
                dve.wait_ge(s_cvm, g + 1)
                nc.vector.scalar_tensor_tensor(out[:, 0:n - 1], bank(g % 4)[:, 1:n],
                                               col(cols, conv + "_w", 2 * ctn + ct), out[:, 0:n - 1],
                                               ALU.mult, ALU.add).then_inc(s_cv, 1)

        def row_buf(n):
            return modrow if n < 8 else modrow_late

        def mod_chunk(pe, n, item):
            ring_wait(pe, item)
            if n == 0:
                pe.wait_ge(s_silu_c, 2)
            if n >= 2:
                pe.wait_ge(s_modrow, n - 1)
            for k in range(KD):
                mm = nc.tensor.matmul(bank(n % 2)[0:2, 0:W_CHUNK], silu_c[:, k, :], ring[:, item % RING, k, :],
                                      start=(k == 0), stop=(k == KD - 1))
            mm.then_inc(s_modmm, 1)
            if n >= 1 and n != 8:
                mod_turn(pe, n - 1)
            if n in (7, 23):
                mod_turn(pe, n)

        def mod_turn(pe, n):
            pe.wait_ge(s_modrow, n + 1)
            for i in range(2):
                mm = nc.tensor.transpose(bank(2)[:, 2 * (2 * n + i):2 * (2 * n + i) + 2],
                                         row_buf(n)[0:2, n % 2, i * P:(i + 1) * P], ident[0:2, 0:2])
            mm.then_inc(s_modtr, 1)

        def mod_rows_act(act, n0, n1):
            for n in range(n0, n1):
                act.wait_ge(s_modmm, n + 1)
                if n >= n0 + 2:
                    act.wait_ge(s_modtr, n - 1)
                nc.scalar.copy(row_buf(n)[0:2, n % 2, :], bank(n % 2)[0:2, 0:W_CHUNK]).then_inc(s_modrow, 1)

        def pool_xdte(pool, u, dirn, c):
            if u == 0:
                pool.wait_ge(s_dte, 1)
                pool.wait_ge(s_te, SSM_TURNED)
            else:
                pool.wait_ge(s_st, u)
            nc.gpsimd.tensor_tensor(xdte.rearrange("p (h e) -> p h e", e=HD),
                                    xs_tok[:, c].rearrange("p (h e) -> p h e", e=HD),
                                    over(dte[:, c, 16 * dirn:16 * dirn + 16], HD), ALU.mult).then_inc(s_xe, 1)

        def state_pe(pe, u):
            dirn, c = STATE_UPDATES[u]
            pe.wait_ge(s_xe, u + 1)
            if u < 7:
                if u >= 1:
                    pe.wait_ge(s_stu, u)
            else:
                pe.wait_ge(s_offr, 2 * (u - 7) + 2)
            for g in range(GROUPS):
                mm = nc.tensor.matmul(bank(4 + g), B_tok[:, c, g * NS:(g + 1) * NS],
                                      xdte[:, g * 512:(g + 1) * 512], start=True, stop=True)
            mm.then_inc(s_st, 1)

        def state_dve(dve, link, u):
            dirn, c = STATE_UPDATES[u]
            new = ps[:, 4:6, :].rearrange("p b (h e) -> p (b h) e", e=HD)
            heads = lambda ap: ap.rearrange("p (h e) -> p h e", e=HD)
            src, dst = {0: (None, sf_in), 1: (sf_in, sf_in), 2: (None, sb_in[:, 3]),
                        3: (sb_in[:, 3], sb_in[:, 3]), 4: (sb_in[:, 3], sb_in[:, 2]),
                        5: (sb_in[:, 2], sb_in[:, 1]), 6: (sb_in[:, 1], sb_in[:, 0])}.get(u, (sf_in, sf_in))
            dve.wait_ge(s_st, u + 1)
            if src is None:
                nc.vector.tensor_copy(heads(dst), new).then_inc(s_stu, 1)
            else:
                link(nc.vector.tensor_tensor(heads(dst), heads(src),
                                             over(ecs[:, c, 64 + 16 * dirn:80 + 16 * dirn], HD), ALU.mult))
                nc.vector.tensor_tensor(heads(dst), new, heads(dst), ALU.add).then_inc(s_stu, 1)
            dve.wait_ge(s_stu, u + 1)

        def off_pe(pe, c, dirn):
            if dirn == 0:
                pe.wait_ge(s_stu, 7 + c)
            else:
                pe.wait_ge(s_offr, 2 * c + 1)
            state = sb_in[:, c] if dirn else sf_in
            for g in range(GROUPS):
                mm = nc.tensor.matmul(bank(4 + g), CT[:, g, c * P:(c + 1) * P],
                                      state[:, g * 512:(g + 1) * 512], start=True, stop=True)
            mm.then_inc(s_off, 1)

        def quad_pe(pe, n):
            c, q = n // 4, n % 4
            pe.wait_ge(s_msk, 2 * n + 2)
            if q == 0:
                pe.wait_ge(s_xdt, 2 * c + 2)
                if c >= 1:
                    pe.wait_ge(s_yc, c)
            for i in range(4):
                h = 4 * q + i
                for dirn in range(2):
                    mm = nc.tensor.matmul(bank(6 + h // 8)[:, (h % 8) * HD:(h % 8 + 1) * HD],
                                          decay[:, n % 2, dirn, i, :], xdt[:, c % 2, dirn, h * HD:(h + 1) * HD],
                                          start=(dirn == 0), stop=(dirn == 1))
            mm.then_inc(s_y, 1)

        def gate_squares(act, c):
            act.wait_ge(s_yc, c + 1)
            for g in range(GROUPS):
                if 2 * c + g >= 1:
                    act.wait_ge(s_vss, 2 * c + g)
                nc.scalar.activation(squares, zs[:, c, g * 512:(g + 1) * 512], ACT.Square,
                                     accum_out=v_ss[:, 2 * c + g:2 * c + g + 1]).then_inc(s_vss, 1)

        HY_STEPS = [(q + i, o) for q in range(0, D // HQ, 2) for o in range(2) for i in range(2)]
        N_STEPS = len(HY_STEPS)
        N_SSM, N_ALL = len(SSM_TILES), len(tiles)

        def mlp_pe(pe, layer):
            if layer == 0:
                pe.wait_ge(s_hyin, 48)
                nc.tensor.matmul(bank(6)[0:64, :], hy_w1, zpos, start=True, stop=True).then_inc(s_mlp, 1)
            else:
                pe.wait_ge(s_sin, layer)
                nc.tensor.matmul(bank(6)[0:64, :], hy_w23[:, layer - 1, :], hdnT, start=True,
                                 stop=True).then_inc(s_mlp, 1)

        def mlp_act(act, layer):
            if layer == 0:
                act.wait_ge(s_fb, 1)
            act.wait_ge(s_mlp, layer + 1)
            nc.scalar.activation(sin_arg, bank(6)[0:64, :], ACT.Identity, scale=col(cols, "mlp", 3 + layer)[0:64],
                                 bias=small[0:64, 48 + layer:49 + layer]).then_inc(s_arg, 1)
            act.wait_ge(s_red, layer + 1)
            nc.scalar.activation(hdnT, sin_r, ACT.Sin).then_inc(s_sin, 1)

        def mlp_dve(dve, link, layer):
            dve.wait_ge(s_arg, layer + 1)
            link(nc.vector.tensor_scalar(sin_n, sin_arg, 1.0 / TWO_PI, ROUND_MAGIC, ALU.mult, ALU.add))
            link(nc.vector.tensor_scalar(sin_n, sin_n, ROUND_MAGIC, None, ALU.subtract))
            link(nc.vector.scalar_tensor_tensor(sin_r, sin_n, -TP_HI, sin_arg, ALU.mult, ALU.add))
            link(nc.vector.scalar_tensor_tensor(sin_r, sin_n, -TP_LO, sin_r, ALU.mult, ALU.add))
            nc.vector.tensor_scalar(sin_r, sin_r, PI_SAFE, -PI_SAFE, ALU.min, ALU.max).then_inc(s_red, 1)

        def rows_dma(act, s):
            q, o = HY_STEPS[s]
            c0 = o * D + q * HQ
            if s >= 1:
                act.wait_ge(s_fmm, s)
                act.wait_ge(s_fd, s)
                act.wait_ge(s_win, s)
            src = d["hy_w_out"].rearrange("p (a n) -> p a n", a=2)[:, :, c0:c0 + HQ]
            act.dma_start(w_f, src).then_inc(s_rows, 16)
            act.dma_start(decay_row, d["hy_decay"][c0:c0 + HQ].partition_broadcast(P)).then_inc(s_rows, 16)
            act.dma_start(skip_row, d["hy_bias"][c0:c0 + HQ].partition_broadcast(1)).then_inc(s_rows, 16)

        def filter_pe(pe, s):
            pe.wait_ge(s_rows, 48 * (s + 1))
            if s >= 3:
                pe.wait_ge(s_iv, s - 2)
            for a in range(LT_):
                for way in range(2):
                    mm = nc.tensor.matmul(bank(a)[:, way * HQ:(way + 1) * HQ], hdnT[:, a * P:(a + 1) * P],
                                          w_f[:, way, :], start=True, stop=True)
            mm.then_inc(s_fmm, 1)

        def filter_act(act, s):
            act.wait_ge(s_drow, s + 1)
            if s >= 1:
                act.wait_ge(s_fp, s)
            for a in range(LT_):
                last = nc.scalar.activation(window[:, a, :], decay_row, ACT.Exp, scale=col(cols, "neg_t", a))
            last.then_inc(s_win, 1)
            act.wait_ge(s_fmm, s + 1)
            if s >= 1:
                act.wait_ge(s_fd, s)
            nc.scalar.activation(h_bwd[:, 0, :], ps[:, 0, HQ:], ACT.Identity, scale=col(cols, "not_t0", 0))
            nc.scalar.copy(h_bwd[:, 1:4, :], ps[:, 1:4, HQ:]).then_inc(s_hb, 1)
            if s < N_STEPS - 1:
                rows_dma(act, s + 1)

        def filter_dve(dve, link, s):
            dve.wait_ge(s_rows, 48 * (s + 1))
            nc.vector.scalar_tensor_tensor(decay_row, decay_row, -1.0, decay_row, ALU.mult,
                                           ALU.max).then_inc(s_drow, 1)
            dve.wait_ge(s_hb, s + 1)
            f = ps[:, 0:4, 0:HQ]
            link(nc.vector.tensor_tensor(filt[:, 0], f, h_bwd, ALU.add))
            nc.vector.tensor_tensor(filt[0:1, 0, 0, :], filt[0:1, 0, 0, :], skip_row, ALU.add)
            nc.vector.tensor_tensor(filt[:, 1], f, h_bwd, ALU.subtract).then_inc(s_fd, 1)

        def filter_pool(pool, s):
            pool.wait_ge(s_fd, s + 1)
            pool.wait_ge(s_win, s + 1)
            nc.gpsimd.tensor_tensor(filt[:, 0], filt[:, 0], window, ALU.mult)
            nc.gpsimd.tensor_tensor(filt[:, 1], filt[:, 1], window, ALU.mult).then_inc(s_fp, 1)

        def transform_pe(cos_of, sin_of, done):
            for ft in range(2):
                for par in range(2):
                    for cs, src in enumerate((cos_of, sin_of)):
                        for h in range(2):
                            a = 2 * par + h
                            mm = nc.tensor.matmul(bank(4 + 2 * ft + par)[:, cs * HQ:(cs + 1) * HQ],
                                                  dft_f[:, cs, a, ft * P:(ft + 1) * P], src[:, a, :],
                                                  start=(h == 0), stop=(h == 1))
                mm.then_inc(done, 1)

        def spectrum_pe(pe, s):
            pe.wait_ge(s_fp, s + 1)
            if s >= 1:
                pe.wait_ge(s_ub, s)
            transform_pe(filt[:, 0], filt[:, 1], s_kmm)

        def signal_pe(pe, s):
            q, o = HY_STEPS[s]
            pe.wait_ge(s_kb, s + 1)
            if o:
                pe.wait_ge(s_iv, s - 1)
            v = v_tok[:, :, q * HQ:(q + 1) * HQ]
            transform_pe(v, v, s_umm)

        def odd_act(act, s, mm, read, reads, done):
            if reads:
                act.wait_ge(read, reads)
            for ft in range(2):
                act.wait_ge(mm, 2 * s + ft + 1)
                nc.scalar.copy(odd[:, ft, :], bank(5 + 2 * ft)).then_inc(done, 1)

        def mirror_dve(dve, s, copied, dst, done):
            dve.wait_ge(copied, 2 * s + 2)
            even = ps[:, 4:8, :].rearrange("p (f e) n -> p f e n", e=2)[:, :, 0, :]
            nc.vector.tensor_tensor(dst[:, 0], even, odd, ALU.add)
            nc.vector.tensor_tensor(dst[:, 1], even, odd, ALU.subtract).then_inc(done, 1)

        def product_dve(dve, s):
            u, k = u4.rearrange("p m f (c n) -> p (m f) c n", c=2), spec.rearrange(
                "p m f (c n) -> p (m f) c n", c=2)
            dve.wait_ge(s_ub, s + 1)
            if s >= 1:
                dve.wait_ge(s_yq, s)
            nc.vector.tensor_tensor(prod_a, u4, spec, ALU.mult).then_inc(s_pa, 1)
            b = prod_b.rearrange("p m f (c n) -> p (m f) c n", c=2)
            nc.vector.tensor_tensor(b[:, :, 0, :], u[:, :, 0, :], k[:, :, 1, :], ALU.mult)
            nc.vector.tensor_tensor(b[:, :, 1, :], u[:, :, 1, :], k[:, :, 0, :], ALU.mult).then_inc(s_pb, 1)

        def product_pool(pool, s):
            a, b, y = (t.rearrange("p m f (c n) -> p (m f) c n", c=2) for t in (prod_a, prod_b, u4))
            pool.wait_ge(s_pb, s + 1)
            nc.gpsimd.tensor_tensor(y[:, :, 0, :], a[:, :, 0, :], a[:, :, 1, :], ALU.subtract)
            nc.gpsimd.tensor_tensor(y[:, :, 1, :], b[:, :, 0, :], b[:, :, 1, :], ALU.add).then_inc(s_yq, 1)

        def fold_dve(dve, s):
            dve.wait_ge(s_yq, s + 1)
            if s >= 1:
                dve.wait_ge(s_imm, s)
            nc.vector.tensor_tensor(y4[:, 0], u4[:, 0], u4[:, 1], ALU.add)
            nc.vector.tensor_tensor(y4[:, 1], u4[:, 0], u4[:, 1], ALU.subtract).then_inc(s_ua, 1)

        def inverse_pe(pe, s):
            q, o = HY_STEPS[s]
            pe.wait_ge(s_ua, s + 1)
            if s < N_STEPS - 2:
                pe.wait_ge(s_fd, s + 3)
            else:
                pe.wait_ge(s_iv, s)
            terms = [(cs, ft) for cs in range(2) for ft in range(2)]
            for i in range(4):
                for n, (cs, ft) in enumerate(terms):
                    par, h = i // 2, i % 2
                    y, w = y4[:, par, ft, cs * HQ:(cs + 1) * HQ], dft_i[:, cs, ft, par * 256:(par + 1) * 256]
                    if o:
                        out, lhsT, rhs = bank(h)[:, par * 256:(par + 1) * 256], y[:, h * P:(h + 1) * P], w
                    else:
                        out, lhsT, rhs = bank(i)[:, 0:HQ], w[:, h * P:(h + 1) * P], y
                    mm = nc.tensor.matmul(out, lhsT, rhs, start=(n == 0), stop=(n == 3))
            mm.then_inc(s_imm, 1)

        def inverse_dve(dve, s):
            q, o = HY_STEPS[s]
            dve.wait_ge(s_imm, s + 1)
            cs = slice(q * HQ, (q + 1) * HQ)
            if o == 0:
                nc.vector.tensor_tensor(v_tok[:, :, cs], ps[:, 0:4, 0:HQ], p0_tok[:, :, cs], ALU.mult).then_inc(s_iv, 1)
            else:
                for h in range(2):
                    p1 = p1T[:, 2 * q + h, :].rearrange("p (t a) -> p a t", a=2)
                    last = nc.vector.tensor_tensor(p1, bank(h).rearrange("p (a t) -> p a t", a=2), p1, ALU.mult)
                last.then_inc(s_iv, 1)

        LATE_ROWS = [(mod[:, 16:24, :], 0), (mod[:, 24:32, :], 0), (scale2.unsqueeze(2), 0), (mod[:, 40:48, :], 0)]

        SENTINEL, MARK, FAR = -3.0e38, 3.0e38, 1.0e30

        def turn_rows(pe, u):
            for k in range(KD):
                mm = nc.tensor.transpose(bank(3 + k // 4)[:, (k % 4) * P:(k % 4 + 1) * P],
                                         xg[:, u, k * P:(k + 1) * P], ident)
            mm.then_inc(s_xt, 1)

        def gate_up(pe, u):
            for k in range(KD):
                mm = nc.tensor.matmul(bank(u), xgT[:, u, k, :], gu_w[:, u, k, :], start=(k == 0), stop=(k == KD - 1))
            mm.then_inc(s_gu, 1)

        def turn_hidden(pe, u):
            for f in range(2):
                mm = nc.tensor.transpose(bank(2)[:, (2 * u + f) * P:(2 * u + f + 1) * P],
                                         hh[:, u, f * P:(f + 1) * P], ident)
            mm.then_inc(s_th, 1)

        def down(pe, u, half):
            for f in range(2):
                mm = nc.tensor.matmul(bank(5 + half), hhT[:, u, f, :], down_w[:, u, f, half * 512:(half + 1) * 512],
                                      start=(f == 0), stop=(f == 1))
            mm.then_inc(s_ym, 1)

        def rowsT_low(u):
            return nc.scalar.copy(xgT[:, u, 0:4, :], bank(3).rearrange("p (k n) -> p k n", k=4))

        def rowsT_high(u):
            return nc.vector.tensor_copy(xgT[:, u, 4:8, :], bank(4).rearrange("p (k n) -> p k n", k=4))
        block = ctx.enter_context(nc.Block())

        @block.sync
        def _(sp):
            for dst, src in ((ident, d["ident"]), (tri_le, d["tri_le"]), (tri_gt, d["tri_gt"]),
                             (tri_ge, d["tri_ge"]), (tri_lt, d["tri_lt"]), (cols[:, 0:N_COLS], d["cols"])):
                sp.dma_start(dst, src).then_inc(s_const, 16)
            for i in range(2):
                item = i
                sp.dma_start(ring[:, item % RING], d["ada"][item]).then_inc(s_ring[item % RING], 16)
            for t in range(TA):
                src = d["x"][t * P:(t + 1) * P, :] if t < LT_ else d["ctx"][(t - LT_) * P:(t - LT_ + 1) * P, :]
                sp.dma_start(xin[:, t], src).then_inc(s_x, 16)
            for item in range(2, N_RING):
                name, chunk = RING_ITEMS[item]
                if item >= RING:
                    sp.wait_ge(*freed[item - RING])
                sp.dma_start(ring[:, item % RING], d[name][chunk]).then_inc(s_ring[item % RING], 16)
                if item == AT_XBC + 1:
                    sp.wait_ge(s_pe, 4)
                    sp.dma_start(w_dt, d["w_dt"]).then_inc(s_w_dt, 16)
                    sp.dma_start(rows_ssd, d["rows_ssd"].partition_broadcast(P)).then_inc(s_w_dt, 16)
                if item == AT_Z + 3:
                    sp.wait_ge(s_pe, 8)
                    sp.dma_start(zpos, d["zpos"]).then_inc(s_hyin, 16)
                    sp.dma_start(hy_w1, d["hy_w1"]).then_inc(s_hyin, 16)
                    sp.dma_start(hy_w23, d["hy_w23"]).then_inc(s_hyin, 16)
                if item == AT_HY + 5:
                    sp.dma_start(dft_f, d["dft_f"]).then_inc(s_dft, 16)
                    sp.dma_start(dft_i, d["dft_i"]).then_inc(s_dft, 16)
                if item == AT_HYO:
                    sp.wait_ge(s_pe, 12)
                    sp.dma_start(x1, d["x"].rearrange("(t p) c -> p t c", p=P)).then_inc(s_x1l, 16)
                    sp.dma_start(router_w, d["router_w"]).then_inc(s_rw, 16)
                    sp.dma_start(bias_row, d["router_bias"].partition_broadcast(P)).then_inc(s_rw, 16)
                    sp.dma_start(iota_row, d["iota64"]).then_inc(s_rw, 16)
                    sp.dma_start(pair_ids, d["pair_ids"]).then_inc(s_rw, 16)
            sp.wait_ge(s_pe, 16)
            sp.dma_start(h2_dram.rearrange("(t p) c -> p t c", p=P), h2).then_inc(s_h2st, 16)
            sp.dma_start(gu_w[:, 2], d["sh_gu"]).then_inc(s_shl, 16)
            sp.dma_start(down_w[:, 2], d["sh_down"]).then_inc(s_shl, 16)
            sp.wait_ge(s_brow, 2)
            for u in range(2):
                e = nc.sync.value_load(erow[0:1, u:u + 1], min_val=0, max_val=E - 1)
                sp.dma_start(gu_w[:, u], d["w_gu"][bass.ds(e, 1)].rearrange("a p k n -> p (a k) n")).then_inc(s_gul[u], 16)
                sp.dma_start(down_w[:, u], d["w_down"][bass.ds(e, 1)].rearrange("a p k n -> p (a k) n")).then_inc(s_dnl[u], 16)
            steps_n = nc.sync.value_load(nstep[0:1, 0:1], min_val=1, max_val=NPAIR_IT)
            with sp.Fori(1, NPAIR_IT) as i:
                with sp.If(i < steps_n):
                    for u in range(2):
                        e = nc.sync.value_load(erow[0:1, bass.ds(i * 2 + u, 1)], min_val=0, max_val=E - 1)
                        sp.wait_ge(s_gu, i * 2 + u - 1)
                        sp.wait_ge(s_brow, 2)
                        sp.dma_start(gu_w[:, u], d["w_gu"][bass.ds(e, 1)].rearrange("a p k n -> p (a k) n")).then_inc(s_gul[u], 16)
                        sp.wait_ge(s_ym, i * 4 + 2 * u - 2)
                        sp.wait_ge(s_brow, 2)
                        sp.dma_start(down_w[:, u], d["w_down"][bass.ds(e, 1)].rearrange("a p k n -> p (a k) n")).then_inc(s_dnl[u], 16)
            for u in range(2):
                sp.wait_ge(s_sca[u], steps_n * 16)
            sp.dma_start(fin_row, d["final_g"].partition_broadcast(P)).then_inc(s_fl, 16)
            for t in range(LT_):
                if t >= 2:
                    sp.wait_ge(s_cmb, t - 1)
                src = y_dram.rearrange("(t p k) c -> t p k c", p=P, k=PAIR_STRIDE)[t, :, 0:TOPK, :]
                sp.dma_start(y_in[:, t % 2], src).then_inc(s_yl[t % 2], 16)
            for t in range(LT_):
                sp.wait_ge(s_fo, t + 1)
                sp.dma_start(d["out"][t * P:(t + 1) * P, :], x_out[t]).then_inc(s_out, 16)
            sp.wait_ge(s_out, 16 * LT_)

        @block.gpsimd
        def _(pool):
            nc.gpsimd.memset(ones[:, :], 1.0).then_inc(s_const, 16)
            pool.wait_ge(s_const, 16 * 7)
            phase_end(pool, 1)
            for u, (dirn, c) in enumerate(STATE_UPDATES[:7]):
                pool_xdte(pool, u, dirn, c)
            for c in range(LT_):
                pool.wait_ge(s_te, SSM_TURNED)
                for dirn in range(2):
                    if c >= 2:
                        pool.wait_ge(s_y, 4 * (c - 1))
                    nc.gpsimd.tensor_tensor(
                        xdt[:, c % 2, dirn].rearrange("p (h e) -> p h e", e=HD),
                        xs_tok[:, c].rearrange("p (h e) -> p h e", e=HD),
                        over(dt_tok[:, c, 16 * dirn:16 * dirn + 16], HD), ALU.mult).then_inc(s_xdt, 1)
                for q in range(4):
                    n = 4 * c + q
                    if n >= 1:
                        pool.wait_ge(s_seg, 2 * n)
                    for dirn in range(2):
                        nc.gpsimd.tensor_tensor(
                            seg_rhs[:, dirn], each(tri_ge if dirn else tri_le, 4),
                            over(a_tok[:, c, 16 * dirn + 4 * q:16 * dirn + 4 * q + 4], P),
                            ALU.mult).then_inc(s_rhs, 1)
                if c < LT_ - 1:
                    pool_xdte(pool, 7 + c, 0, c)
            pool.wait_ge(s_xe, 10)
            pool.wait_ge(s_rhs, 2 * 16)
            phase_end(pool, 2)
            filter_pool(pool, 0)
            filter_pool(pool, 1)
            for s in range(N_STEPS):
                product_pool(pool, s)
                if s < N_STEPS - 2:
                    filter_pool(pool, s + 2)
            pool.wait_ge(s_yq, N_STEPS)
            phase_end(pool, 3)
            for m in range(8):
                pool.wait_ge(s_mg, 8 + m + 1)
                nc.gpsimd.tensor_tensor(mergedT[:, m, :], mergedT[:, m, :], gates[:, 1, m, :], ALU.add).then_inc(s_mga, 1)
            pool.wait_ge(s_mga, 8)
            phase_end(pool, 4)
            nc.gpsimd.memset(xg, 0.0).then_inc(s_xz, 1)
            nc.gpsimd.memset(pad_tab, PAD_PAIR).then_inc(s_xz, 1)
            pool.wait_ge(s_xz, 2)
            pool.dma_start(slot_dram.rearrange("(p j) a -> p (j a)", p=P), pad_tab).then_inc(s_pad, 16)
            pool.wait_ge(s_pad, 16)
            pool.wait_ge(s_dst, 1)
            for c in range(LT_ * TOPK):
                nc.gpsimd.indirect_dma_start(
                    out=slot_dram, out_offset=bass.IndirectOffsetOnAxis(ap=dest_i[:, c:c + 1], axis=0),
                    in_=pair_ids[:, c:c + 1], in_offset=None).then_inc(s_scat, 16)
            pool.wait_ge(s_scat, 16 * LT_ * TOPK)
            pool.dma_start(slots, slot_dram.rearrange("(p j) a -> p (j a)", p=P)).then_inc(s_slot, 16)
            pool.wait_ge(s_tok, 1)
            pool.wait_ge(s_h2st, 16)

            def gather_rows(u, j):
                return nc.gpsimd.indirect_dma_start(
                    out=xg[:, u], out_offset=None, in_=h2_dram,
                    in_offset=bass.IndirectOffsetOnAxis(ap=idx_g[:, u], axis=0), bounds_check=L - 1,
                    oob_is_err=False)

            for u in range(2):
                nc.gpsimd.tensor_copy(idx_g[:, u], tokens[:, u:u + 1]).then_inc(s_pi, 1)
                pool.wait_ge(s_pi, u + 1)
                gather_rows(u, u).then_inc(s_xg[u], 16)
            pool.wait_ge(s_brow, 2)
            steps_n = nc.gpsimd.value_load(nstep[0:1, 0:1], min_val=1, max_val=NPAIR_IT)
            with pool.Fori(0, NPAIR_IT) as i:
                with pool.If(i < steps_n):
                    for u in range(2):
                        pool.wait_ge(s_xt, i * 2 + u + 1)
                        pool.wait_ge(s_xg[u], i * 16 + 16)
                        pool.wait_ge(s_tok, 1)
                        nc.gpsimd.tensor_copy(idx_g[:, u], tokens[:, bass.ds(i * 2 + 2 + u, 1)]).then_inc(s_pi, 1)
                        pool.wait_ge(s_pi, i * 4 + u + 3)
                        pool.sem_inc(s_pseen, 1)
                        gather_rows(u, None).then_inc(s_xg[u], 16)
                    for u in range(2):
                        pool.wait_ge(s_sca[u], i * 16)
                        pool.wait_ge(s_slot, 16)
                        nc.gpsimd.tensor_copy(idx_s[:, u], slots[:, bass.ds(i * 2 + u, 1)]).then_inc(s_pi, 1)
                        pool.wait_ge(s_pi, i * 4 + u + 5)
                        pool.wait_ge(s_yea, i * 2 + u + 1)
                        pool.wait_ge(s_yeb, i * 2 + u + 1)
                        pool.sem_inc(s_pseen, 1)
                        nc.gpsimd.indirect_dma_start(
                            out=y_dram, out_offset=bass.IndirectOffsetOnAxis(ap=idx_s[:, u], axis=0),
                            in_=yo[:, u], in_offset=None, bounds_check=PAD_PAIR - 1,
                            oob_is_err=False).then_inc(s_sca[u], 16)

        @block.tensor
        def _(pe):
            pe.wait_ge(s_const, 16 * 7)
            for j in range(8):
                mod_chunk(pe, j, AT_ADA1 + j)
            for k in range(KD):
                for part, (t0, n) in enumerate(((0, LT_), (LT_, CT_))):
                    g = 2 * k + part
                    if k == 0:
                        pe.wait_ge(s_xn, t0 + n)
                    if g >= 4:
                        pe.wait_ge(s_hT, g - 3)
                    for t in range(n):
                        mm = nc.tensor.transpose(bank(4 + g % 4)[:, t * P:(t + 1) * P],
                                                 xin[:, t0 + t, k * P:(k + 1) * P], ident)
                    mm.then_inc(s_htr, 1)
            pe.wait_ge(s_htr, 2 * KD)
            phase_end(pe, 1)
            pe.wait_ge(s_hT, 2 * KD)
            conv_pe(pe, 0, len(SSM_TILES), 0)
            pe.wait_ge(s_w_dt, 32)
            for t in range(TA):
                for k in range(KD):
                    mm = nc.tensor.matmul(bank(6)[:, t * 32:(t + 1) * 32], hT[:, k, t * P:(t + 1) * P],
                                          w_dt[:, k, :], start=(k == 0), stop=(k == KD - 1))
            mm.then_inc(s_dtmm, 1)
            for j in range(4):
                ring_wait(pe, AT_Z + j)
                for t in range(LT_):
                    n = LT_ * j + t
                    if n == 0:
                        pe.wait_ge(s_cv, len(SSM_TILES))
                    if n >= 2:
                        pe.wait_ge(s_z, n - 1)
                    for k in range(KD):
                        mm = nc.tensor.matmul(bank(n % 2)[:, 0:W_CHUNK], hT[:, k, t * P:(t + 1) * P],
                                              ring[:, (AT_Z + j) % RING, k, :], start=(k == 0), stop=(k == KD - 1))
                    mm.then_inc(s_zmm, 1)
            pe.wait_ge(s_dt, DT_READY)
            for t in range(TA):
                b = bank(2 + t // 3)[:, 96 * (t % 3):96 * (t % 3) + 96]
                af, ab, a2 = a_tok[:, t, 0:16], a_tok[:, t, 16:32], a_tok[:, t, :]
                for at, tri, rhs in ((0, tri_le, af), (16, tri_ge, ab), (32, tri_gt, af), (48, tri_lt, ab),
                                     (64, ones, a2)):
                    mm = nc.tensor.matmul(b[:, at:at + rhs.shape[1]], tri, rhs, start=True, stop=True)
            mm.then_inc(s_cs, 1)
            pe.wait_ge(s_te, SSM_TURNED)
            for c in range(LT_):
                if c >= 2:
                    pe.wait_ge(s_cbm, 2 * (c - 1))
                for g in range(GROUPS):
                    mm = nc.tensor.matmul(bank(4 + c % 2)[:, g * P:(g + 1) * P], BT[:, g, c * P:(c + 1) * P],
                                          CT[:, g, c * P:(c + 1) * P], start=True, stop=True)
                mm.then_inc(s_cb, 1)
            pe.wait_ge(s_z, 4 * LT_)
            for u in range(7):
                if u == 0:
                    pe.wait_ge(s_cbm, 2 * LT_)
                state_pe(pe, u)
            for c in range(LT_):
                pe.wait_ge(s_ecs, 2)
                for q in range(4):
                    n = 4 * c + q
                    pe.wait_ge(s_rhs, 2 * n + 2)
                    for dirn in range(2):
                        if n >= 2:
                            pe.wait_ge(s_exp, 2 * (n - 2) + dirn + 1)
                        nc.tensor.matmul(bank(2 * (n % 2) + dirn), tri_lt if dirn else tri_gt,
                                         seg_rhs[:, dirn].rearrange("p a b -> p (a b)"),
                                         start=True, stop=True).then_inc(s_seg, 1)
                    if q in (1, 2):
                        off_pe(pe, c, q - 1)
                    if q == 3 and c < LT_ - 1:
                        state_pe(pe, 7 + c)
                    if n >= 1:
                        quad_pe(pe, n - 1)
                if c == LT_ - 1:
                    quad_pe(pe, 4 * c + 3)
            pe.wait_ge(s_yc, LT_)
            for m in range(KD):
                if m == 0:
                    pe.wait_ge(s_vn, 2 * LT_)
                if m >= 4:
                    pe.wait_ge(s_yT, m - 3)
                for t in range(LT_):
                    mm = nc.tensor.transpose(bank(m % 4)[:, t * P:(t + 1) * P], zs[:, t, m * P:(m + 1) * P], ident)
                mm.then_inc(s_ytr, 1)
            pe.wait_ge(s_ytr, KD)
            phase_end(pe, 2)
            mlp_pe(pe, 0)
            conv_pe(pe, N_SSM, N_SSM + 2, N_SSM)
            mlp_pe(pe, 1)
            conv_pe(pe, N_SSM + 2, N_SSM + 4, N_SSM)
            mlp_pe(pe, 2)
            conv_pe(pe, N_SSM + 4, N_ALL, N_SSM)
            pe.wait_ge(s_te, turned_before(N_ALL))
            pe.wait_ge(s_cv, N_ALL)
            pe.wait_ge(s_sin, 3)
            pe.wait_ge(s_dft, 32)
            filter_pe(pe, 0)
            spectrum_pe(pe, 0)
            filter_pe(pe, 1)
            for s in range(N_STEPS):
                signal_pe(pe, s)
                if s >= 1:
                    inverse_pe(pe, s - 1)
                if s < N_STEPS - 1:
                    spectrum_pe(pe, s + 1)
                if s < N_STEPS - 2:
                    filter_pe(pe, s + 2)
            inverse_pe(pe, N_STEPS - 1)
            pe.wait_ge(s_imm, N_STEPS)
            phase_end(pe, 3)
            for n in range(32):
                item, c = AT_GATE + n // 2, n % 2
                src = hT[:, :, 0:L] if n < 16 else p1T if n < 24 else yT
                ring_wait(pe, item)
                if 4 <= n < 20:
                    pe.wait_ge(s_gt, n - 3)
                elif n >= 20:
                    pe.wait_ge(s_mg, n - 19)
                for k in range(KD):
                    mm = nc.tensor.matmul(bank(n % 4), ring[:, item % RING, k, c * P:(c + 1) * P], src[:, k, :],
                                          start=(k == 0), stop=(k == KD - 1))
                mm.then_inc(s_mp, 1)
            pe.wait_ge(s_mg, 16)
            for n in range(8, 24):
                mod_chunk(pe, n, AT_ADA2 + n - 8)
            pe.wait_ge(s_mod2, 1)
            for i, (v, w) in enumerate(LATE_ROWS):
                for half in range(2):
                    if 2 * i + half >= 4:
                        pe.wait_ge(s_row, 2 * i + half - 3)
                    for k in range(4):
                        kk = 4 * half + k
                        mm = nc.tensor.matmul(bank(4 + (2 * i + half) % 4)[:, k * P:(k + 1) * P],
                                              v[:, kk, w:w + 1].to_broadcast([P, P]), ident, start=True, stop=True)
                    mm.then_inc(s_rowmm, 1)
            pe.wait_ge(s_mga, 8)
            for j in range(4):
                ring_wait(pe, AT_WO + j)
                for t in range(LT_):
                    n = 4 * j + t
                    if n >= 4:
                        pe.wait_ge(s_x1, n - 3)
                    for k in range(KD):
                        mm = nc.tensor.matmul(bank(n % 4)[:, 0:W_CHUNK], mergedT[:, k, t * P:(t + 1) * P],
                                              ring[:, (AT_WO + j) % RING, k, :], start=(k == 0), stop=(k == KD - 1))
                    mm.then_inc(s_xmm, 1)
            pe.wait_ge(s_xmm, 16)
            phase_end(pe, 4)
            for m in range(KD):
                if m >= 4:
                    pe.wait_ge(s_h2T, m - 3)
                for t in range(LT_):
                    mm = nc.tensor.transpose(bank(m % 4)[:, t * P:(t + 1) * P], h2[:, t, m * P:(m + 1) * P], ident)
                mm.then_inc(s_h2t, 1)
            pe.wait_ge(s_rw, 64)
            pe.wait_ge(s_h2T, KD)
            for t in range(LT_):
                for k in range(KD):
                    mm = nc.tensor.matmul(bank(4)[:, t * E:(t + 1) * E], h2T[:, k, t * P:(t + 1) * P],
                                          router_w[:, k, :], start=(k == 0), stop=(k == KD - 1))
            mm.then_inc(s_lg, 1)
            pe.wait_ge(s_shl, 32)
            for f in range(4):
                for k in range(KD):
                    mm = nc.tensor.matmul(bank(f), gu_w[:, 2, k, f * P:(f + 1) * P], h2T[:, k, :],
                                          start=(k == 0), stop=(k == KD - 1))
                mm.then_inc(s_shm, 1)
            pe.wait_ge(s_msk2, LT_)
            for t in range(LT_):
                for b in range(t + 1):
                    mm = nc.tensor.matmul(bank(5)[:, t * E:(t + 1) * E], tri_lt if b == t else ones, mask[:, b, :],
                                          start=(b == 0), stop=(b == t))
            for b in range(LT_):
                mm = nc.tensor.matmul(bank(5)[:, LT_ * E:(LT_ + 1) * E], ones, mask[:, b, :], start=(b == 0),
                                      stop=(b == LT_ - 1))
            mm.then_inc(s_rk, 1)
            pe.wait_ge(s_shh, 2)
            for t in range(LT_):
                for half in range(2):
                    n = 2 * t + half
                    if n == 2:
                        pe.wait_ge(s_be, 1)
                        nc.tensor.transpose(bank(4)[0:1, 0:P], ecol[:, 0:1], ident).then_inc(s_bt, 1)
                    if n >= 2:
                        pe.wait_ge(s_shx, n - 1)
                    for f in range(2):
                        mm = nc.tensor.matmul(bank(6 + half), shg[:, f, t * P:(t + 1) * P],
                                              down_w[:, 2, f, half * 512:(half + 1) * 512], start=(f == 0), stop=(f == 1))
                    mm.then_inc(s_shy, 1)
            pe.wait_ge(s_shx, 8)
            pe.wait_ge(s_brow, 2)
            for u in range(2):
                pe.wait_ge(s_xg[u], 16)
                if u:
                    pe.wait_ge(s_xea, 1)
                    pe.wait_ge(s_xeb, 1)
                turn_rows(pe, u)
            steps_n = nc.tensor.value_load(nstep[0:1, 0:1], min_val=1, max_val=NPAIR_IT)
            with pe.Fori(0, NPAIR_IT) as i:
                with pe.If(i < steps_n):
                    for u in range(2):
                        pe.wait_ge(s_gul[u], i * 16 + 16)
                        pe.wait_ge(s_xea, i * 2 + u + 1)
                        pe.wait_ge(s_xeb, i * 2 + u + 1)
                        gate_up(pe, u)
                    for u in range(2):
                        pe.wait_ge(s_h, i * 2 + u + 1)
                        turn_hidden(pe, u)
                        pe.wait_ge(s_xg[u], i * 16 + 32)
                        pe.wait_ge(s_xea, i * 2 + u + 2)
                        pe.wait_ge(s_xeb, i * 2 + u + 2)
                        turn_rows(pe, u)
                        pe.wait_ge(s_hte, i * 2 + u + 1)
                        pe.wait_ge(s_dnl[u], i * 16 + 16)
                        pe.wait_ge(s_yea, i * 2 + u)
                        down(pe, u, 0)
                        pe.wait_ge(s_yeb, i * 2 + u)
                        down(pe, u, 1)

        @block.scalar
        def _(act):
            act.wait_ge(s_const, 16 * 7)
            for i, name in enumerate(("c", "c_ctx")):
                nc.scalar.activation(silu_c[:, :, i], col(cols, name, 0, KD), ACT.Silu).then_inc(s_silu_c, 1)
            for t in range(TA):
                act.wait_ge(s_x, 16 * TA)
                if t >= 1:
                    act.wait_ge(s_ss, t)
                nc.scalar.activation(junk, xin[:, t], ACT.Square,
                                     accum_out=small[:, 16 + t:17 + t]).then_inc(s_ss, 1)
            act.wait_ge(s_rs, 1)
            nc.scalar.activation(small[:, 32:32 + TA], small[:, 24:24 + TA], ACT.Sqrt).then_inc(s_rs, 1)
            mod_rows_act(act, 0, 8)
            act.wait_ge(s_mod, 4)
            for k in range(KD):
                for part, (t0, n) in enumerate(((0, L), (L, LC))):
                    g = 2 * k + part
                    act.wait_ge(s_htr, g + 1)
                    nc.scalar.activation(hT[:, k, t0:t0 + n], bank(4 + g % 4)[:, 0:n], ACT.Identity,
                                         scale=scale1[:, k, part:part + 1],
                                         bias=mod[:, k, part:part + 1]).then_inc(s_hT, 1)
            act.wait_ge(s_hT, 2 * KD)
            phase_end(act, 1)
            conv_act(act, 0, len(SSM_TILES), 0)
            act.wait_ge(s_w_dt, 32)
            act.wait_ge(s_dt, 2)
            nc.scalar.activation(dtw[:, 2], dtw[:, 1], ACT.Exp, scale=-1.0).then_inc(s_dta, 1)
            nc.scalar.activation(rows_ssd[:, 32:64], rows_ssd[:, 32:64], ACT.Exp).then_inc(s_dta, 1)
            act.wait_ge(s_dt, 3)
            nc.scalar.activation(dtw[:, 4], dtw[:, 3], ACT.Ln).then_inc(s_dta, 1)
            for j in range(4):
                for t in range(LT_):
                    n = LT_ * j + t
                    act.wait_ge(s_zmm, n + 1)
                    nc.scalar.activation(zs[:, t, j * W_CHUNK:(j + 1) * W_CHUNK], bank(n % 2)[:, 0:W_CHUNK],
                                         ACT.Silu).then_inc(s_z, 1)
            act.wait_ge(s_cs, 1)
            for i in range(2):
                nc.scalar.activation(ecs[:, 3 * i:3 * i + 3, :],
                                     bank(2 + i)[:, 0:288].rearrange("p (a b) -> p a b", a=3),
                                     ACT.Exp).then_inc(s_ecs, 1)
            for n in range(4 * LT_):
                for dirn in range(2):
                    act.wait_ge(s_seg, 2 * n + dirn + 1)
                    if n >= 2:
                        act.wait_ge(s_y, n - 1)
                    nc.scalar.activation(decay[:, n % 2, dirn].rearrange("p a b -> p (a b)"),
                                         bank(2 * (n % 2) + dirn), ACT.Exp).then_inc(s_exp, 1)
                if n % 4 == 1 and n >= 5:
                    gate_squares(act, n // 4 - 1)
            gate_squares(act, LT_ - 1)
            act.wait_ge(s_vr, 1)
            nc.scalar.activation(v_rstd, v_rstd, ACT.Sqrt).then_inc(s_vr, 1)
            for m in range(KD):
                act.wait_ge(s_ytr, m + 1)
                nc.scalar.activation(yT[:, m, :], bank(m % 4), ACT.Identity,
                                     scale=col(cols, "ssm_norm_g", m)).then_inc(s_yT, 1)
            act.wait_ge(s_yT, KD)
            phase_end(act, 2)
            mlp_act(act, 0)
            conv_act(act, N_SSM, N_SSM + 2, N_SSM)
            mlp_act(act, 1)
            conv_act(act, N_SSM + 2, N_SSM + 4, N_SSM)
            mlp_act(act, 2)
            conv_act(act, N_SSM + 4, N_ALL, N_SSM)
            act.wait_ge(s_cv, N_ALL)
            rows_dma(act, 0)
            filter_act(act, 0)
            odd_act(act, 0, s_kmm, s_ub, 0, s_kod)
            filter_act(act, 1)
            for s in range(N_STEPS):
                odd_act(act, s, s_umm, s_kb, s + 1, s_uod)
                if s < N_STEPS - 1:
                    odd_act(act, s + 1, s_kmm, s_ub, s + 1, s_kod)
                if s < N_STEPS - 2:
                    filter_act(act, s + 2)
            act.wait_ge(s_uod, 2 * N_STEPS)
            phase_end(act, 3)
            for n in range(16):
                act.wait_ge(s_mp, n + 1)
                nc.scalar.activation(gates[:, n // 8, n % 8, :], bank(n % 4), ACT.Sigmoid).then_inc(s_gt, 1)
            mod_rows_act(act, 8, 24)
            for n in range(8):
                act.wait_ge(s_rowmm, n + 1)
                nc.scalar.copy(rows[:, n // 2, (n % 2) * 512:(n % 2 + 1) * 512], bank(4 + n % 4)).then_inc(s_row, 1)
            act.wait_ge(s_row, 8)
            for t in range(LT_):
                act.wait_ge(s_x1, 16)
                if t >= 1:
                    act.wait_ge(s_ss2, t)
                nc.scalar.activation(squares2, x1[:, t], ACT.Square, accum_out=small[:, 16 + t:17 + t]).then_inc(s_ss2, 1)
            act.wait_ge(s_rs2, 1)
            nc.scalar.activation(small[:, 32:32 + LT_], small[:, 24:24 + LT_], ACT.Sqrt).then_inc(s_rs2, 1)
            act.wait_ge(s_rs2, 2)
            phase_end(act, 4)
            for m in range(KD):
                act.wait_ge(s_h2t, m + 1)
                nc.scalar.copy(h2T[:, m, :], bank(m % 4)).then_inc(s_h2T, 1)
            act.wait_ge(s_lg, 1)
            for t in range(LT_):
                nc.scalar.activation(scores[:, t], bank(4)[:, t * E:(t + 1) * E], ACT.Sigmoid).then_inc(s_sc0, 1)
            for f in range(2):
                act.wait_ge(s_shm, f + 1)
                nc.scalar.activation(shg[:, f, :], bank(f), ACT.Silu).then_inc(s_sha, 1)
            act.wait_ge(s_xt, 1)
            rowsT_low(0).then_inc(s_xea, 1)
            act.wait_ge(s_xt, 2)
            rowsT_low(1).then_inc(s_xea, 1)
            steps_n = nc.scalar.value_load(nstep[0:1, 0:1], min_val=1, max_val=NPAIR_IT)
            with act.Fori(0, NPAIR_IT) as i:
                with act.If(i < steps_n):
                    for u in range(2):
                        act.wait_ge(s_gu, i * 2 + u + 1)
                        nc.scalar.activation(sg[:, u, :], bank(u)[:, 0:DE], ACT.Silu).then_inc(s_sg, 1)
                    for u in range(2):
                        act.wait_ge(s_xt, i * 2 + u + 3)
                        rowsT_low(u).then_inc(s_xea, 1)
                        act.wait_ge(s_ym, i * 4 + 2 * u + 1)
                        act.wait_ge(s_sca[u], i * 16)
                        nc.scalar.copy(yo[:, u, 0:512], bank(5)).then_inc(s_yea, 1)
            for t in range(LT_):
                act.wait_ge(s_cmb, t + 1)
                if t >= 1:
                    act.wait_ge(s_ss3, t)
                nc.scalar.activation(squares2, x1[:, t], ACT.Square, accum_out=small[:, 16 + t:17 + t]).then_inc(s_ss3, 1)
                act.wait_ge(s_rs3, 2 * t + 1)
                nc.scalar.activation(small[:, 32 + t:33 + t], small[:, 24 + t:25 + t], ACT.Sqrt).then_inc(s_rs3, 1)

        @block.vector
        def _(dve):
            steps = [0]

            def link(ins):
                steps[0] += 1
                ins.then_inc(s_dve, 1)
                dve.wait_ge(s_dve, steps[0])

            V = nc.vector
            dve.wait_ge(s_const, 16 * 7)
            dve.wait_ge(s_ss, TA)
            V.tensor_scalar(small[:, 24:24 + TA], small[:, 16:16 + TA], 1.0 / D, EPS, ALU.mult,
                            ALU.add).then_inc(s_rs, 1)
            dve.wait_ge(s_rs, 2)
            link(V.reciprocal(small[:, 40:40 + TA], small[:, 32:32 + TA]))
            for t in range(TA):
                V.tensor_scalar(xin[:, t], xin[:, t], small[:, 40 + t:41 + t], None, ALU.mult).then_inc(s_xn, 1)
            dve.wait_ge(s_modtr, 8)
            link(V.tensor_tensor(mod[:, 0:16, :], bank(2)[:, 0:32].rearrange("p (a b) -> p a b", b=2),
                                 over(col(cols, "ada_b", 0, 16), 2), ALU.add))
            link(V.tensor_scalar(scale1[:, :, :], mod[:, 8:16, :], 1.0, None, ALU.add))
            V.tensor_tensor(scale1[:, :, :], scale1[:, :, :], over(col(cols, "norm1_g", 0, 8), 2),
                            ALU.mult).then_inc(s_mod, 4)
            dve.wait_ge(s_mod, 4)
            dve.wait_ge(s_xn, TA)
            phase_end(dve, 1)
            conv_dve(dve, 0, len(SSM_TILES))
            dve.wait_ge(s_dtmm, 1)
            dve.wait_ge(s_w_dt, 32)
            V.tensor_tensor(dtw[:, 0], bank(6)[:, 0:192].rearrange("p (t n) -> p t n", t=TA),
                            each(rows_ssd[:, 0:32], TA), ALU.add).then_inc(s_dt, 1)
            dve.wait_ge(s_dt, 1)
            V.scalar_tensor_tensor(dtw[:, 1], dtw[:, 0], -1.0, dtw[:, 0], ALU.mult, ALU.max).then_inc(s_dt, 1)
            dve.wait_ge(s_dta, 2)
            V.tensor_scalar(dtw[:, 3], dtw[:, 2], 1.0, None, ALU.add).then_inc(s_dt, 1)
            dve.wait_ge(s_dt, 3)
            link(V.reciprocal(dtw[:, 1], dtw[:, 3]))
            link(V.scalar_tensor_tensor(dt_tok[:, :, :], dtw[:, 3], -1.0, dtw[:, 2], ALU.add, ALU.subtract))
            link(V.tensor_tensor(dt_tok[:, :, :], dt_tok[:, :, :], dtw[:, 1], ALU.mult))
            dve.wait_ge(s_dta, 3)
            link(V.tensor_tensor(dt_tok[:, :, :], dtw[:, 4], dt_tok[:, :, :], ALU.subtract))
            link(V.scalar_tensor_tensor(dt_tok[:, :, :], dtw[:, 0], 0.0, dt_tok[:, :, :], ALU.max, ALU.add))
            V.scalar_tensor_tensor(a_tok[:, :, :], dt_tok[:, :, :], -1.0, each(rows_ssd[:, 32:64], TA),
                                   ALU.mult, ALU.mult).then_inc(s_dt, 1)
            dve.wait_ge(s_ecs, 2)
            V.tensor_tensor(dte[:, :, :], dt_tok[:, :, :], ecs[:, :, 32:64], ALU.mult).then_inc(s_dte, 1)
            for c in range(LT_):
                dve.wait_ge(s_cb, c + 1)
                for dirn in range(2):
                    V.tensor_tensor(cbm[:, dirn, c], bank(4 + c % 2)[:, 0:GROUPS * P].rearrange(
                        "p (g l) -> p g l", g=GROUPS), each(tri_ge if dirn else tri_le, GROUPS),
                        ALU.mult).then_inc(s_cbm, 1)
            dve.wait_ge(s_cbm, 2 * LT_)
            for u in range(7):
                state_dve(dve, link, u)
            for c in range(LT_):
                for q in range(4):
                    n = 4 * c + q
                    for dirn in range(2):
                        dve.wait_ge(s_exp, 2 * n + dirn + 1)
                        V.tensor_tensor(decay[:, n % 2, dirn], decay[:, n % 2, dirn],
                                        each(cbm[:, dirn, c, q // 2], 4), ALU.mult).then_inc(s_msk, 1)
                    if q in (1, 2):
                        dve.wait_ge(s_off, 2 * c + q)
                        dst = y1 if q == 1 else y2
                        V.tensor_tensor(dst.rearrange("p (h e) -> p h e", e=HD),
                                        ps[:, 4:6, :].rearrange("p b (h e) -> p (b h) e", e=HD),
                                        over(ecs[:, c, 16 * (q - 1):16 * q], HD), ALU.mult).then_inc(s_offr, 1)
                dve.wait_ge(s_offr, 2 * c + 2)
                link(V.tensor_tensor(y1, y1, y2, ALU.add))
                if c < LT_ - 1:
                    state_dve(dve, link, 7 + c)
                link(V.tensor_tensor(y2.rearrange("p (h e) -> p h e", e=HD),
                                     xs_tok[:, c].rearrange("p (h e) -> p h e", e=HD),
                                     over(rows_ssd[:, 64:80], HD), ALU.mult))
                link(V.tensor_tensor(y1, y1, y2, ALU.add))
                dve.wait_ge(s_y, 4 * c + 4)
                link(V.tensor_tensor(y1, ps[:, 6:8, :].rearrange("p b e -> p (b e)"), y1, ALU.add))
                V.tensor_tensor(zs[:, c], y1, zs[:, c], ALU.mult).then_inc(s_yc, 1)
                dve.wait_ge(s_yc, c + 1)
            dve.wait_ge(s_vss, 2 * LT_)
            V.tensor_scalar(v_rstd, v_ss, 1.0 / 512, EPS, ALU.mult, ALU.add).then_inc(s_vr, 1)
            dve.wait_ge(s_vr, 2)
            link(V.reciprocal(v_rstd, v_rstd))
            for c in range(LT_):
                for g in range(GROUPS):
                    V.tensor_scalar(zs[:, c, g * 512:(g + 1) * 512], zs[:, c, g * 512:(g + 1) * 512],
                                    v_rstd[:, 2 * c + g:2 * c + g + 1], None, ALU.mult).then_inc(s_vn, 1)
            dve.wait_ge(s_vn, 2 * LT_)
            phase_end(dve, 2)
            V.tensor_tensor(small[0:64, 48:51], col(cols, "mlp", 0, 3)[0:64], col(cols, "mlp", 3, 3)[0:64],
                            ALU.mult).then_inc(s_fb, 1)
            mlp_dve(dve, link, 0)
            conv_dve(dve, N_SSM, N_SSM + 2)
            mlp_dve(dve, link, 1)
            conv_dve(dve, N_SSM + 2, N_SSM + 4)
            mlp_dve(dve, link, 2)
            conv_dve(dve, N_SSM + 4, N_ALL)
            filter_dve(dve, link, 0)
            mirror_dve(dve, 0, s_kod, spec, s_kb)
            filter_dve(dve, link, 1)
            for s in range(N_STEPS):
                mirror_dve(dve, s, s_uod, u4, s_ub)
                product_dve(dve, s)
                if s >= 1:
                    inverse_dve(dve, s - 1)
                fold_dve(dve, s)
                if s < N_STEPS - 1:
                    mirror_dve(dve, s + 1, s_kod, spec, s_kb)
                if s < N_STEPS - 2:
                    filter_dve(dve, link, s + 2)
            inverse_dve(dve, N_STEPS - 1)
            dve.wait_ge(s_iv, N_STEPS)
            phase_end(dve, 3)
            for n in range(16):
                dve.wait_ge(s_mp, 16 + n + 1)
                dst = mergedT[:, n, :] if n < 8 else gates[:, 1, n - 8, :]
                if n == 0:
                    dve.wait_ge(s_gt, 16)
                V.tensor_tensor(dst, bank(n % 4), gates[:, n // 8, n % 8, :], ALU.mult).then_inc(s_mg, 1)
            dve.wait_ge(s_modtr, 24)
            link(V.tensor_tensor(mod[:, 16:48, :], bank(2)[:, 32:96].rearrange("p (a b) -> p a b", b=2),
                                 over(col(cols, "ada_b", 16, 32), 2), ALU.add))
            V.scalar_tensor_tensor(scale2.unsqueeze(2), mod[:, 32:40, 0:1], 1.0,
                                   col(cols, "norm2_g", 0, 8).unsqueeze(2), ALU.add, ALU.mult).then_inc(s_mod2, 1)
            dve.wait_ge(s_row, 8)
            dve.wait_ge(s_x1l, 16)
            for j in range(4):
                for t in range(LT_):
                    n = 4 * j + t
                    cs = slice(j * W_CHUNK, (j + 1) * W_CHUNK)
                    dve.wait_ge(s_xmm, n + 1)
                    link(V.tensor_tensor(xmix[:, n % 2, :], bank(n % 4)[:, 0:W_CHUNK], rows[:, 0, cs], ALU.mult))
                    V.tensor_tensor(x1[:, t, cs], x1[:, t, cs], xmix[:, n % 2, :], ALU.add).then_inc(s_x1, 1)
            dve.wait_ge(s_ss2, LT_)
            V.tensor_scalar(small[:, 24:24 + LT_], small[:, 16:16 + LT_], 1.0 / D, EPS, ALU.mult,
                            ALU.add).then_inc(s_rs2, 1)
            dve.wait_ge(s_rs2, 2)
            link(V.reciprocal(small[:, 40:40 + LT_], small[:, 32:32 + LT_]))
            for t in range(LT_):
                link(V.scalar_tensor_tensor(h2[:, t], x1[:, t], small[:, 40 + t:41 + t], rows[:, 2],
                                            ALU.mult, ALU.mult))
                V.tensor_tensor(h2[:, t], h2[:, t], rows[:, 1], ALU.add).then_inc(s_h2, 1)
            dve.wait_ge(s_h2, LT_)
            phase_end(dve, 4)
            V.memset(grp[:, 8:16], SENTINEL)
            V.memset(grp_rep, SENTINEL)
            V.memset(top_rep, SENTINEL)
            link(V.memset(sel[:, :, E:E + 8], SENTINEL))
            for t in range(LT_):
                dve.wait_ge(s_sc0, t + 1)
                link(V.tensor_tensor(sel[:, t, 0:E], scores[:, t], bias_row, ALU.add))
                for g in range(EG):
                    last = V.max(grp8[:, g, :], sel[:, t, g * 8:(g + 1) * 8])
                link(last)
                link(V.tensor_tensor(grp[:, 0:EG].unsqueeze(2), grp8[:, :, 0:1], grp8[:, :, 1:2], ALU.add))
                link(V.max(grp_top, grp[:, 0:EG]))
                link(V.tensor_copy(grp_rep[:, 0:TOPG], grp_top[:, 0:TOPG]))
                link(V.match_replace(grp_mark[:, 0:12], grp_rep, grp[:, 0:12], MARK))
                link(V.tensor_scalar(keep, grp_mark[:, 0:EG], MARK, None, ALU.is_equal))
                link(V.tensor_scalar(drop, keep, FAR, -FAR, ALU.mult, ALU.add))
                s3 = sel[:, t, 0:E].rearrange("p (g e) -> p g e", g=EG)
                link(V.tensor_tensor(s3, s3, over(keep, 8), ALU.mult))
                link(V.tensor_tensor(s3, s3, over(drop, 8), ALU.add))
                link(V.max(top8[:, t, :], sel[:, t, 0:E]))
                V.tensor_copy(top_rep[:, 0:TOPK], top8[:, t, 0:TOPK])
                link(V.max_index(idx_u[:, t, :], top8[:, t, :], sel[:, t, 0:E]))
                link(V.match_replace(marked, top_rep, sel[:, t, :], MARK))
                V.tensor_scalar(mask[:, t, :], marked[:, 0:E], MARK, None, ALU.is_equal).then_inc(s_msk2, 1)
            link(V.tensor_copy(idx_f, idx_u))
            for f in range(2):
                dve.wait_ge(s_sha, f + 1)
                dve.wait_ge(s_shm, f + 3)
                V.tensor_tensor(shg[:, f, :], bank(2 + f), shg[:, f, :], ALU.mult).then_inc(s_shh, 1)
            dve.wait_ge(s_rk, 1)
            V.tensor_copy(rank, bank(5)[:, 0:LT_ * E].rearrange("p (t e) -> p t e", e=E))
            link(V.tensor_copy(counts, bank(5)[:, LT_ * E:(LT_ + 1) * E]))
            link(V.tensor_scalar(nblk, counts, 0.0, None, ALU.is_gt))
            for b in range(1, LT_):
                link(V.scalar_tensor_tensor(nblk, counts, float(b * P), nblk, ALU.is_gt, ALU.add))
            link(V.tensor_tensor_scan(cend, ones[:, 0:E], nblk, 0.0, ALU.mult, ALU.add))
            link(V.tensor_scalar(picked, cend, col(cols, "jcol"), None, ALU.is_le))
            link(V.tensor_reduce(ecol[:, 0:1], picked, AX.X, ALU.add))
            V.tensor_scalar(ecol[:, 0:1], ecol[:, 0:1], float(E - 1), None, ALU.min).then_inc(s_be, 1)
            link(V.tensor_scalar(nstep_f[:, 0:1], cend[0:1, E - 1:E], 0.5, 0.25, ALU.mult, ALU.add))
            link(V.tensor_scalar(nstep_f[:, 0:1], nstep_f[:, 0:1], ROUND_MAGIC, None, ALU.add))
            link(V.tensor_scalar(nstep_f[:, 0:1], nstep_f[:, 0:1], ROUND_MAGIC, None, ALU.subtract))
            V.tensor_copy(nstep[:, 0:1], nstep_f[:, 0:1]).then_inc(s_brow, 1)
            link(V.tensor_tensor(base, cend, nblk, ALU.subtract))
            link(V.tensor_scalar(over_b, rank, float(P), None, ALU.is_ge))
            for b in range(2, LT_):
                link(V.scalar_tensor_tensor(over_b, rank, float(b * P), over_b, ALU.is_ge, ALU.add))
            link(V.scalar_tensor_tensor(dest, over_b, float(-P), rank, ALU.mult, ALU.add))
            link(V.scalar_tensor_tensor(dest, dest, float(NBLK), over_b, ALU.mult, ALU.add))
            link(V.tensor_tensor(dest, dest, each(base, LT_), ALU.add))
            for t in range(LT_):
                link(V.tensor_tensor(onehot, each(iota_row, TOPK), over(idx_f[:, t, 0:TOPK], E), ALU.is_equal))
                V.tensor_tensor(chosen[:, 0], onehot, each(dest[:, t], TOPK), ALU.mult)
                link(V.tensor_tensor(chosen[:, 1], onehot, each(scores[:, t], TOPK), ALU.mult))
                V.tensor_reduce(dest_k[:, t], chosen[:, 0], AX.X, ALU.add)
                link(V.tensor_reduce(w_tok[:, t], chosen[:, 1], AX.X, ALU.add))
            V.tensor_copy(dest_i, dest_k.rearrange("p t k -> p (t k)")).then_inc(s_dst, 1)
            link(V.tensor_reduce(w_sum, w_tok, AX.X, ALU.add))
            link(V.reciprocal(w_sum, w_sum))
            link(V.scalar_tensor_tensor(w_tok, w_tok, SCALE_R, over(w_sum, TOPK), ALU.mult, ALU.mult))
            dve.wait_ge(s_bt, 1)
            V.tensor_copy(erow, bank(4)[0:1, 0:P]).then_inc(s_brow, 1)
            for t in range(LT_):
                for half in range(2):
                    n = 2 * t + half
                    cs = slice(half * 512, (half + 1) * 512)
                    dve.wait_ge(s_shy, n + 1)
                    link(V.tensor_tensor(acc2[:, 0, cs], bank(6 + half), rows[:, 3, cs], ALU.mult))
                    V.tensor_tensor(x1[:, t, cs], x1[:, t, cs], acc2[:, 0, cs], ALU.add).then_inc(s_shx, 1)
            dve.wait_ge(s_slot, 16)
            V.tensor_scalar(tokens, slots, 3, None, ALU.logical_shift_right).then_inc(s_tok, 1)
            for u in range(2):
                dve.wait_ge(s_xt, u + 1)
                rowsT_high(u).then_inc(s_xeb, 1)
            dve.wait_ge(s_brow, 2)
            steps_n = nc.vector.value_load(nstep[0:1, 0:1], min_val=1, max_val=NPAIR_IT)
            with dve.Fori(0, NPAIR_IT) as i:
                with dve.If(i < steps_n):
                    for u in range(2):
                        dve.wait_ge(s_sg, i * 2 + u + 1)
                        V.tensor_tensor(hh[:, u, :], bank(u)[:, DE:2 * DE], sg[:, u, :], ALU.mult).then_inc(s_h, 1)
                    for u in range(2):
                        dve.wait_ge(s_th, i * 2 + u + 1)
                        V.tensor_copy(hhT[:, u], bank(2)[:, 2 * u * P:(2 * u + 2) * P].rearrange(
                            "p (f n) -> p f n", f=2)).then_inc(s_hte, 1)
                        dve.wait_ge(s_xt, i * 2 + u + 3)
                        rowsT_high(u).then_inc(s_xeb, 1)
                        dve.wait_ge(s_ym, i * 4 + 2 * u + 2)
                        dve.wait_ge(s_sca[u], i * 16)
                        V.tensor_copy(yo[:, u, 512:1024], bank(6)).then_inc(s_yeb, 1)
            dve.wait_ge(s_fl, 16)
            for t in range(LT_):
                a, b = acc2[:, 0], acc2[:, 1]
                dve.wait_ge(s_yl[t % 2], 16 * (t // 2 + 1))
                link(V.tensor_scalar(a, y_in[:, t % 2, 0, :], w_tok[:, t, 0:1], None, ALU.mult))
                for k in range(1, TOPK):
                    link(V.scalar_tensor_tensor(a, y_in[:, t % 2, k, :], w_tok[:, t, k:k + 1], a, ALU.mult, ALU.add))
                link(V.tensor_tensor(b, a, rows[:, 3], ALU.mult))
                V.tensor_tensor(x1[:, t], x1[:, t], b, ALU.add).then_inc(s_cmb, 1)
                dve.wait_ge(s_ss3, t + 1)
                V.tensor_scalar(small[:, 24 + t:25 + t], small[:, 16 + t:17 + t], 1.0 / D, EPS, ALU.mult,
                                ALU.add).then_inc(s_rs3, 1)
                dve.wait_ge(s_rs3, 2 * t + 2)
                link(V.reciprocal(small[:, 40 + t:41 + t], small[:, 32 + t:33 + t]))
                V.scalar_tensor_tensor(x_out[t], x1[:, t], small[:, 40 + t:41 + t], fin_row, ALU.mult,
                                       ALU.mult).then_inc(s_fo, 1)


def kernel(**inputs):
    import numpy as np
    import concourse.bacc as bacc
    from concourse.bass_utils import run_bass_kernel_spmd

    arrays = host_arrays(inputs, np)
    nc = bacc.Bacc("TRN2", target_bir_lowering=False, num_devices=1)
    d = {n: nc.dram_tensor("in_" + n, a.shape, mybir.dt.from_np(a.dtype), kind="ExternalInput").ap()
         for n, a in arrays.items()}
    d["out"] = nc.dram_tensor("out_x", (L, D), F32, kind="ExternalOutput").ap()
    build(nc, d)
    r = run_bass_kernel_spmd(nc, [{"in_" + n: a for n, a in arrays.items()}], core_ids=[0])
    return r.results[0]["out_x"].reshape(1, L, D)


def host_arrays(inputs, np):
    x = {k: np.asarray(v) for k, v in inputs.items()}

    def chunks(w, n):
        k = w.shape[0] // P
        return np.ascontiguousarray(
            w.reshape(k, P, w.shape[1] // n, n).transpose(2, 1, 0, 3)).reshape(w.shape[1] // n, P, k, n)

    def columns(v):
        return np.ascontiguousarray(v.reshape(-1, P).T)

    w_in = x["w_in"][0]
    n_x, n_dt = D_XBC, 2 * HEADS
    pos = np.arange(L, dtype=np.float64)
    pos2 = np.concatenate([pos[0::2], pos[1::2]])
    mlp = np.zeros((P, 6), np.float32)
    for i, n in enumerate(("hy_b1", "hy_b2", "hy_b3")):
        mlp[0:64, i] = x[n][0]
    mlp[0:64, 3:6] = x["hy_freq"][0].T
    consts = {"neg_t": columns((-(pos2 / (L - 1))).astype(np.float32)),
              "not_t0": columns((pos2 > 0).astype(np.float32)),
              "mlp": mlp, "jcol": np.arange(P, dtype=np.float32)[:, None]}
    named = {"c": x["c"], "c_ctx": x["c_ctx"], "norm1_g": x["norm1_g"], "norm2_g": x["norm2_g"],
             "ada_b": x["ada_b"], "ssm_norm_g": x["ssm_norm_g"], "ssm_w": x["ssm_conv_w"],
             "ssm_b": x["ssm_conv_b"], "hy_w": x["hy_conv_w"], "hy_b": x["hy_conv_b"]}
    cols = np.concatenate([consts[n] if n in consts else columns(named[n]) for n in COLS], axis=1)
    j, i = np.arange(P)[:, None], np.arange(P)[None, :]
    f32 = lambda a: np.ascontiguousarray(a, dtype=np.float32)
    omega = np.pi * (2 * pos[0:L // 2] + 1) / (2 * L)
    ang = pos2[:, None] * omega[None, :]
    fwd = np.stack([np.cos(ang), np.sin(ang)]).reshape(2, LT_, P, L // 2).transpose(2, 0, 1, 3)
    inv = (np.stack([np.cos(ang).T, np.sin(ang).T]) / L).reshape(2, 2, P, L).transpose(2, 0, 1, 3)
    bands = np.linspace(1e-4, 15, 16)
    pa = (2.0 * np.pi / L) * pos2[:, None] * bands[None, :]
    zpos = np.concatenate([(pos2 / (L - 1))[:, None], np.cos(pa), -np.sin(pa)], axis=-1)
    out = {
        "x": x["x"][0], "ctx": x["ctx"][0], "cols": cols,
        "ident": f32(j == i), "tri_le": f32(j <= i), "tri_gt": f32(j > i), "tri_ge": f32(j >= i),
        "tri_lt": f32(j < i),
        "ada": chunks(x["ada_w"][0], W_CHUNK),
        "w_in": chunks(np.concatenate([w_in[:, 0:n_x], w_in[:, n_x + n_dt:]], axis=1), W_CHUNK),
        "w_dt": chunks(w_in[:, n_x:n_x + n_dt], n_dt)[0],
        "rows_ssd": np.concatenate([x["ssm_dt_bias"].reshape(-1), x["ssm_a_log"].reshape(-1),
                                    x["ssm_d"].reshape(-1)]),
        "w_hy_out": chunks(x["w_hy_out"][0], W_CHUNK), "w_ssm_out": chunks(x["w_ssm_out"][0], W_CHUNK),
        "w_o": chunks(x["w_o"][0], W_CHUNK),
        "dft_f": f32(fwd), "dft_i": f32(inv),
        "zpos": f32(zpos.T), "hy_w1": x["hy_w1"][0],
        "hy_w23": np.ascontiguousarray(np.stack([x["hy_w2"][0], x["hy_w3"][0]], axis=1)),
        "hy_w_out": x["hy_w_out"][0], "hy_decay": x["hy_decay"].reshape(-1), "hy_bias": x["hy_bias"].reshape(-1),
        "router_w": np.ascontiguousarray(x["router_w"][0].reshape(KD, P, E).transpose(1, 0, 2)),
        "router_bias": x["router_bias"][0], "final_g": x["final_g"],
        "w_gu": np.ascontiguousarray(
            np.stack([x["e_w_gate"][0], x["e_w_up"][0]], axis=2).reshape(E, KD, P, 2 * DE).transpose(0, 2, 1, 3)),
        "w_down": np.ascontiguousarray(x["e_w_down"][0].reshape(E, 2, P, D).transpose(0, 2, 1, 3)),
        "sh_gu": np.ascontiguousarray(
            np.stack([x["sh_w_gate"][0], x["sh_w_up"][0]], axis=1).reshape(KD, P, 2 * DE).transpose(1, 0, 2)),
        "sh_down": np.ascontiguousarray(x["sh_w_down"][0].reshape(2, P, D).transpose(1, 0, 2)),
        "pair_ids": ((np.arange(LT_)[None, :, None] * P + np.arange(P)[:, None, None]) * PAIR_STRIDE
                     + np.arange(TOPK)[None, None, :]).reshape(P, LT_ * TOPK).astype(np.int32),
        "iota64": np.tile(np.arange(E, dtype=np.float32), (P, 1)),
    }
    return {n: np.ascontiguousarray(a) for n, a in out.items()}
```

```python
from contextlib import ExitStack

import concourse.bass as bass
from concourse import mybir

ALU = mybir.AluOpType
ACT = mybir.ActivationFunctionType
AX = mybir.AxisListType
F32 = mybir.dt.float32
F32R = mybir.dt.float32r
I32 = mybir.dt.int32
U32 = mybir.dt.uint32

P = 128
D = 1024
KD = D // P
L = 512
LT_ = L // P
LC = 256
CT_ = LC // P
TA = LT_ + CT_
HEADS, HD, GROUPS, NS = 16, 64, 2, 128
D_XBC = D + 2 * GROUPS * NS
N_HY = 3 * D
EPS = 1e-6
HQ = 256
W_CHUNK = 256
RING = 4
E, TOPK, DE = 64, 6, 256
EG, TOPG = 8, 4
SCALE_R = 2.5
PAIR_STRIDE = 8
PAD_PAIR = L * PAIR_STRIDE
MAX_BLOCKS = E + (L * TOPK - E) // P
NPAIR_IT = (MAX_BLOCKS + 1) // 2
NBLK = 2 * NPAIR_IT + 2
TWO_PI = 6.283185307179586
TP_HI = 6.28125
TP_LO = TWO_PI - TP_HI
ROUND_MAGIC = 12582912.0
PI_SAFE = 3.1415925

COLS = {}
_at = 0
for _n, _w in (("c", 8), ("c_ctx", 8), ("norm1_g", 8), ("ada_b", 16), ("ssm_norm_g", 8),
               ("ssm_w", 36), ("ssm_b", 12), ("hy_w", 72), ("hy_b", 24), ("neg_t", 4), ("not_t0", 4),
               ("mlp", 6), ("jcol", 1)):
    COLS[_n] = (_at, _at + _w)
    _at += _w
N_COLS = _at
ADA_EARLY = [("ada", j) for j in range(8)]
XBC_CHUNKS = [("w_in", j) for j in range(6)]
Z_CHUNKS = [("w_in", j) for j in range(6, 10)]
HY_CHUNKS = [("w_in", 10 + j) for j in (8, 9, 10, 11, 0, 1, 2, 3, 4, 5, 6, 7)]
MERGE_CHUNKS = ([("w_in", 22 + j) for j in range(8)] + [("w_hy_out", j) for j in range(4)]
                + [("w_ssm_out", j) for j in range(4)])
MERGE_CHUNKS = [c for j in range(16) for c in (MERGE_CHUNKS[j], ("ada", 8 + j))]
WO_CHUNKS = [("w_o", j) for j in range(4)]
RING_ITEMS = (ADA_EARLY + XBC_CHUNKS + Z_CHUNKS + HY_CHUNKS + MERGE_CHUNKS + WO_CHUNKS)
AT_ADA1 = 0
AT_XBC = AT_ADA1 + 8
AT_Z = AT_XBC + 6
AT_HY = AT_Z + 4
AT_GATE = AT_HY + 12
AT_WO = AT_GATE + 32
N_RING = AT_WO + 4
assert N_RING == len(RING_ITEMS)

SSM_TILES = []
for _m in range(12):
    _kind = ("xs", _m) if _m < 8 else ("B", _m - 8) if _m < 10 else ("C", _m - 10)
    SSM_TILES.append((AT_XBC + _m // 2, _m % 2, "ssm", _m, False) + _kind)
    if _m < 10:
        SSM_TILES.append((AT_XBC + _m // 2, _m % 2, "ssm", _m, True) + _kind)
HY_TILES = []
for _i in range(24):
    _part, _m = ("v", _i) if _i < 8 else ("p0", _i - 8) if _i < 16 else ("p1", _i - 16)
    _conv = {"v": 16, "p0": 0, "p1": 8}[_part] + _m
    HY_TILES.append((AT_HY + _i // 2, _i % 2, "hy", _conv, False, _part, _m))


def col(cols, name, i=0, n=1):
    at = COLS[name][0] + i
    return cols[:, at:at + n]


def over(ap, n):
    return ap.unsqueeze(2).to_broadcast([ap.shape[0], ap.shape[1], n])


def each(ap, n):
    return ap.unsqueeze(1).to_broadcast([ap.shape[0], n, ap.shape[1]])


def build(nc, d):
    with ExitStack() as ctx:
        arena_len = 53200
        with nc.sbuf_tensor("arena", [P, arena_len], F32) as arena:
            pass
        ps = ctx.enter_context(nc.psum_tensor("ps", [P, 8, 512], F32))

        class Region:

            def __init__(self, at):
                self.at = at

            def take(self, *shape, parts=P, dtype=F32):
                n = 1
                for s in shape:
                    n *= s
                v = arena[0:parts, self.at:self.at + n]
                self.at += n
                assert self.at <= arena_len, self.at
                if dtype is not F32:
                    v = v.bitcast(dtype)
                if len(shape) == 1:
                    return v
                names = "abcd"[:len(shape)]
                sizes = {k: s for k, s in zip(names, shape)}
                return v.rearrange(f"p ({' '.join(names)}) -> p {' '.join(names)}", **sizes)

        fixed = Region(0)
        ident = fixed.take(P)
        tri_le, tri_gt, tri_ge, tri_lt = (fixed.take(P) for _ in range(4))
        ones = fixed.take(P)
        cols = fixed.take(N_COLS + N_COLS % 2)
        silu_c = fixed.take(KD, 2)
        mod = fixed.take(16, 2)
        scale1 = fixed.take(KD, 2)
        small = fixed.take(64)
        ring_at = fixed.at
        ring = fixed.take(RING, KD, W_CHUNK)
        yT = fixed.take(KD, L)
        hT = fixed.take(KD, L + LC)
        phase_at = fixed.at

        r = Region(phase_at)
        xin = r.take(TA, D)
        junk = r.take(D)
        modrow = r.take(2, W_CHUNK, parts=2)

        r = Region(phase_at)
        xs_tok = r.take(TA, D)
        BT = r.take(GROUPS, L)
        CT = r.take(GROUPS, L)
        B_tok = r.take(TA, GROUPS * NS)
        zs = r.take(LT_, D)
        xdt = r.take(2, 2, D)
        xdte = r.take(D)
        sb_in = r.take(LT_, D)
        sf_in = r.take(D)
        seg_rhs = r.take(2, 4, P)
        decay = r.take(2, 2, 4, P)
        cbm = r.take(2, LT_, GROUPS, P)
        acc = decay.rearrange("p a b c e -> p (a b c e)")[:, 0:3 * L].rearrange("p (a b) -> p a b", a=3)
        squares = r.take(512)
        y1 = r.take(D)
        y2 = r.take(D)
        w_dt = y1[:, 0:KD * 32].rearrange("p (k n) -> p k n", k=KD)
        dtT = sb_in[0:32, 0, 0:TA * P]
        dtw = xdte[:, 0:5 * 192].rearrange("p (w t n) -> p w t n", w=5, t=TA)
        dt_tok = r.take(TA, 32)
        a_tok = r.take(TA, 32)
        ecs = r.take(TA, 96)
        dte = r.take(TA, 32)
        rows_ssd = r.take(80)
        v_ss = small[:, 0:8]
        v_rstd = small[:, 8:16]
        ssd_end = r.at

        r = Region(phase_at)
        dft_f = r.take(2, LT_, 256)
        dft_i = r.take(2, 2, 512)
        filt = r.take(2, LT_, HQ)
        y4 = r.take(2, 2, 2 * HQ)
        v_tok = r.take(LT_, D)
        p0_tok = r.take(LT_, D)
        p1T = r.take(KD, L)
        spec = r.take(2, 2, 2 * HQ)
        u4 = r.take(2, 2, 2 * HQ)
        prod_a = r.take(2, 2, 2 * HQ)
        prod_b = r.take(2, 2, 2 * HQ)
        odd = r.take(2, 2 * HQ)
        w_f = r.take(2, HQ, parts=64)
        hdnT = r.take(L, parts=64)
        hy_w1 = r.take(64, parts=33)
        hy_w23 = r.take(2, 64, parts=64)
        decay_row = r.take(HQ)
        skip_row = r.take(HQ, parts=1)
        window = r.take(LT_, HQ)
        h_bwd = r.take(LT_, HQ)
        acc_hy = u4.rearrange("p a b c -> p (a b c)")[:, 0:3 * L].rearrange("p (a b) -> p a b", a=3)
        zpos = prod_a.rearrange("p a b c -> p (a b c)")[0:33, 0:L]
        sin_arg, sin_n, sin_r = (prod_a.rearrange("p a b c -> p (a b c)")[0:64, (1 + i) * L:(2 + i) * L]
                                 for i in range(3))

        r = Region(phase_at)
        gates = r.take(2, KD, L)
        mergedT_at = r.at
        mergedT = r.take(KD, L)
        x1_at = r.at
        x1 = r.take(LT_, D)
        after_x1 = r.at
        r.take(KD, L)
        rows_at = r.at
        rows = r.take(4, D)
        h2_at = r.at
        h2 = r.take(LT_, D)
        squares2 = r.take(D)
        mod_part = r.take(2, W_CHUNK)
        xmix = r.take(2, W_CHUNK)
        router_w = r.take(KD, E)
        bias_row = r.take(E)
        iota_row = r.take(E)
        pair_ids = r.take(LT_ * TOPK, dtype=I32)
        sg = r.take(2, DE)

        r = Region(ring_at)
        gu_w = r.take(3, KD, 2 * DE)
        down_w = r.take(3, 2, D)
        assert r.at <= phase_at
        h2T = r.take(KD, L)
        scores = r.take(LT_, E)
        sel = r.take(LT_, E + 8)
        grp8 = r.take(EG, 8)
        grp = r.take(16)
        grp_top = r.take(8)
        grp_rep = r.take(8)
        grp_mark = r.take(16)
        keep = r.take(8)
        drop = r.take(8)
        top8 = r.take(LT_, 8)
        top_rep = r.take(8)
        marked = r.take(E + 8)
        mask = r.take(LT_, E)
        idx_u = r.take(LT_, 8, dtype=U32)
        idx_f = r.take(LT_, 8)
        w_tok = r.take(LT_, TOPK)
        w_sum = r.take(LT_)
        counts = r.take(E)
        nblk = r.take(E)
        cend = r.take(E)
        base = r.take(E)
        rank = r.take(LT_, E)
        over_b = r.take(LT_, E)
        dest = r.take(LT_, E)
        picked = r.take(E)
        dest_k = r.take(LT_, TOPK)
        dest_i = r.take(LT_ * TOPK, dtype=I32)
        ecol = r.take(2)
        erow = r.take(P, dtype=I32, parts=1)
        nstep = r.take(4, dtype=I32, parts=1)
        nstep_f = r.take(4, parts=1)
        pad_tab = r.take(NBLK, dtype=I32)
        slots = r.take(NBLK, dtype=I32)
        tokens = r.take(NBLK, dtype=I32)
        idx_g = r.take(2, 1, dtype=I32)
        idx_s = r.take(2, 1, dtype=I32)
        assert r.at <= phase_at + 2 * KD * L, r.at
        r = Region(phase_at + 2 * KD * L)
        shg = r.take(2, L)
        hh = r.take(2, DE)
        hhT = r.take(2, 2, P)
        yo = r.take(2, D)
        assert r.at <= phase_at + 3 * KD * L, r.at
        r = Region(after_x1)
        xg = r.take(2, D)
        xgT_at = r.at
        onehot = r.take(LT_, TOPK, E)
        chosen = r.take(TOPK, E)
        y_in = Region(ring_at).take(3, TOPK, D)
        acc2 = Region(phase_at).take(2, D)

        def rounded(name, at, *shape):
            n = 1
            for s in shape:
                n *= s
            with nc.sbuf_tensor(name + "_below", [P, at], F32):
                with nc.sbuf_tensor(name, [P, n], F32R) as t:
                    pass
            names = "abcd"[:len(shape)]
            return t[:, :].rearrange(f"p ({' '.join(names)}) -> p {' '.join(names)}",
                                     **{k: s for k, s in zip(names, shape)})

        w_parts = [rounded("weight_parts_low", ring_at + 2 * KD * 2 * DE, 2, KD // 2, 2 * DE),
                   rounded("weight_parts_high", h2_at, 2, KD // 2, 2 * DE)]
        x_round = rounded("rows_rounded", xgT_at, 2, KD, P)
        x_rest = rounded("rows_rest", rows_at, 2, KD, P)
        h_parts = [[rounded(f"h_{name}_{i}", at + i * KD // 4 * L, KD // 4, L) for i in range(4)]
                   for name, at in (("rounded", mergedT_at), ("rest", h2_at))]
        t_parts = rounded("tile_parts", x1_at, 2, 2, KD, P)
        n2_row = squares2
        fin_row = h2[:, 0]
        x_out = [h2[:, 1], h2[:, 2], h2[:, 3], rows[:, 0]]

        def sem(name):
            return ctx.enter_context(nc.semaphore(name))

        s_const = sem("constants_loaded")
        s_x = sem("x_loaded")
        s_ring = [sem(f"ring_loaded_{i}") for i in range(RING)]
        s_pe = sem("phases_ended")
        s_silu_c = sem("silu_c_ready")
        s_modmm = sem("mod_rows_summed")
        s_modrow = sem("mod_row_copied")
        s_modtr = sem("mod_rows_turned")
        s_mod = sem("mod_columns_ready")
        s_ss = sem("x_squares_summed")
        s_rs = sem("x_rstd_step")
        s_xn = sem("x_normalised")
        s_htr = sem("h_turned")
        s_hT = sem("hT_written")
        s_proj = sem("tile_projected")
        s_cva = sem("conv_centre_done")
        s_cvm = sem("conv_left_done")
        s_cv = sem("conv_done")
        s_sl = sem("silu_done")
        s_tr = sem("tile_turned")
        s_te = sem("turned_tile_copied")
        s_w_dt = sem("w_dt_loaded")
        s_dtmm = sem("dt_projected")
        s_dt = sem("dt_steps")
        s_dta = sem("dt_act_steps")
        s_zmm = sem("z_projected")
        s_zc = sem("z_copied")
        s_z = sem("z_silu_done")
        s_cs = sem("cumulative_sums_done")
        s_ecs = sem("decays_ready")
        s_cb = sem("cb_done")
        s_cbm = sem("cb_masked")
        s_dte = sem("dt_to_end_ready")
        s_xe = sem("xdte_ready")
        s_st = sem("chunk_state_done")
        s_stu = sem("state_updated")
        s_xdt = sem("xdt_ready")
        s_rhs = sem("segment_rhs_ready")
        s_seg = sem("segments_summed")
        s_exp = sem("segments_exponentiated")
        s_msk = sem("decay_masked")
        s_y = sem("y_quad_done")
        s_off = sem("y_off_done")
        s_offr = sem("y_off_read")
        s_dve = sem("vector_steps")
        s_yc = sem("chunk_gated")
        s_vss = sem("gated_squares_summed")
        s_vr = sem("gated_rstd_ready")
        s_vn = sem("gated_normalised")
        s_ytr = sem("y_turned")
        s_yT = sem("yT_written")
        s_hyin = sem("filter_network_loaded")
        s_fb = sem("freq_bias_ready")
        s_mlp = sem("filter_layer_summed")
        s_arg = sem("sine_argument_ready")
        s_red = sem("sine_argument_reduced")
        s_sin = sem("sine_done")
        s_dft = sem("dft_tables_loaded")
        s_rows = sem("filter_rows_loaded")
        s_drow = sem("decay_row_positive")
        s_fmm = sem("filter_summed")
        s_win = sem("window_ready")
        s_hb = sem("backward_filter_copied")
        s_fd = sem("filter_parts_ready")
        s_fp = sem("filter_windowed")
        s_kmm = sem("filter_spectrum_summed")
        s_kod = sem("filter_odd_part_copied")
        s_kb = sem("filter_spectrum_ready")
        s_umm = sem("signal_spectrum_summed")
        s_uod = sem("signal_odd_part_copied")
        s_ub = sem("signal_spectrum_ready")
        s_pb = sem("cross_products_ready")
        s_yq = sem("product_spectrum_ready")
        s_ua = sem("product_transforms_ready")
        s_imm = sem("output_in_time_summed")
        s_iv = sem("output_in_time_gated")
        s_mp = sem("merge_tile_summed")
        s_gt = sem("gate_ready")
        s_mg = sem("merge_tile_gated")
        s_mga = sem("merged_ready")
        s_wh = sem("gate_operand_rounded")
        s_wl = sem("gate_operand_rest_ready")
        s_x1l = sem("residual_loaded")
        s_rowin = sem("row_biases_loaded")
        s_part = sem("late_modulation_part_ready")
        s_rowmm = sem("modulation_row_spread")
        s_row = sem("modulation_row_added")
        s_xmm = sem("mixer_output_summed")
        s_x1 = sem("residual_updated")
        s_ss2 = sem("residual_squares_summed")
        s_rs2 = sem("residual_rstd_step")
        s_h2 = sem("h2_ready")
        s_h2st = sem("h2_stored")
        s_h2t = sem("h2_turned")
        s_h2T = sem("h2T_written")
        s_rw = sem("router_loaded")
        s_lg = sem("logits_summed")
        s_sc0 = sem("scores_ready")
        s_msk2 = sem("expert_mask_ready")
        s_rk = sem("ranks_summed")
        s_be = sem("block_experts_ready")
        s_bt = sem("block_experts_turned")
        s_brow = sem("block_row_ready")
        s_dst = sem("slots_ready")
        s_pad = sem("slot_table_padded")
        s_scat = sem("pairs_scattered")
        s_slot = sem("slot_table_loaded")
        s_tok = sem("token_table_ready")
        s_shl = sem("shared_weights_loaded")
        s_shm = sem("shared_hidden_summed")
        s_sha = sem("shared_silu_done")
        s_shh = sem("shared_hidden_ready")
        s_shy = sem("shared_output_summed")
        s_shx = sem("shared_output_added")
        s_pi = sem("pool_index_ready")
        s_pseen = sem("waits_met")
        s_half = sem("block_half_summed")
        s_hi = sem("weights_rounded")
        s_lo = sem("weights_rest_ready")
        s_sg = sem("block_silu_done")
        s_h = sem("block_hidden_ready")
        s_th = sem("hidden_turned")
        s_hte = sem("hiddenT_copied")
        s_xt = sem("rows_turned")
        s_xea = sem("rowsT_rounded")
        s_xeb = sem("rowsT_rest_ready")
        s_ym = sem("block_output_summed")
        s_yea = sem("output_low_copied")
        s_yeb = sem("output_high_copied")
        s_fl = sem("final_gain_loaded")
        s_cw = sem("token_first_share_ready")
        s_cmb = sem("token_sum_ready")
        s_cg = sem("token_sum_gated")
        s_cx = sem("final_residual_ready")
        s_cx3 = sem("last_final_residual_ready")
        s_ss3 = sem("final_squares_summed")
        s_rs3 = sem("final_rstd_step")
        s_fo = sem("output_tile_ready")
        s_xz = sem("rows_cleared")
        s_gul = [sem(f"gate_up_loaded_{u}") for u in range(2)]
        s_dnl = [sem(f"down_loaded_{u}") for u in range(2)]
        s_xg = [sem(f"rows_gathered_{u}") for u in range(2)]
        s_sca = [sem(f"outputs_scattered_{u}") for u in range(2)]
        s_yl = [sem(f"token_outputs_loaded_{u}") for u in range(6)]
        s_out = sem("stores_done")

        def bank(b):
            return ps[:, b, :]

        h2_dram = nc.dram_tensor("h2_rows", (L, D), F32, kind="Internal").ap()
        y_dram = nc.dram_tensor("pair_outputs", (L * PAIR_STRIDE, D), F32, kind="Internal").ap()
        slot_dram = nc.dram_tensor("slot_table", (P * NBLK, 1), I32, kind="Internal").ap()

        def merge_item(n):
            return AT_GATE + 2 * (n // 2)

        def late_item(m):
            return AT_GATE + 2 * m + 1

        freed = {}
        for j in range(8):
            freed[AT_ADA1 + j] = (s_modmm, j + 1)
        for g, t in enumerate(SSM_TILES):
            freed[t[0]] = (s_proj, g + 1)
        for j in range(4):
            freed[AT_Z + j] = (s_zmm, 4 * (LT_ - 1) + j + 1)
        for g, t in enumerate(HY_TILES):
            freed[t[0]] = (s_proj, len(SSM_TILES) + g + 1)

        for n in range(32):
            freed[merge_item(n)] = (s_mp, n + 1)
        for m in range(16):
            freed[late_item(m)] = (s_part, m + 1)
        tiles = SSM_TILES + HY_TILES

        def ring_wait(eng, item):
            eng.wait_ge(s_ring[item % RING], 16 * (item // RING + 1))

        def phase_end(eng, n):
            eng.sem_inc(s_pe, 1)
            eng.wait_ge(s_pe, 4 * n)

        V = nc.vector
        SSM_TURNED = sum(t[5] != "C" for t in SSM_TILES)
        Z_AHEAD = 11
        N_SSM, N_ALL = len(SSM_TILES), len(tiles)
        HY_EARLY = 4
        DT_READY = 4
        STATE_UPDATES = [(0, 4), (0, 5), (1, 5), (1, 4), (1, 3), (1, 2), (1, 1), (0, 0), (0, 1), (0, 2)]

        def turned_before(g):
            return sum(t[5] in ("xs", "B", "v", "p0") for t in tiles[:g])

        def silu_before(g):
            return sum(t[2] == "ssm" for t in tiles[:g])

        def in_ring(t):
            return t[5] in ("xs", "v", "p0") or (t[5] == "B" and t[4])

        def conv_out(g):
            item, c, conv, ct, is_ctx, what, m = tiles[g]
            n = LC if is_ctx else L
            if in_ring(tiles[g]):
                return (acc if conv == "ssm" else acc_hy)[:, sum(map(in_ring, tiles[:g])) % 3, 0:n]
            return {"B": BT, "C": CT, "p1": p1T}[what][:, m, :]

        def project_pe(pe, g, first):
            item, c, conv, ct, is_ctx, what, m = tiles[g]
            n, t0 = (LC, L) if is_ctx else (L, 0)
            ring_wait(pe, item)
            if g >= first + 4:
                pe.wait_ge(s_cv, g - 3)
            for k in range(KD):
                mm = nc.tensor.matmul(bank(g % 4)[:, 0:n], ring[:, item % RING, k, c * P:(c + 1) * P],
                                      hT[:, k, t0:t0 + n], start=(k == 0), stop=(k == KD - 1))
            mm.then_inc(s_proj, 1)

        def conv_pe(pe, g0, g1, first, projected=0):
            for g in range(g0, g1):
                if g >= g0 + projected:
                    project_pe(pe, g, first)
                if g > g0:
                    turn_pe(pe, g - 1, first)
            turn_pe(pe, g1 - 1, first)

        def turn_pe(pe, g, first):
            t = tiles[g]
            if t[5] not in ("xs", "B", "v", "p0"):
                return
            j = turned_before(g)
            if t[2] == "ssm":
                pe.wait_ge(s_sl, silu_before(g) + 1)
            else:
                pe.wait_ge(s_cv, g + 1)
            if j >= turned_before(first) + 2:
                pe.wait_ge(s_te, j - 1)
            for i in range(CT_ if t[4] else LT_):
                src = conv_out(g)[:, i * P:(i + 1) * P]
                if t[2] == "hy":
                    src = conv_out(g).rearrange("p (h t a) -> p a h t", a=2, h=2)[:, i // 2, i % 2]
                mm = nc.tensor.transpose(bank(4 + j % 2)[:, i * P:(i + 1) * P], src, ident)
            mm.then_inc(s_tr, 1)

        def conv_act(act, g0, g1, first):
            for g in range(g0, g1):
                item, c, conv, ct, is_ctx, what, m = tiles[g]
                out = conv_out(g)
                act.wait_ge(s_proj, g + 1)
                if in_ring(tiles[g]):
                    before = [h for h in range(first, g) if in_ring(tiles[h])]
                    if len(before) >= 3:
                        act.wait_ge(s_tr, turned_before(before[-3]) + 1)
                ctn = 12 if conv == "ssm" else 24
                nc.scalar.activation(out, bank(g % 4)[:, 0:out.shape[1]], ACT.Identity,
                                     scale=col(cols, conv + "_w", ctn + ct),
                                     bias=col(cols, conv + "_b", ct)).then_inc(s_cva, 1)
                if conv == "ssm":
                    act.wait_ge(s_cv, g + 1)
                    nc.scalar.activation(out, out, ACT.Silu).then_inc(s_sl, 1)
                if g > g0:
                    turned_act(act, g - 1)
            turned_act(act, g1 - 1)

        def turned_act(act, g):
            t = tiles[g]
            if t[5] not in ("xs", "B", "v", "p0"):
                return
            j = turned_before(g)
            n, t0 = (CT_, LT_) if t[4] else (LT_, 0)
            dst = {"xs": xs_tok, "B": B_tok, "v": v_tok, "p0": p0_tok}[t[5]]
            act.wait_ge(s_tr, j + 1)
            nc.scalar.copy(dst[:, t0:t0 + n, t[6] * P:(t[6] + 1) * P],
                           bank(4 + j % 2)[:, 0:n * P].rearrange("p (t c) -> p t c", c=P)).then_inc(s_te, 1)

        def conv_dve(dve, g0, g1):
            for g in range(g0, g1):
                item, c, conv, ct, is_ctx, what, m = tiles[g]
                out, ctn = conv_out(g), 12 if conv == "ssm" else 24
                n = out.shape[1]
                dve.wait_ge(s_cva, g + 1)
                nc.vector.scalar_tensor_tensor(out[:, 1:n], bank(g % 4)[:, 0:n - 1], col(cols, conv + "_w", ct),
                                               out[:, 1:n], ALU.mult, ALU.add).then_inc(s_cvm, 1)
                dve.wait_ge(s_cvm, g + 1)
                nc.vector.scalar_tensor_tensor(out[:, 0:n - 1], bank(g % 4)[:, 1:n],
                                               col(cols, conv + "_w", 2 * ctn + ct), out[:, 0:n - 1],
                                               ALU.mult, ALU.add).then_inc(s_cv, 1)

        def mod_chunk(pe, n, item):
            ring_wait(pe, item)
            if n == 0:
                pe.wait_ge(s_silu_c, 2)
            if n >= 2:
                pe.wait_ge(s_modrow, n - 1)
            for k in range(KD):
                mm = nc.tensor.matmul(bank(n % 2)[0:2, 0:W_CHUNK], silu_c[:, k, :], ring[:, item % RING, k, :],
                                      start=(k == 0), stop=(k == KD - 1))
            mm.then_inc(s_modmm, 1)
            if n >= 1:
                mod_turn(pe, n - 1)
            if n == 7:
                mod_turn(pe, n)

        def mod_turn(pe, n):
            pe.wait_ge(s_modrow, n + 1)
            for i in range(2):
                mm = nc.tensor.transpose(bank(2)[:, 2 * (2 * n + i):2 * (2 * n + i) + 2],
                                         modrow[0:2, n % 2, i * P:(i + 1) * P], ident[0:2, 0:2])
            mm.then_inc(s_modtr, 1)

        def mod_rows_act(act, n0, n1):
            for n in range(n0, n1):
                act.wait_ge(s_modmm, n + 1)
                if n >= 2:
                    act.wait_ge(s_modtr, n - 1)
                nc.scalar.copy(modrow[0:2, n % 2, :], bank(n % 2)[0:2, 0:W_CHUNK]).then_inc(s_modrow, 1)

        def pool_xdte(pool, u, dirn, c):
            if u == 0:
                pool.wait_ge(s_dte, 1)
                pool.wait_ge(s_te, SSM_TURNED)
            else:
                pool.wait_ge(s_st, u)
            nc.gpsimd.tensor_tensor(xdte.rearrange("p (h e) -> p h e", e=HD),
                                    xs_tok[:, c].rearrange("p (h e) -> p h e", e=HD),
                                    over(dte[:, c, 16 * dirn:16 * dirn + 16], HD), ALU.mult).then_inc(s_xe, 1)

        def state_pe(pe, u):
            dirn, c = STATE_UPDATES[u]
            pe.wait_ge(s_xe, u + 1)
            if u < 7:
                if u >= 1:
                    pe.wait_ge(s_stu, u)
            else:
                pe.wait_ge(s_offr, 2 * (u - 7) + 2)
            for g in range(GROUPS):
                mm = nc.tensor.matmul(bank(4 + g), B_tok[:, c, g * NS:(g + 1) * NS],
                                      xdte[:, g * 512:(g + 1) * 512], start=True, stop=True)
            mm.then_inc(s_st, 1)

        def state_dve(dve, link, u):
            dirn, c = STATE_UPDATES[u]
            new = ps[:, 4:6, :].rearrange("p b (h e) -> p (b h) e", e=HD)
            heads = lambda ap: ap.rearrange("p (h e) -> p h e", e=HD)
            src, dst = {0: (None, sf_in), 1: (sf_in, sf_in), 2: (None, sb_in[:, 3]),
                        3: (sb_in[:, 3], sb_in[:, 3]), 4: (sb_in[:, 3], sb_in[:, 2]),
                        5: (sb_in[:, 2], sb_in[:, 1]), 6: (sb_in[:, 1], sb_in[:, 0])}.get(u, (sf_in, sf_in))
            dve.wait_ge(s_st, u + 1)
            if src is None:
                nc.vector.tensor_copy(heads(dst), new).then_inc(s_stu, 1)
            else:
                link(nc.vector.tensor_tensor(heads(dst), heads(src),
                                             over(ecs[:, c, 64 + 16 * dirn:80 + 16 * dirn], HD), ALU.mult))
                nc.vector.tensor_tensor(heads(dst), new, heads(dst), ALU.add).then_inc(s_stu, 1)
            dve.wait_ge(s_stu, u + 1)

        def off_pe(pe, c, dirn):
            if dirn == 0:
                pe.wait_ge(s_stu, 7 + c)
            else:
                pe.wait_ge(s_offr, 2 * c + 1)
            state = sb_in[:, c] if dirn else sf_in
            for g in range(GROUPS):
                mm = nc.tensor.matmul(bank(4 + g), CT[:, g, c * P:(c + 1) * P],
                                      state[:, g * 512:(g + 1) * 512], start=True, stop=True)
            mm.then_inc(s_off, 1)

        def quad_pe(pe, n):
            c, q = n // 4, n % 4
            pe.wait_ge(s_msk, 2 * n + 2)
            if q == 0:
                pe.wait_ge(s_xdt, 2 * c + 2)
                if c >= 1:
                    pe.wait_ge(s_yc, c)
            for i in range(4):
                h = 4 * q + i
                for dirn in range(2):
                    mm = nc.tensor.matmul(bank(6 + h // 8)[:, (h % 8) * HD:(h % 8 + 1) * HD],
                                          decay[:, n % 2, dirn, i, :], xdt[:, c % 2, dirn, h * HD:(h + 1) * HD],
                                          start=(dirn == 0), stop=(dirn == 1))
            mm.then_inc(s_y, 1)

        def z_pe(pe, n):
            c, q = n // 4, n % 4
            if c == 0:
                ring_wait(pe, AT_Z + q)
            if n >= 1:
                pe.wait_ge(s_zc, n)
            for k in range(KD):
                mm = nc.tensor.matmul(bank(3)[:, 0:W_CHUNK], hT[:, k, c * P:(c + 1) * P],
                                      ring[:, (AT_Z + q) % RING, k, :], start=(k == 0), stop=(k == KD - 1))
            mm.then_inc(s_zmm, 1)

        def z_act(act, n):
            c, q = n // 4, n % 4
            act.wait_ge(s_zmm, n + 1)
            nc.scalar.copy(zs[:, c, q * W_CHUNK:(q + 1) * W_CHUNK], bank(3)[:, 0:W_CHUNK]).then_inc(s_zc, 1)
            if q == 3:
                act.wait_ge(s_zc, n + 1)
                nc.scalar.activation(zs[:, c], zs[:, c], ACT.Silu).then_inc(s_z, 1)

        def gate_squares(act, c):
            act.wait_ge(s_yc, c + 1)
            for g in range(GROUPS):
                if 2 * c + g >= 1:
                    act.wait_ge(s_vss, 2 * c + g)
                nc.scalar.activation(squares, zs[:, c, g * 512:(g + 1) * 512], ACT.Square,
                                     accum_out=v_ss[:, 2 * c + g:2 * c + g + 1]).then_inc(s_vss, 1)

        HY_STEPS = [(q + i, o) for q in range(0, D // HQ, 2) for o in range(2) for i in range(2)]
        N_STEPS = len(HY_STEPS)

        def mlp_pe(pe, layer):
            if layer == 0:
                pe.wait_ge(s_hyin, 48)
                nc.tensor.matmul(bank(6)[0:64, :], hy_w1, zpos, start=True, stop=True).then_inc(s_mlp, 1)
            else:
                pe.wait_ge(s_sin, layer)
                nc.tensor.matmul(bank(6)[0:64, :], hy_w23[:, layer - 1, :], hdnT, start=True,
                                 stop=True).then_inc(s_mlp, 1)

        def mlp_act(act, layer):
            if layer == 0:
                act.wait_ge(s_fb, 1)
            act.wait_ge(s_mlp, layer + 1)
            nc.scalar.activation(sin_arg, bank(6)[0:64, :], ACT.Identity, scale=col(cols, "mlp", 3 + layer)[0:64],
                                 bias=small[0:64, 48 + layer:49 + layer]).then_inc(s_arg, 1)
            act.wait_ge(s_red, layer + 1)
            nc.scalar.activation(hdnT, sin_r, ACT.Sin).then_inc(s_sin, 1)

        def mlp_dve(dve, link, layer):
            dve.wait_ge(s_arg, layer + 1)
            link(nc.vector.tensor_scalar(sin_n, sin_arg, 1.0 / TWO_PI, ROUND_MAGIC, ALU.mult, ALU.add))
            link(nc.vector.tensor_scalar(sin_n, sin_n, ROUND_MAGIC, None, ALU.subtract))
            link(nc.vector.scalar_tensor_tensor(sin_r, sin_n, -TP_HI, sin_arg, ALU.mult, ALU.add))
            link(nc.vector.scalar_tensor_tensor(sin_r, sin_n, -TP_LO, sin_r, ALU.mult, ALU.add))
            nc.vector.tensor_scalar(sin_r, sin_r, PI_SAFE, -PI_SAFE, ALU.min, ALU.max).then_inc(s_red, 1)

        def rows_dma(act, s):
            q, o = HY_STEPS[s]
            c0 = o * D + q * HQ
            if s >= 1:
                act.wait_ge(s_fmm, s)
                act.wait_ge(s_fd, s)
                act.wait_ge(s_win, s)
            src = d["hy_w_out"].rearrange("p (a n) -> p a n", a=2)[:, :, c0:c0 + HQ]
            act.dma_start(w_f, src).then_inc(s_rows, 16)
            act.dma_start(decay_row, d["hy_decay"][c0:c0 + HQ].partition_broadcast(P)).then_inc(s_rows, 16)
            act.dma_start(skip_row, d["hy_bias"][c0:c0 + HQ].partition_broadcast(1)).then_inc(s_rows, 16)

        def filter_bank(s):
            return 4 if s < 2 else 0

        def filter_pe(pe, s):
            pe.wait_ge(s_rows, 48 * (s + 1))
            if s == 1:
                pe.wait_ge(s_kb, 1)
            if s == 2:
                pe.wait_ge(s_cv, N_ALL)
            if s >= 3:
                pe.wait_ge(s_iv, s - 2)
            for a in range(LT_):
                for way in range(2):
                    mm = nc.tensor.matmul(bank(filter_bank(s) + a)[:, way * HQ:(way + 1) * HQ], hdnT[:, a * P:(a + 1) * P],
                                          w_f[:, way, :], start=True, stop=True)
            mm.then_inc(s_fmm, 1)

        def filter_act(act, s):
            act.wait_ge(s_drow, s + 1)
            if s >= 1:
                act.wait_ge(s_fp, s)
            for a in range(LT_):
                last = nc.scalar.activation(window[:, a, :], decay_row, ACT.Exp, scale=col(cols, "neg_t", a))
            last.then_inc(s_win, 1)
            act.wait_ge(s_fmm, s + 1)
            b = filter_bank(s)
            if s >= 1:
                act.wait_ge(s_fd, s)
            nc.scalar.activation(h_bwd[:, 0, :], ps[:, b, HQ:], ACT.Identity, scale=col(cols, "not_t0", 0))
            nc.scalar.copy(h_bwd[:, 1:4, :], ps[:, b + 1:b + 4, HQ:]).then_inc(s_hb, 1)
            if s < N_STEPS - 1:
                rows_dma(act, s + 1)

        def filter_dve(dve, link, s):
            dve.wait_ge(s_rows, 48 * (s + 1))
            nc.vector.scalar_tensor_tensor(decay_row, decay_row, -1.0, decay_row, ALU.mult,
                                           ALU.max).then_inc(s_drow, 1)
            dve.wait_ge(s_hb, s + 1)
            f = ps[:, filter_bank(s):filter_bank(s) + 4, 0:HQ]
            link(nc.vector.tensor_tensor(filt[:, 0], f, h_bwd, ALU.add))
            nc.vector.tensor_tensor(filt[0:1, 0, 0, :], filt[0:1, 0, 0, :], skip_row, ALU.add)
            nc.vector.tensor_tensor(filt[:, 1], f, h_bwd, ALU.subtract).then_inc(s_fd, 1)

        def filter_pool(pool, s):
            pool.wait_ge(s_fd, s + 1)
            pool.wait_ge(s_win, s + 1)
            nc.gpsimd.tensor_tensor(filt[:, 0], filt[:, 0], window, ALU.mult)
            nc.gpsimd.tensor_tensor(filt[:, 1], filt[:, 1], window, ALU.mult).then_inc(s_fp, 1)

        def transform_pe(cos_of, sin_of, done):
            for ft in range(2):
                for par in range(2):
                    for cs, src in enumerate((cos_of, sin_of)):
                        for h in range(2):
                            a = 2 * par + h
                            mm = nc.tensor.matmul(bank(4 + 2 * ft + par)[:, cs * HQ:(cs + 1) * HQ],
                                                  dft_f[:, cs, a, ft * P:(ft + 1) * P], src[:, a, :],
                                                  start=(h == 0), stop=(h == 1))
                mm.then_inc(done, 1)

        def spectrum_pe(pe, s):
            pe.wait_ge(s_fp, s + 1)
            if s >= 1:
                pe.wait_ge(s_ub, s)
            transform_pe(filt[:, 0], filt[:, 1], s_kmm)

        def signal_pe(pe, s):
            q, o = HY_STEPS[s]
            pe.wait_ge(s_kb, s + 1)
            if s == 0:
                pe.wait_ge(s_fd, 2)
            if o:
                pe.wait_ge(s_iv, s - 1)
            v = v_tok[:, :, q * HQ:(q + 1) * HQ]
            transform_pe(v, v, s_umm)

        def odd_act(act, s, mm, read, reads, done):
            if reads:
                act.wait_ge(read, reads)
            for ft in range(2):
                act.wait_ge(mm, 2 * s + ft + 1)
                nc.scalar.copy(odd[:, ft, :], bank(5 + 2 * ft)).then_inc(done, 1)

        def mirror_dve(dve, s, copied, dst, done):
            dve.wait_ge(copied, 2 * s + 2)
            even = ps[:, 4:8, :].rearrange("p (f e) n -> p f e n", e=2)[:, :, 0, :]
            nc.vector.tensor_tensor(dst[:, 0], even, odd, ALU.add)
            nc.vector.tensor_tensor(dst[:, 1], even, odd, ALU.subtract).then_inc(done, 1)

        def product_dve(dve, s):
            u, k = u4.rearrange("p m f (c n) -> p (m f) c n", c=2), spec.rearrange(
                "p m f (c n) -> p (m f) c n", c=2)
            dve.wait_ge(s_ub, s + 1)
            if s >= 1:
                dve.wait_ge(s_yq, s)
            nc.vector.tensor_tensor(prod_a, u4, spec, ALU.mult)
            b = prod_b.rearrange("p m f (c n) -> p (m f) c n", c=2)
            nc.vector.tensor_tensor(b[:, :, 0, :], u[:, :, 0, :], k[:, :, 1, :], ALU.mult)
            nc.vector.tensor_tensor(b[:, :, 1, :], u[:, :, 1, :], k[:, :, 0, :], ALU.mult).then_inc(s_pb, 1)

        def product_pool(pool, s):
            a, b, y = (t.rearrange("p m f (c n) -> p (m f) c n", c=2) for t in (prod_a, prod_b, u4))
            pool.wait_ge(s_pb, s + 1)
            nc.gpsimd.tensor_tensor(y[:, :, 0, :], a[:, :, 0, :], a[:, :, 1, :], ALU.subtract)
            nc.gpsimd.tensor_tensor(y[:, :, 1, :], b[:, :, 0, :], b[:, :, 1, :], ALU.add).then_inc(s_yq, 1)

        def fold_dve(dve, s):
            dve.wait_ge(s_yq, s + 1)
            if s >= 1:
                dve.wait_ge(s_imm, s)
            nc.vector.tensor_tensor(y4[:, 0], u4[:, 0], u4[:, 1], ALU.add)
            nc.vector.tensor_tensor(y4[:, 1], u4[:, 0], u4[:, 1], ALU.subtract).then_inc(s_ua, 1)

        def inverse_pe(pe, s):
            q, o = HY_STEPS[s]
            pe.wait_ge(s_ua, s + 1)
            if s < N_STEPS - 2:
                pe.wait_ge(s_fd, s + 3)
            else:
                pe.wait_ge(s_iv, s)
            terms = [(cs, ft) for cs in range(2) for ft in range(2)]
            for i in range(4):
                for n, (cs, ft) in enumerate(terms):
                    par, h = i // 2, i % 2
                    y, w = y4[:, par, ft, cs * HQ:(cs + 1) * HQ], dft_i[:, cs, ft, par * 256:(par + 1) * 256]
                    if o:
                        out, lhsT, rhs = bank(h)[:, par * 256:(par + 1) * 256], y[:, h * P:(h + 1) * P], w
                    else:
                        out, lhsT, rhs = bank(i)[:, 0:HQ], w[:, h * P:(h + 1) * P], y
                    mm = nc.tensor.matmul(out, lhsT, rhs, start=(n == 0), stop=(n == 3))
            mm.then_inc(s_imm, 1)

        def inverse_dve(dve, s):
            q, o = HY_STEPS[s]
            dve.wait_ge(s_imm, s + 1)
            cs = slice(q * HQ, (q + 1) * HQ)
            if o == 0:
                nc.vector.tensor_tensor(v_tok[:, :, cs], ps[:, 0:4, 0:HQ], p0_tok[:, :, cs], ALU.mult).then_inc(s_iv, 1)
            else:
                for h in range(2):
                    p1 = p1T[:, 2 * q + h, :].rearrange("p (t a) -> p a t", a=2)
                    last = nc.vector.tensor_tensor(p1, bank(h).rearrange("p (a t) -> p a t", a=2), p1, ALU.mult)
                last.then_inc(s_iv, 1)

        GATE_SPLIT = range(6, 16)

        def merge_pe(pe, n):
            item, c = merge_item(n), n % 2
            src = hT[:, :, 0:L] if n < 16 else p1T if n < 24 else yT
            ring_wait(pe, item)
            if 4 <= n < 20:
                pe.wait_ge(s_gt, n - 3)
            elif n >= 20:
                pe.wait_ge(s_mg, n - 19)
            if n in GATE_SPLIT:
                pe.wait_ge(s_wl, 4 + n - GATE_SPLIT[0] + 1)
            for k in range(KD):
                if n in GATE_SPLIT:
                    for a, b in ((0, 0), (0, 1), (1, 0)):
                        mm = nc.tensor.matmul(bank(4 + n % 4), t_parts[:, n % 2, a, k], h_parts[b][k // 2][:, k % 2],
                                              start=(k == 0 and a + b == 0), stop=(k == KD - 1 and a == 1))
                else:
                    mm = nc.tensor.matmul(bank(4 + n % 4), ring[:, item % RING, k, c * P:(c + 1) * P], src[:, k, :],
                                          start=(k == 0), stop=(k == KD - 1))
            mm.then_inc(s_mp, 1)

        def round_h(j):
            ks = slice(2 * j, 2 * j + 2)
            nc.scalar.copy(h_parts[0][j], hT[:, ks, 0:L]).then_inc(s_wh, 1)

        def rest_h(dve, j):
            ks = slice(2 * j, 2 * j + 2)
            dve.wait_ge(s_wh, j + 1)
            V.tensor_tensor(h_parts[1][j], hT[:, ks, 0:L], h_parts[0][j].bitcast(F32),
                            ALU.subtract).then_inc(s_wl, 1)

        def gate_weights(n):
            return ring[:, merge_item(n) % RING, :, n % 2 * P:(n % 2 + 1) * P]

        def round_gate(act, n):
            ring_wait(act, merge_item(n))
            nc.scalar.copy(t_parts[:, n % 2, 0], gate_weights(n)).then_inc(s_wh, 1)

        def rest_gate(dve, n):
            dve.wait_ge(s_wh, 4 + n - GATE_SPLIT[0] + 1)
            V.tensor_tensor(t_parts[:, n % 2, 1], gate_weights(n), t_parts[:, n % 2, 0].bitcast(F32),
                            ALU.subtract).then_inc(s_wl, 1)

        def late_part(dve, link, m):
            item = late_item(m)
            ring_wait(dve, item)
            if m >= 2:
                dve.wait_ge(s_rowmm, m - 1)
            part, w = mod_part[:, m % 2, :], ring[:, item % RING]
            link(V.tensor_scalar(part, w[:, 0, :], silu_c[:, 0, 0:1], None, ALU.mult))
            for k in range(1, KD):
                last = V.scalar_tensor_tensor(part, w[:, k, :], silu_c[:, k, 0:1], part, ALU.mult, ALU.add)
                if k < KD - 1:
                    link(last)
            last.then_inc(s_part, 1)

        def late_spread(pe, m):
            pe.wait_ge(s_part, m + 1)
            if m >= 2:
                pe.wait_ge(s_row, m - 1)
            nc.tensor.matmul(bank(m % 2)[:, 0:W_CHUNK], ones, mod_part[:, m % 2, :], start=True,
                             stop=True).then_inc(s_rowmm, 1)

        def late_row(dve, link, m):
            sec, cs = m // 4, slice((m % 4) * W_CHUNK, (m % 4 + 1) * W_CHUNK)
            row, total = rows[:, sec, cs], bank(m % 2)[:, 0:W_CHUNK]
            dve.wait_ge(s_rowmm, m + 1)
            if m == 0:
                dve.wait_ge(s_rowin, 32)
            if sec == 2:
                link(V.scalar_tensor_tensor(row, total, 1.0, row, ALU.add, ALU.add))
                V.tensor_tensor(row, row, n2_row[:, cs], ALU.mult).then_inc(s_row, 1)
            else:
                V.tensor_tensor(row, total, row, ALU.add).then_inc(s_row, 1)

        def turn_h2(pe, t):
            pe.wait_ge(s_h2, t + 1)
            if t >= 1:
                pe.wait_ge(s_h2T, t)
            for k in range(KD):
                mm = nc.tensor.transpose(bank(4 + k // 4)[:, (k % 4) * P:(k % 4 + 1) * P],
                                         h2[:, t, k * P:(k + 1) * P], ident)
            mm.then_inc(s_h2t, 1)

        def logits_pe(pe, t):
            pe.wait_ge(s_rw, 64)
            pe.wait_ge(s_h2T, t + 1)
            for k in range(KD):
                mm = nc.tensor.matmul(bank(6)[:, t * E:(t + 1) * E], h2T[:, k, t * P:(t + 1) * P],
                                      router_w[:, k, :], start=(k == 0), stop=(k == KD - 1))
            mm.then_inc(s_lg, 1)

        def h2T_act(act, t):
            act.wait_ge(s_h2t, t + 1)
            nc.scalar.copy(h2T[:, :, t * P:(t + 1) * P],
                           ps[:, 4:6, :].rearrange("p b (k n) -> p (b k) n", k=4)).then_inc(s_h2T, 1)

        def scores_act(act, t):
            act.wait_ge(s_lg, t + 1)
            nc.scalar.activation(scores[:, t], bank(6)[:, t * E:(t + 1) * E], ACT.Sigmoid).then_inc(s_sc0, 1)

        SENTINEL, MARK, FAR = -3.0e38, 3.0e38, 1.0e30

        def ranks_pe(pe):
            pe.wait_ge(s_msk2, LT_)
            for t in range(LT_):
                for b in range(t + 1):
                    mm = nc.tensor.matmul(bank(5)[:, t * E:(t + 1) * E], tri_lt if b == t else ones, mask[:, b, :],
                                          start=(b == 0), stop=(b == t))
            for b in range(LT_):
                mm = nc.tensor.matmul(bank(5)[:, LT_ * E:(LT_ + 1) * E], ones, mask[:, b, :], start=(b == 0),
                                      stop=(b == LT_ - 1))
            mm.then_inc(s_rk, 1)

        def route_dve(dve, link, t):
            dve.wait_ge(s_sc0, t + 1)
            link(V.tensor_tensor(sel[:, t, 0:E], scores[:, t], bias_row, ALU.add))
            for g in range(EG):
                last = V.max(grp8[:, g, :], sel[:, t, g * 8:(g + 1) * 8])
            link(last)
            link(V.tensor_tensor(grp[:, 0:EG].unsqueeze(2), grp8[:, :, 0:1], grp8[:, :, 1:2], ALU.add))
            link(V.max(grp_top, grp[:, 0:EG]))
            link(V.tensor_copy(grp_rep[:, 0:TOPG], grp_top[:, 0:TOPG]))
            link(V.match_replace(grp_mark[:, 0:12], grp_rep, grp[:, 0:12], MARK))
            link(V.tensor_scalar(keep, grp_mark[:, 0:EG], MARK, None, ALU.is_equal))
            link(V.tensor_scalar(drop, keep, FAR, -FAR, ALU.mult, ALU.add))
            s3 = sel[:, t, 0:E].rearrange("p (g e) -> p g e", g=EG)
            link(V.tensor_tensor(s3, s3, over(keep, 8), ALU.mult))
            link(V.tensor_tensor(s3, s3, over(drop, 8), ALU.add))
            link(V.max(top8[:, t, :], sel[:, t, 0:E]))
            V.tensor_copy(top_rep[:, 0:TOPK], top8[:, t, 0:TOPK])
            link(V.max_index(idx_u[:, t, :], top8[:, t, :], sel[:, t, 0:E]))
            link(V.match_replace(marked, top_rep, sel[:, t, :], MARK))
            V.tensor_scalar(mask[:, t, :], marked[:, 0:E], MARK, None, ALU.is_equal).then_inc(s_msk2, 1)

        def turn_rows(pe, u):
            for k in range(KD):
                mm = nc.tensor.transpose(bank(3 + k // 4)[:, (k % 4) * P:(k % 4 + 1) * P],
                                         xg[:, u, k * P:(k + 1) * P], ident)
            mm.then_inc(s_xt, 1)

        def gate_up_half(pe, u, half):
            w, last = w_parts[half], KD // 2 - 1
            for k in range(KD // 2):
                kk = half * (KD // 2) + k
                nc.tensor.matmul(bank(u), x_round[:, u, kk, :], w[:, 0, k, :], start=(kk == 0), stop=False)
                nc.tensor.matmul(bank(u), x_rest[:, u, kk, :], w[:, 0, k, :], start=False, stop=False)
                mm = nc.tensor.matmul(bank(u), x_round[:, u, kk, :], w[:, 1, k, :], start=False,
                                      stop=(half == 1 and k == last))
            mm.then_inc(s_half, 1)

        def round_weights(u, half):
            return nc.scalar.copy(w_parts[half][:, 0], gu_w[:, u, half * (KD // 2):(half + 1) * (KD // 2), :])

        def rest_weights(u, half):
            return nc.vector.tensor_tensor(w_parts[half][:, 1], gu_w[:, u, half * (KD // 2):(half + 1) * (KD // 2), :],
                                           w_parts[half][:, 0].bitcast(F32), ALU.subtract)

        def turn_hidden(pe, u):
            for f in range(2):
                mm = nc.tensor.transpose(bank(2)[:, (2 * u + f) * P:(2 * u + f + 1) * P],
                                         hh[:, u, f * P:(f + 1) * P], ident)
            mm.then_inc(s_th, 1)

        def down(pe, u, half):
            for f in range(2):
                mm = nc.tensor.matmul(bank(5 + half), hhT[:, u, f, :], down_w[:, u, f, half * 512:(half + 1) * 512],
                                      start=(f == 0), stop=(f == 1))
            mm.then_inc(s_ym, 1)

        def round_rows(u):
            return nc.scalar.copy(x_round[:, u], ps[:, 3:5, :].rearrange("p b (k n) -> p (b k) n", k=4))

        def rest_rows(u):
            return nc.vector.tensor_tensor(x_rest[:, u], ps[:, 3:5, :].rearrange("p b (k n) -> p (b k) n", k=4),
                                           x_round[:, u].bitcast(F32), ALU.subtract)

        def final_act(act, t):
            if t < LT_ - 1:
                act.wait_ge(s_cx, t + 1)
            else:
                act.wait_ge(s_cx3, 1)
            if t >= 1:
                act.wait_ge(s_ss3, t)
            nc.scalar.activation(squares2, x1[:, t], ACT.Square, accum_out=small[:, 16 + t:17 + t]).then_inc(s_ss3, 1)
            act.wait_ge(s_rs3, 2 * t + 1)
            nc.scalar.activation(small[:, 32 + t:33 + t], small[:, 24 + t:25 + t], ACT.Sqrt).then_inc(s_rs3, 1)

        def final_dve(dve, link, t):
            dve.wait_ge(s_ss3, t + 1)
            V.tensor_scalar(small[:, 24 + t:25 + t], small[:, 16 + t:17 + t], 1.0 / D, EPS, ALU.mult,
                            ALU.add).then_inc(s_rs3, 1)
            dve.wait_ge(s_rs3, 2 * t + 2)
            link(V.reciprocal(small[:, 40 + t:41 + t], small[:, 32 + t:33 + t]))
            if t < LT_ - 1:
                dve.wait_ge(s_cx, t + 1)
            V.scalar_tensor_tensor(x_out[t], x1[:, t], small[:, 40 + t:41 + t], fin_row, ALU.mult,
                                   ALU.mult).then_inc(s_fo, 1)
        block = ctx.enter_context(nc.Block())

        @block.sync
        def _(sp):
            for dst, src in ((ident, d["ident"]), (tri_le, d["tri_le"]), (tri_gt, d["tri_gt"]),
                             (tri_ge, d["tri_ge"]), (tri_lt, d["tri_lt"]), (cols[:, 0:N_COLS], d["cols"])):
                sp.dma_start(dst, src).then_inc(s_const, 16)
            for item in range(RING):
                sp.dma_start(ring[:, item % RING], d["ada"][item]).then_inc(s_ring[item % RING], 16)
            for t in range(TA):
                src = d["x"][t * P:(t + 1) * P, :] if t < LT_ else d["ctx"][(t - LT_) * P:(t - LT_ + 1) * P, :]
                sp.dma_start(xin[:, t], src).then_inc(s_x, 16)
            for item in range(RING, N_RING):
                name, chunk = RING_ITEMS[item]
                sp.wait_ge(*freed[item - RING])
                sp.dma_start(ring[:, item % RING], d[name][chunk]).then_inc(s_ring[item % RING], 16)
                if item == AT_XBC + 1:
                    sp.wait_ge(s_pe, 4)
                    sp.dma_start(w_dt, d["w_dt"]).then_inc(s_w_dt, 16)
                    sp.dma_start(rows_ssd, d["rows_ssd"].partition_broadcast(P)).then_inc(s_w_dt, 16)
                if item == AT_HY + 3:
                    sp.wait_ge(s_pe, 8)
                    sp.dma_start(zpos, d["zpos"]).then_inc(s_hyin, 16)
                    sp.dma_start(hy_w1, d["hy_w1"]).then_inc(s_hyin, 16)
                    sp.dma_start(hy_w23, d["hy_w23"]).then_inc(s_hyin, 16)
                if item == AT_HY + 5:
                    sp.dma_start(dft_f, d["dft_f"]).then_inc(s_dft, 16)
                    sp.dma_start(dft_i, d["dft_i"]).then_inc(s_dft, 16)
                if item == AT_GATE + 6:
                    sp.wait_ge(s_pe, 12)
                    sp.dma_start(rows, d["ada_b_late"].rearrange("(s c) -> s c", s=4).partition_broadcast(P)).then_inc(s_rowin, 16)
                    sp.dma_start(n2_row, d["norm2_g"].partition_broadcast(P)).then_inc(s_rowin, 16)
                if item == AT_GATE + 20:
                    sp.wait_ge(s_mp, 16)
                    sp.dma_start(x1, d["x"].rearrange("(t p) c -> p t c", p=P)).then_inc(s_x1l, 16)
                    sp.dma_start(router_w, d["router_w"]).then_inc(s_rw, 16)
                    sp.dma_start(bias_row, d["router_bias"].partition_broadcast(P)).then_inc(s_rw, 16)
                    sp.dma_start(iota_row, d["iota64"]).then_inc(s_rw, 16)
                    sp.dma_start(pair_ids, d["pair_ids"]).then_inc(s_rw, 16)
            sp.wait_ge(s_mp, 32)
            sp.dma_start(gu_w[:, 2], d["sh_gu"]).then_inc(s_shl, 16)
            sp.dma_start(down_w[:, 2], d["sh_down"]).then_inc(s_shl, 16)
            for t in range(LT_):
                sp.wait_ge(s_h2, t + 1)
                sp.dma_start(h2_dram[t * P:(t + 1) * P, :], h2[:, t]).then_inc(s_h2st, 16)
            sp.wait_ge(s_brow, 2)
            steps_n = nc.sync.value_load(nstep[0:1, 0:1], min_val=1, max_val=NPAIR_IT)

            def expert_dma(dst, name, e, done):
                sp.dma_start(dst, d[name][bass.ds(e, 1)].rearrange("a p k n -> p (a k) n")).then_inc(done, 16)

            def expert_of(j):
                return nc.sync.value_load(erow[0:1, bass.ds(j, 1)], min_val=0, max_val=E - 1)

            def load_if_new(e, before, dst, name, done):
                sp.sem_inc(s_pseen, 1)
                with sp.If(before < e):
                    expert_dma(dst, name, e, done)
                with sp.Else():
                    sp.sem_inc(done, 16)

            first = [expert_of(steps_n * u) for u in range(2)]
            for u in range(2):
                expert_dma(gu_w[:, u], "w_gu", first[u], s_gul[u])
            for u in range(2):
                sp.wait_ge(s_xg[u], 16)
            for u in range(2):
                expert_dma(down_w[:, u], "w_down", first[u], s_dnl[u])
            second = [expert_of(steps_n * u + 1) for u in range(2)]
            for u in range(2):
                sp.wait_ge(s_lo, 2 * u + 2)
                load_if_new(second[u], first[u], gu_w[:, u], "w_gu", s_gul[u])
            with sp.Fori(1, NPAIR_IT) as i:
                with sp.If(i < steps_n):
                    for u in range(2):
                        e = [expert_of(i + steps_n * u + j - 1) for j in range(3)]
                        sp.wait_ge(s_ym, i * 4 + 2 * u - 2)
                        load_if_new(e[1], e[0], down_w[:, u], "w_down", s_dnl[u])
                        sp.wait_ge(s_lo, i * 4 + 2 * u + 2)
                        load_if_new(e[2], e[1], gu_w[:, u], "w_gu", s_gul[u])
            sp.wait_ge(s_lo, steps_n * 4 + 4)
            sp.sem_inc(s_pseen, 1)
            sp.wait_ge(s_half, steps_n * 4 + 2)
            sp.sem_inc(s_pseen, 1)
            for u in range(2):
                sp.wait_ge(s_sca[u], steps_n * 16)
            sp.dma_start(fin_row, d["final_g"].partition_broadcast(P)).then_inc(s_fl, 16)
            for t in range(LT_):
                if t >= 3:
                    sp.wait_ge(s_cmb, t - 2)
                for half in range(2):
                    ks = slice(half * 3, half * 3 + 3)
                    src = y_dram.rearrange("(t p k) c -> t p k c", p=P, k=PAIR_STRIDE)[t, :, ks, :]
                    sp.dma_start(y_in[:, t % 3, ks], src).then_inc(s_yl[2 * (t % 3) + half], 16)
            for t in range(LT_):
                sp.wait_ge(s_fo, t + 1)
                sp.dma_start(d["out"][t * P:(t + 1) * P, :], x_out[t]).then_inc(s_out, 16)
            sp.wait_ge(s_out, 16 * LT_)

        @block.gpsimd
        def _(pool):
            nc.gpsimd.memset(ones[:, :], 1.0).then_inc(s_const, 16)
            pool.wait_ge(s_const, 16 * 7)
            phase_end(pool, 1)
            for u, (dirn, c) in enumerate(STATE_UPDATES[:7]):
                pool_xdte(pool, u, dirn, c)
            for c in range(LT_):
                pool.wait_ge(s_te, SSM_TURNED)
                for dirn in range(2):
                    if c >= 2:
                        pool.wait_ge(s_y, 4 * (c - 1))
                    nc.gpsimd.tensor_tensor(
                        xdt[:, c % 2, dirn].rearrange("p (h e) -> p h e", e=HD),
                        xs_tok[:, c].rearrange("p (h e) -> p h e", e=HD),
                        over(dt_tok[:, c, 16 * dirn:16 * dirn + 16], HD), ALU.mult).then_inc(s_xdt, 1)
                for q in range(4):
                    n = 4 * c + q
                    if n >= 1:
                        pool.wait_ge(s_seg, 2 * n)
                    for dirn in range(2):
                        nc.gpsimd.tensor_tensor(
                            seg_rhs[:, dirn], each(tri_ge if dirn else tri_le, 4),
                            over(a_tok[:, c, 16 * dirn + 4 * q:16 * dirn + 4 * q + 4], P),
                            ALU.mult).then_inc(s_rhs, 1)
                if c < LT_ - 1:
                    pool_xdte(pool, 7 + c, 0, c)
            pool.wait_ge(s_xe, 10)
            pool.wait_ge(s_rhs, 2 * 16)
            phase_end(pool, 2)
            filter_pool(pool, 0)
            filter_pool(pool, 1)
            for s in range(N_STEPS):
                product_pool(pool, s)
                if s < N_STEPS - 2:
                    filter_pool(pool, s + 2)
            pool.wait_ge(s_yq, N_STEPS)
            phase_end(pool, 3)
            for m in range(8):
                pool.wait_ge(s_mg, 8 + m + 1)
                nc.gpsimd.tensor_tensor(mergedT[:, m, :], mergedT[:, m, :], gates[:, 1, m, :], ALU.add).then_inc(s_mga, 1)
            pool.wait_ge(s_mga, 8)
            nc.gpsimd.memset(xg, 0.0).then_inc(s_xz, 1)
            nc.gpsimd.memset(pad_tab, PAD_PAIR).then_inc(s_xz, 1)
            pool.wait_ge(s_xz, 2)
            pool.dma_start(slot_dram.rearrange("(p j) a -> p (j a)", p=P), pad_tab).then_inc(s_pad, 16)
            pool.wait_ge(s_pad, 16)
            for c in range(LT_ * TOPK):
                if c % TOPK == 0:
                    pool.wait_ge(s_dst, c // TOPK + 1)
                nc.gpsimd.indirect_dma_start(
                    out=slot_dram, out_offset=bass.IndirectOffsetOnAxis(ap=dest_i[:, c:c + 1], axis=0),
                    in_=pair_ids[:, c:c + 1], in_offset=None).then_inc(s_scat, 16)
            pool.wait_ge(s_scat, 16 * LT_ * TOPK)
            pool.dma_start(slots, slot_dram.rearrange("(p j) a -> p (j a)", p=P)).then_inc(s_slot, 16)
            pool.wait_ge(s_tok, 1)
            pool.wait_ge(s_h2st, 16 * LT_)

            def gather_rows(u):
                return nc.gpsimd.indirect_dma_start(
                    out=xg[:, u], out_offset=None, in_=h2_dram,
                    in_offset=bass.IndirectOffsetOnAxis(ap=idx_g[:, u], axis=0), bounds_check=L - 1,
                    oob_is_err=False)

            pool.wait_ge(s_brow, 2)
            steps_n = nc.gpsimd.value_load(nstep[0:1, 0:1], min_val=1, max_val=NPAIR_IT)
            for j in range(2):
                for u in range(2):
                    if j:
                        pool.wait_ge(s_xt, u + 1)
                        pool.wait_ge(s_xg[u], 16)
                    nc.gpsimd.tensor_copy(idx_g[:, u], tokens[:, bass.ds(steps_n * u + j, 1)]).then_inc(s_pi, 1)
                    pool.wait_ge(s_pi, 2 * j + u + 1)
                    gather_rows(u).then_inc(s_xg[u], 16)
            with pool.Fori(0, NPAIR_IT) as i:
                with pool.If(i < steps_n):
                    for u in range(2):
                        pool.wait_ge(s_xt, i * 2 + u + 3)
                        pool.wait_ge(s_xg[u], i * 16 + 32)
                        pool.wait_ge(s_tok, 1)
                        nc.gpsimd.tensor_copy(idx_g[:, u], tokens[:, bass.ds(i + steps_n * u + 2, 1)]).then_inc(s_pi, 1)
                        pool.wait_ge(s_pi, i * 4 + 2 * u + 5)
                        pool.sem_inc(s_pseen, 1)
                        gather_rows(u).then_inc(s_xg[u], 16)
                        pool.wait_ge(s_sca[u], i * 16)
                        pool.wait_ge(s_slot, 16)
                        nc.gpsimd.tensor_copy(idx_s[:, u], slots[:, bass.ds(i + steps_n * u, 1)]).then_inc(s_pi, 1)
                        pool.wait_ge(s_pi, i * 4 + 2 * u + 6)
                        pool.wait_ge(s_yea, i * 2 + u + 1)
                        pool.wait_ge(s_yeb, i * 2 + u + 1)
                        pool.sem_inc(s_pseen, 1)
                        nc.gpsimd.indirect_dma_start(
                            out=y_dram, out_offset=bass.IndirectOffsetOnAxis(ap=idx_s[:, u], axis=0),
                            in_=yo[:, u], in_offset=None, bounds_check=PAD_PAIR - 1,
                            oob_is_err=False).then_inc(s_sca[u], 16)
            for u in range(2):
                pool.wait_ge(s_xg[u], steps_n * 16 + 32)
                pool.sem_inc(s_pseen, 1)
            for t in range(LT_ - 1):
                pool.wait_ge(s_cmb, t + 1)
                if t >= 1:
                    pool.wait_ge(s_cx, t)
                nc.gpsimd.tensor_tensor(acc2[:, t % 2], acc2[:, t % 2], rows[:, 3], ALU.mult).then_inc(s_cg, 1)
                pool.wait_ge(s_cg, t + 1)
                nc.gpsimd.tensor_tensor(x1[:, t], x1[:, t], acc2[:, t % 2], ALU.add).then_inc(s_cx, 1)

        @block.tensor
        def _(pe):
            pe.wait_ge(s_const, 16 * 7)
            for j in range(8):
                mod_chunk(pe, j, AT_ADA1 + j)
            for k in range(KD):
                for part, (t0, n) in enumerate(((0, LT_), (LT_, CT_))):
                    g = 2 * k + part
                    if k == 0:
                        pe.wait_ge(s_xn, t0 + n)
                    if g >= 4:
                        pe.wait_ge(s_hT, g - 3)
                    for t in range(n):
                        mm = nc.tensor.transpose(bank(4 + g % 4)[:, t * P:(t + 1) * P],
                                                 xin[:, t0 + t, k * P:(k + 1) * P], ident)
                    mm.then_inc(s_htr, 1)
            pe.wait_ge(s_htr, 2 * KD)
            phase_end(pe, 1)
            pe.wait_ge(s_hT, 2 * KD)
            conv_pe(pe, 0, 8, 0)
            pe.wait_ge(s_w_dt, 32)
            for b, (t0, n) in enumerate(((0, L), (L, LC))):
                for k in range(KD):
                    mm = nc.tensor.matmul(bank(6 + b)[0:32, 0:n], w_dt[:, k, :], hT[:, k, t0:t0 + n],
                                          start=(k == 0), stop=(k == KD - 1))
            mm.then_inc(s_dtmm, 1)
            conv_pe(pe, 8, 10, 0)
            pe.wait_ge(s_dta, 1)
            for t in range(TA):
                mm = nc.tensor.transpose(bank(7)[:, LC + t * 32:LC + (t + 1) * 32], dtT[:, t * P:(t + 1) * P],
                                         ident[0:32, 0:32])
            mm.then_inc(s_dtmm, 1)
            conv_pe(pe, 10, 16, 0)
            pe.wait_ge(s_dt, DT_READY)
            for i in range(2):
                b = bank(6 + i)[:, 0:288].rearrange("p (t n) -> p t n", t=3)
                af, ab, a2 = (a_tok[:, 3 * i:3 * i + 3, cs] for cs in (slice(0, 16), slice(16, 32), slice(0, 32)))
                for at, tri, rhs in ((0, tri_le, af), (16, tri_ge, ab), (32, tri_gt, af), (48, tri_lt, ab),
                                     (64, ones, a2)):
                    mm = nc.tensor.matmul(b[:, :, at:at + rhs.shape[2]], tri, rhs, start=True, stop=True)
            mm.then_inc(s_cs, 1)
            conv_pe(pe, 16, N_SSM, 0)
            pe.wait_ge(s_sl, N_SSM)
            pe.wait_ge(s_te, SSM_TURNED)
            for c in range(LT_):
                if c >= 2:
                    pe.wait_ge(s_cbm, 2 * (c - 1))
                for g in range(GROUPS):
                    mm = nc.tensor.matmul(bank(4 + c % 2)[:, g * P:(g + 1) * P], BT[:, g, c * P:(c + 1) * P],
                                          CT[:, g, c * P:(c + 1) * P], start=True, stop=True)
                mm.then_inc(s_cb, 1)
            pe.wait_ge(s_cv, N_SSM)
            for n in range(4):
                z_pe(pe, n)
            for u in range(7):
                if u == 0:
                    pe.wait_ge(s_cbm, 2 * LT_)
                state_pe(pe, u)
                z_pe(pe, 4 + u)
            for c in range(LT_):
                pe.wait_ge(s_ecs, 2)
                for q in range(4):
                    n = 4 * c + q
                    pe.wait_ge(s_rhs, 2 * n + 2)
                    for dirn in range(2):
                        i = 2 * n + dirn
                        if i >= 3:
                            pe.wait_ge(s_exp, i - 2)
                        nc.tensor.matmul(bank(i % 3), tri_lt if dirn else tri_gt,
                                         seg_rhs[:, dirn].rearrange("p a b -> p (a b)"),
                                         start=True, stop=True).then_inc(s_seg, 1)
                    if q in (1, 2):
                        off_pe(pe, c, q - 1)
                    if q == 3 and c < LT_ - 1:
                        state_pe(pe, 7 + c)
                    if n + Z_AHEAD < 4 * LT_:
                        z_pe(pe, n + Z_AHEAD)
                    if n >= 1:
                        quad_pe(pe, n - 1)
                if c == LT_ - 1:
                    quad_pe(pe, 4 * c + 3)
            pe.wait_ge(s_exp, 8 * LT_)
            pe.wait_ge(s_zc, 4 * LT_)
            for g in range(N_SSM, N_SSM + HY_EARLY):
                project_pe(pe, g, N_SSM)
            pe.wait_ge(s_yc, LT_)
            for m in range(KD):
                if m == 0:
                    pe.wait_ge(s_vn, 2 * LT_)
                if m >= 4:
                    pe.wait_ge(s_yT, m - 3)
                for t in range(LT_):
                    mm = nc.tensor.transpose(bank(4 + m % 4)[:, t * P:(t + 1) * P], zs[:, t, m * P:(m + 1) * P], ident)
                mm.then_inc(s_ytr, 1)
            pe.wait_ge(s_ytr, KD)
            phase_end(pe, 2)
            conv_pe(pe, N_SSM, N_SSM + 4, N_SSM, HY_EARLY)
            mlp_pe(pe, 0)
            conv_pe(pe, N_SSM + 4, N_SSM + 6, N_SSM)
            mlp_pe(pe, 1)
            conv_pe(pe, N_SSM + 6, N_SSM + 8, N_SSM)
            mlp_pe(pe, 2)
            conv_pe(pe, N_SSM + 8, N_ALL - 6, N_SSM)
            pe.wait_ge(s_te, turned_before(N_ALL))
            pe.wait_ge(s_sin, 3)
            pe.wait_ge(s_dft, 32)
            filter_pe(pe, 0)
            conv_pe(pe, N_ALL - 6, N_ALL - 3, N_SSM)
            spectrum_pe(pe, 0)
            conv_pe(pe, N_ALL - 3, N_ALL - 1, N_SSM)
            filter_pe(pe, 1)
            conv_pe(pe, N_ALL - 1, N_ALL, N_SSM)
            for s in range(N_STEPS):
                signal_pe(pe, s)
                if s >= 1:
                    inverse_pe(pe, s - 1)
                if s < N_STEPS - 1:
                    spectrum_pe(pe, s + 1)
                if s < N_STEPS - 2:
                    filter_pe(pe, s + 2)
            pe.wait_ge(s_ub, N_STEPS)
            for n in range(2):
                merge_pe(pe, n)
            inverse_pe(pe, N_STEPS - 1)
            for n in range(2, 4):
                merge_pe(pe, n)
            phase_end(pe, 3)
            for n in range(4, 32):
                merge_pe(pe, n)
                if n >= 5 and n % 2:
                    late_spread(pe, (n - 5) // 2)
            for m in range(14, 16):
                late_spread(pe, m)
            pe.wait_ge(s_mga, 8)
            pe.wait_ge(s_row, 16)
            for t in range(LT_):
                for j in range(4):
                    n = 4 * t + j
                    if t == 0:
                        ring_wait(pe, AT_WO + j)
                    if n >= 4:
                        pe.wait_ge(s_x1, n - 3)
                    for k in range(KD):
                        mm = nc.tensor.matmul(bank(n % 4)[:, 0:W_CHUNK], mergedT[:, k, t * P:(t + 1) * P],
                                              ring[:, (AT_WO + j) % RING, k, :], start=(k == 0), stop=(k == KD - 1))
                    mm.then_inc(s_xmm, 1)
                    if t >= 1 and j == 2:
                        turn_h2(pe, t - 1)
                if t >= 1:
                    logits_pe(pe, t - 1)
            turn_h2(pe, LT_ - 1)
            logits_pe(pe, LT_ - 1)
            pe.wait_ge(s_shl, 32)
            pe.wait_ge(s_x1, 16)
            for f in range(4):
                for k in range(KD):
                    mm = nc.tensor.matmul(bank(f), gu_w[:, 2, k, f * P:(f + 1) * P], h2T[:, k, :],
                                          start=(k == 0), stop=(k == KD - 1))
                mm.then_inc(s_shm, 1)
                if f == 2:
                    ranks_pe(pe)
            pe.wait_ge(s_shh, 2)
            for t in range(LT_):
                for half in range(2):
                    n = 2 * t + half
                    if n == 2:
                        pe.wait_ge(s_be, 1)
                        nc.tensor.transpose(bank(4)[0:1, 0:P], ecol[:, 0:1], ident).then_inc(s_bt, 1)
                    if n >= 2:
                        pe.wait_ge(s_shx, n - 1)
                    for f in range(2):
                        mm = nc.tensor.matmul(bank(6 + half), shg[:, f, t * P:(t + 1) * P],
                                              down_w[:, 2, f, half * 512:(half + 1) * 512], start=(f == 0), stop=(f == 1))
                    mm.then_inc(s_shy, 1)
            pe.wait_ge(s_shx, 8)
            pe.wait_ge(s_brow, 2)
            for u in range(2):
                pe.wait_ge(s_xg[u], 16)
                if u:
                    pe.wait_ge(s_xeb, 1)
                turn_rows(pe, u)
            pe.wait_ge(s_xeb, 1)
            for half in range(2):
                pe.wait_ge(s_lo, half + 1)
                gate_up_half(pe, 0, half)
            steps_n = nc.tensor.value_load(nstep[0:1, 0:1], min_val=1, max_val=NPAIR_IT)
            with pe.Fori(0, NPAIR_IT) as i:
                with pe.If(i < steps_n):
                    for u in range(2):
                        pe.wait_ge(s_xeb, i * 2 + u + 2)
                        pe.wait_ge(s_lo, i * 4 + 2 * u + 3)
                        gate_up_half(pe, 1 - u, 0)
                        pe.wait_ge(s_h, i * 2 + u + 1)
                        turn_hidden(pe, u)
                        pe.wait_ge(s_lo, i * 4 + 2 * u + 4)
                        gate_up_half(pe, 1 - u, 1)
                        pe.wait_ge(s_xg[u], i * 16 + 32)
                        turn_rows(pe, u)
                        pe.wait_ge(s_hte, i * 2 + u + 1)
                        pe.wait_ge(s_dnl[u], i * 16 + 16)
                        pe.wait_ge(s_yea, i * 2 + u)
                        down(pe, u, 0)
                        pe.wait_ge(s_yeb, i * 2 + u)
                        down(pe, u, 1)

        @block.scalar
        def _(act):
            act.wait_ge(s_const, 16 * 7)
            for i, name in enumerate(("c", "c_ctx")):
                nc.scalar.activation(silu_c[:, :, i], col(cols, name, 0, KD), ACT.Silu).then_inc(s_silu_c, 1)
            mod_rows_act(act, 0, 4)
            for t in range(TA):
                act.wait_ge(s_x, 16 * TA)
                if t >= 1:
                    act.wait_ge(s_ss, t)
                nc.scalar.activation(junk, xin[:, t], ACT.Square,
                                     accum_out=small[:, 16 + t:17 + t]).then_inc(s_ss, 1)
            act.wait_ge(s_rs, 1)
            nc.scalar.activation(small[:, 32:32 + TA], small[:, 24:24 + TA], ACT.Sqrt).then_inc(s_rs, 1)
            mod_rows_act(act, 4, 8)
            act.wait_ge(s_mod, 4)
            for k in range(KD):
                for part, (t0, n) in enumerate(((0, L), (L, LC))):
                    g = 2 * k + part
                    act.wait_ge(s_htr, g + 1)
                    nc.scalar.activation(hT[:, k, t0:t0 + n], bank(4 + g % 4)[:, 0:n], ACT.Identity,
                                         scale=scale1[:, k, part:part + 1],
                                         bias=mod[:, k, part:part + 1]).then_inc(s_hT, 1)
            act.wait_ge(s_hT, 2 * KD)
            phase_end(act, 1)
            conv_act(act, 0, 8, 0)
            act.wait_ge(s_dtmm, 1)
            nc.scalar.copy(dtT, ps[0:32, 6:8, :].rearrange("p b n -> p (b n)")[:, 0:TA * P]).then_inc(s_dta, 1)
            conv_act(act, 8, 10, 0)
            act.wait_ge(s_w_dt, 32)
            act.wait_ge(s_dt, 2)
            nc.scalar.activation(dtw[:, 2], dtw[:, 1], ACT.Exp, scale=-1.0).then_inc(s_dta, 1)
            nc.scalar.activation(rows_ssd[:, 32:64], rows_ssd[:, 32:64], ACT.Exp).then_inc(s_dta, 1)
            act.wait_ge(s_dt, 3)
            nc.scalar.activation(dtw[:, 4], dtw[:, 3], ACT.Ln).then_inc(s_dta, 1)
            conv_act(act, 10, 16, 0)
            act.wait_ge(s_cs, 1)
            for i in range(2):
                nc.scalar.activation(ecs[:, 3 * i:3 * i + 3, :],
                                     bank(6 + i)[:, 0:288].rearrange("p (a b) -> p a b", a=3),
                                     ACT.Exp).then_inc(s_ecs, 1)
            conv_act(act, 16, N_SSM, 0)
            for n in range(Z_AHEAD):
                z_act(act, n)
            for n in range(4 * LT_):
                for dirn in range(2):
                    act.wait_ge(s_seg, 2 * n + dirn + 1)
                    if n >= 2:
                        act.wait_ge(s_y, n - 1)
                    nc.scalar.activation(decay[:, n % 2, dirn].rearrange("p a b -> p (a b)"),
                                         bank((2 * n + dirn) % 3), ACT.Exp).then_inc(s_exp, 1)
                if n % 4 == 1 and n >= 5:
                    gate_squares(act, n // 4 - 1)
                if n + Z_AHEAD < 4 * LT_:
                    z_act(act, n + Z_AHEAD)
            gate_squares(act, LT_ - 1)
            act.wait_ge(s_vr, 1)
            nc.scalar.activation(v_rstd, v_rstd, ACT.Sqrt).then_inc(s_vr, 1)
            for m in range(KD):
                act.wait_ge(s_ytr, m + 1)
                nc.scalar.activation(yT[:, m, :], bank(4 + m % 4), ACT.Identity,
                                     scale=col(cols, "ssm_norm_g", m)).then_inc(s_yT, 1)
            act.wait_ge(s_yT, KD)
            phase_end(act, 2)
            rows_dma(act, 0)
            conv_act(act, N_SSM, N_SSM + 4, N_SSM)
            mlp_act(act, 0)
            conv_act(act, N_SSM + 4, N_SSM + 6, N_SSM)
            mlp_act(act, 1)
            conv_act(act, N_SSM + 6, N_SSM + 8, N_SSM)
            mlp_act(act, 2)
            conv_act(act, N_SSM + 8, N_ALL - 6, N_SSM)
            filter_act(act, 0)
            conv_act(act, N_ALL - 6, N_ALL - 3, N_SSM)
            odd_act(act, 0, s_kmm, s_ub, 0, s_kod)
            conv_act(act, N_ALL - 3, N_ALL - 1, N_SSM)
            filter_act(act, 1)
            conv_act(act, N_ALL - 1, N_ALL, N_SSM)
            for s in range(N_STEPS):
                odd_act(act, s, s_umm, s_kb, s + 1, s_uod)
                if s < N_STEPS - 1:
                    odd_act(act, s + 1, s_kmm, s_ub, s + 1, s_kod)
                if s < N_STEPS - 2:
                    filter_act(act, s + 2)
            act.wait_ge(s_uod, 2 * N_STEPS)
            phase_end(act, 3)
            for n in range(16):
                if n == 4:
                    for j in range(4):
                        round_h(j)
                    for i in range(2):
                        round_gate(act, GATE_SPLIT[i])
                act.wait_ge(s_mp, n + 1)
                if n in GATE_SPLIT and n + 2 in GATE_SPLIT:
                    round_gate(act, n + 2)
                nc.scalar.activation(gates[:, n // 8, n % 8, :], bank(4 + n % 4), ACT.Sigmoid).then_inc(s_gt, 1)
            for t in range(LT_ + 1):
                if t >= 1:
                    h2T_act(act, t - 1)
                if t < LT_:
                    act.wait_ge(s_x1, 4 * t + 4)
                    if t >= 1:
                        act.wait_ge(s_ss2, t)
                    nc.scalar.activation(squares2, x1[:, t], ACT.Square,
                                         accum_out=small[:, 16 + t:17 + t]).then_inc(s_ss2, 1)
                    act.wait_ge(s_rs2, 2 * t + 1)
                    nc.scalar.activation(small[:, 32 + t:33 + t], small[:, 24 + t:25 + t],
                                         ACT.Sqrt).then_inc(s_rs2, 1)
                if t >= 1:
                    scores_act(act, t - 1)
            for f in range(2):
                act.wait_ge(s_shm, f + 1)
                nc.scalar.activation(shg[:, f, :], bank(f), ACT.Silu).then_inc(s_sha, 1)
            act.wait_ge(s_shm, 4)
            act.wait_ge(s_h2st, 16 * LT_)
            act.wait_ge(s_gul[0], 16)
            round_weights(0, 0).then_inc(s_hi, 1)
            round_weights(0, 1).then_inc(s_hi, 1)
            for u in range(2):
                act.wait_ge(s_xt, u + 1)
                round_rows(u).then_inc(s_xea, 1)
            act.wait_ge(s_gul[1], 16)
            act.wait_ge(s_half, 1)
            round_weights(1, 0).then_inc(s_hi, 1)
            act.wait_ge(s_half, 2)
            nc.scalar.activation(sg[:, 0, :], bank(0)[:, 0:DE], ACT.Silu).then_inc(s_sg, 1)
            round_weights(1, 1).then_inc(s_hi, 1)
            steps_n = nc.scalar.value_load(nstep[0:1, 0:1], min_val=1, max_val=NPAIR_IT)
            with act.Fori(0, NPAIR_IT) as i:
                with act.If(i < steps_n):
                    for u in range(2):
                        act.wait_ge(s_gul[u], i * 16 + 32)
                        act.wait_ge(s_half, i * 4 + 2 * u + 3)
                        round_weights(u, 0).then_inc(s_hi, 1)
                        act.wait_ge(s_half, i * 4 + 2 * u + 4)
                        nc.scalar.activation(sg[:, 1 - u, :], bank(1 - u)[:, 0:DE], ACT.Silu).then_inc(s_sg, 1)
                        act.wait_ge(s_xt, i * 2 + u + 3)
                        round_rows(u).then_inc(s_xea, 1)
                        round_weights(u, 1).then_inc(s_hi, 1)
                        act.wait_ge(s_ym, i * 4 + 2 * u + 1)
                        act.wait_ge(s_sca[u], i * 16)
                        nc.scalar.copy(yo[:, u, 0:512], bank(5)).then_inc(s_yea, 1)
            for t in range(LT_ + 1):
                if t < LT_:
                    act.wait_ge(s_yl[2 * (t % 3)], 16 * (t // 3 + 1))
                    if t >= 2:
                        act.wait_ge(s_cx, t - 1)
                    nc.scalar.activation(acc2[:, t % 2], y_in[:, t % 3, 0, :], ACT.Identity,
                                         scale=w_tok[:, t, 0:1]).then_inc(s_cw, 1)
                if t >= 1:
                    final_act(act, t - 1)

        @block.vector
        def _(dve):
            steps = [0]

            def link(ins):
                steps[0] += 1
                ins.then_inc(s_dve, 1)
                dve.wait_ge(s_dve, steps[0])

            dve.wait_ge(s_const, 16 * 7)
            dve.wait_ge(s_ss, TA)
            V.tensor_scalar(small[:, 24:24 + TA], small[:, 16:16 + TA], 1.0 / D, EPS, ALU.mult,
                            ALU.add).then_inc(s_rs, 1)
            dve.wait_ge(s_rs, 2)
            link(V.reciprocal(small[:, 40:40 + TA], small[:, 32:32 + TA]))
            for t in range(TA):
                V.tensor_scalar(xin[:, t], xin[:, t], small[:, 40 + t:41 + t], None, ALU.mult).then_inc(s_xn, 1)
            dve.wait_ge(s_modtr, 8)
            link(V.tensor_tensor(mod[:, 0:16, :], bank(2)[:, 0:32].rearrange("p (a b) -> p a b", b=2),
                                 over(col(cols, "ada_b", 0, 16), 2), ALU.add))
            link(V.tensor_scalar(scale1[:, :, :], mod[:, 8:16, :], 1.0, None, ALU.add))
            V.tensor_tensor(scale1[:, :, :], scale1[:, :, :], over(col(cols, "norm1_g", 0, 8), 2),
                            ALU.mult).then_inc(s_mod, 4)
            dve.wait_ge(s_mod, 4)
            dve.wait_ge(s_xn, TA)
            phase_end(dve, 1)
            conv_dve(dve, 0, 8)
            conv_dve(dve, 8, 10)
            dve.wait_ge(s_dtmm, 2)
            dve.wait_ge(s_w_dt, 32)
            V.tensor_tensor(dtw[:, 0], bank(7)[:, LC:LC + TA * 32].rearrange("p (t n) -> p t n", t=TA),
                            each(rows_ssd[:, 0:32], TA), ALU.add).then_inc(s_dt, 1)
            dve.wait_ge(s_dt, 1)
            V.scalar_tensor_tensor(dtw[:, 1], dtw[:, 0], -1.0, dtw[:, 0], ALU.mult, ALU.max).then_inc(s_dt, 1)
            dve.wait_ge(s_dta, 3)
            V.tensor_scalar(dtw[:, 3], dtw[:, 2], 1.0, None, ALU.add).then_inc(s_dt, 1)
            dve.wait_ge(s_dt, 3)
            link(V.reciprocal(dtw[:, 1], dtw[:, 3]))
            link(V.scalar_tensor_tensor(dt_tok[:, :, :], dtw[:, 3], -1.0, dtw[:, 2], ALU.add, ALU.subtract))
            link(V.tensor_tensor(dt_tok[:, :, :], dt_tok[:, :, :], dtw[:, 1], ALU.mult))
            dve.wait_ge(s_dta, 4)
            link(V.tensor_tensor(dt_tok[:, :, :], dtw[:, 4], dt_tok[:, :, :], ALU.subtract))
            link(V.scalar_tensor_tensor(dt_tok[:, :, :], dtw[:, 0], 0.0, dt_tok[:, :, :], ALU.max, ALU.add))
            V.scalar_tensor_tensor(a_tok[:, :, :], dt_tok[:, :, :], -1.0, each(rows_ssd[:, 32:64], TA),
                                   ALU.mult, ALU.mult).then_inc(s_dt, 1)
            conv_dve(dve, 10, 16)
            dve.wait_ge(s_ecs, 2)
            V.tensor_tensor(dte[:, :, :], dt_tok[:, :, :], ecs[:, :, 32:64], ALU.mult).then_inc(s_dte, 1)
            conv_dve(dve, 16, N_SSM)
            for c in range(LT_):
                dve.wait_ge(s_cb, c + 1)
                for dirn in range(2):
                    V.tensor_tensor(cbm[:, dirn, c], bank(4 + c % 2)[:, 0:GROUPS * P].rearrange(
                        "p (g l) -> p g l", g=GROUPS), each(tri_ge if dirn else tri_le, GROUPS),
                        ALU.mult).then_inc(s_cbm, 1)
            dve.wait_ge(s_cbm, 2 * LT_)
            for u in range(7):
                state_dve(dve, link, u)
            for c in range(LT_):
                for q in range(4):
                    n = 4 * c + q
                    for dirn in range(2):
                        dve.wait_ge(s_exp, 2 * n + dirn + 1)
                        V.tensor_tensor(decay[:, n % 2, dirn], decay[:, n % 2, dirn],
                                        each(cbm[:, dirn, c, q // 2], 4), ALU.mult).then_inc(s_msk, 1)
                    if q in (1, 2):
                        dve.wait_ge(s_off, 2 * c + q)
                        dst = y1 if q == 1 else y2
                        V.tensor_tensor(dst.rearrange("p (h e) -> p h e", e=HD),
                                        ps[:, 4:6, :].rearrange("p b (h e) -> p (b h) e", e=HD),
                                        over(ecs[:, c, 16 * (q - 1):16 * q], HD), ALU.mult).then_inc(s_offr, 1)
                dve.wait_ge(s_offr, 2 * c + 2)
                link(V.tensor_tensor(y1, y1, y2, ALU.add))
                if c < LT_ - 1:
                    state_dve(dve, link, 7 + c)
                link(V.tensor_tensor(y2.rearrange("p (h e) -> p h e", e=HD),
                                     xs_tok[:, c].rearrange("p (h e) -> p h e", e=HD),
                                     over(rows_ssd[:, 64:80], HD), ALU.mult))
                link(V.tensor_tensor(y1, y1, y2, ALU.add))
                dve.wait_ge(s_y, 4 * c + 4)
                link(V.tensor_tensor(y1, ps[:, 6:8, :].rearrange("p b e -> p (b e)"), y1, ALU.add))
                dve.wait_ge(s_z, c + 1)
                V.tensor_tensor(zs[:, c], y1, zs[:, c], ALU.mult).then_inc(s_yc, 1)
                dve.wait_ge(s_yc, c + 1)
            dve.wait_ge(s_vss, 2 * LT_)
            V.tensor_scalar(v_rstd, v_ss, 1.0 / 512, EPS, ALU.mult, ALU.add).then_inc(s_vr, 1)
            dve.wait_ge(s_vr, 2)
            link(V.reciprocal(v_rstd, v_rstd))
            for c in range(LT_):
                for g in range(GROUPS):
                    V.tensor_scalar(zs[:, c, g * 512:(g + 1) * 512], zs[:, c, g * 512:(g + 1) * 512],
                                    v_rstd[:, 2 * c + g:2 * c + g + 1], None, ALU.mult).then_inc(s_vn, 1)
            dve.wait_ge(s_vn, 2 * LT_)
            phase_end(dve, 2)
            V.tensor_tensor(small[0:64, 48:51], col(cols, "mlp", 0, 3)[0:64], col(cols, "mlp", 3, 3)[0:64],
                            ALU.mult).then_inc(s_fb, 1)
            conv_dve(dve, N_SSM, N_SSM + 4)
            mlp_dve(dve, link, 0)
            conv_dve(dve, N_SSM + 4, N_SSM + 6)
            mlp_dve(dve, link, 1)
            conv_dve(dve, N_SSM + 6, N_SSM + 8)
            mlp_dve(dve, link, 2)
            conv_dve(dve, N_SSM + 8, N_ALL - 6)
            filter_dve(dve, link, 0)
            conv_dve(dve, N_ALL - 6, N_ALL - 3)
            mirror_dve(dve, 0, s_kod, spec, s_kb)
            conv_dve(dve, N_ALL - 3, N_ALL - 1)
            filter_dve(dve, link, 1)
            conv_dve(dve, N_ALL - 1, N_ALL)
            for s in range(N_STEPS):
                mirror_dve(dve, s, s_uod, u4, s_ub)
                product_dve(dve, s)
                if s >= 1:
                    inverse_dve(dve, s - 1)
                fold_dve(dve, s)
                if s < N_STEPS - 1:
                    mirror_dve(dve, s + 1, s_kod, spec, s_kb)
                if s < N_STEPS - 2:
                    filter_dve(dve, link, s + 2)
            inverse_dve(dve, N_STEPS - 1)
            dve.wait_ge(s_iv, N_STEPS)
            phase_end(dve, 3)
            for j in range(4):
                rest_h(dve, j)
            for j in range(16):
                late_part(dve, link, j)
                for n in range(2 * j + 4, 2 * j + 6):
                    if n in GATE_SPLIT:
                        rest_gate(dve, n)
                for n in range(2 * j, 2 * j + 2) if j >= 8 else ():
                    i = n - 16
                    dst = mergedT[:, i, :] if i < 8 else gates[:, 1, i - 8, :]
                    dve.wait_ge(s_gt, i + 1)
                    dve.wait_ge(s_mp, n + 1)
                    V.tensor_tensor(dst, bank(4 + n % 4), gates[:, i // 8, i % 8, :], ALU.mult).then_inc(s_mg, 1)
                if j >= 1:
                    late_row(dve, link, j - 1)
            late_row(dve, link, 15)
            dve.wait_ge(s_row, 16)
            dve.wait_ge(s_x1l, 16)
            dve.wait_ge(s_rw, 64)
            dve.wait_ge(s_mga, 8)
            V.memset(grp[:, 8:16], SENTINEL)
            V.memset(grp_rep, SENTINEL)
            V.memset(top_rep, SENTINEL)
            link(V.memset(sel[:, :, E:E + 8], SENTINEL))
            for t in range(LT_):
                for j in range(4):
                    n = 4 * t + j
                    cs = slice(j * W_CHUNK, (j + 1) * W_CHUNK)
                    dve.wait_ge(s_xmm, n + 1)
                    link(V.tensor_tensor(xmix[:, n % 2, :], bank(n % 4)[:, 0:W_CHUNK], rows[:, 0, cs], ALU.mult))
                    V.tensor_tensor(x1[:, t, cs], x1[:, t, cs], xmix[:, n % 2, :], ALU.add).then_inc(s_x1, 1)
                dve.wait_ge(s_ss2, t + 1)
                V.tensor_scalar(small[:, 24 + t:25 + t], small[:, 16 + t:17 + t], 1.0 / D, EPS, ALU.mult,
                                ALU.add).then_inc(s_rs2, 1)
                dve.wait_ge(s_rs2, 2 * t + 2)
                link(V.reciprocal(small[:, 40 + t:41 + t], small[:, 32 + t:33 + t]))
                link(V.scalar_tensor_tensor(h2[:, t], x1[:, t], small[:, 40 + t:41 + t], rows[:, 2],
                                            ALU.mult, ALU.mult))
                V.tensor_tensor(h2[:, t], h2[:, t], rows[:, 1], ALU.add).then_inc(s_h2, 1)
                if t >= 1:
                    route_dve(dve, link, t - 1)
            route_dve(dve, link, LT_ - 1)
            link(V.tensor_copy(idx_f, idx_u))
            for t in range(LT_):
                link(V.tensor_tensor(onehot[:, t], each(iota_row, TOPK), over(idx_f[:, t, 0:TOPK], E), ALU.is_equal))
                link(V.tensor_tensor(chosen, onehot[:, t], each(scores[:, t], TOPK), ALU.mult))
                link(V.tensor_reduce(w_tok[:, t], chosen, AX.X, ALU.add))
            link(V.tensor_reduce(w_sum, w_tok, AX.X, ALU.add))
            link(V.reciprocal(w_sum, w_sum))
            link(V.scalar_tensor_tensor(w_tok, w_tok, SCALE_R, over(w_sum, TOPK), ALU.mult, ALU.mult))
            dve.wait_ge(s_rk, 1)
            V.tensor_copy(rank, bank(5)[:, 0:LT_ * E].rearrange("p (t e) -> p t e", e=E))
            link(V.tensor_copy(counts, bank(5)[:, LT_ * E:(LT_ + 1) * E]))
            link(V.tensor_scalar(nblk, counts, 0.0, None, ALU.is_gt))
            for b in range(1, LT_):
                link(V.scalar_tensor_tensor(nblk, counts, float(b * P), nblk, ALU.is_gt, ALU.add))
            link(V.tensor_tensor_scan(cend, ones[:, 0:E], nblk, 0.0, ALU.mult, ALU.add))
            link(V.tensor_scalar(picked, cend, col(cols, "jcol"), None, ALU.is_le))
            link(V.tensor_reduce(ecol[:, 0:1], picked, AX.X, ALU.add))
            V.tensor_scalar(ecol[:, 0:1], ecol[:, 0:1], float(E - 1), None, ALU.min).then_inc(s_be, 1)
            link(V.tensor_tensor(base, cend, nblk, ALU.subtract))
            link(V.tensor_scalar(over_b, rank, float(P), None, ALU.is_ge))
            for b in range(2, LT_):
                link(V.scalar_tensor_tensor(over_b, rank, float(b * P), over_b, ALU.is_ge, ALU.add))
            link(V.scalar_tensor_tensor(dest, over_b, float(-P), rank, ALU.mult, ALU.add))
            link(V.scalar_tensor_tensor(dest, dest, float(NBLK), over_b, ALU.mult, ALU.add))
            link(V.tensor_tensor(dest, dest, each(base, LT_), ALU.add))
            for t in range(LT_):
                link(V.tensor_tensor(chosen, onehot[:, t], each(dest[:, t], TOPK), ALU.mult))
                link(V.tensor_reduce(dest_k[:, t], chosen, AX.X, ALU.add))
                V.tensor_copy(dest_i[:, t * TOPK:(t + 1) * TOPK], dest_k[:, t]).then_inc(s_dst, 1)
            for f in range(2):
                dve.wait_ge(s_sha, f + 1)
                dve.wait_ge(s_shm, f + 3)
                V.tensor_tensor(shg[:, f, :], bank(2 + f), shg[:, f, :], ALU.mult).then_inc(s_shh, 1)
            link(V.tensor_scalar(nstep_f[:, 0:1], cend[0:1, E - 1:E], 0.5, 0.25, ALU.mult, ALU.add))
            link(V.tensor_scalar(nstep_f[:, 0:1], nstep_f[:, 0:1], ROUND_MAGIC, None, ALU.add))
            link(V.tensor_scalar(nstep_f[:, 0:1], nstep_f[:, 0:1], ROUND_MAGIC, None, ALU.subtract))
            V.tensor_copy(nstep[:, 0:1], nstep_f[:, 0:1]).then_inc(s_brow, 1)
            dve.wait_ge(s_bt, 1)
            V.tensor_copy(erow, bank(4)[0:1, 0:P]).then_inc(s_brow, 1)
            for t in range(LT_):
                for half in range(2):
                    n = 2 * t + half
                    cs = slice(half * 512, (half + 1) * 512)
                    dve.wait_ge(s_shy, n + 1)
                    link(V.tensor_tensor(acc2[:, 0, cs], bank(6 + half), rows[:, 3, cs], ALU.mult))
                    V.tensor_tensor(x1[:, t, cs], x1[:, t, cs], acc2[:, 0, cs], ALU.add).then_inc(s_shx, 1)
            dve.wait_ge(s_slot, 16)
            V.tensor_scalar(tokens, slots, 3, None, ALU.logical_shift_right).then_inc(s_tok, 1)
            for half in range(2):
                dve.wait_ge(s_hi, half + 1)
                rest_weights(0, half).then_inc(s_lo, 1)
            for u in range(2):
                dve.wait_ge(s_xea, u + 1)
                rest_rows(u).then_inc(s_xeb, 1)
            dve.wait_ge(s_hi, 3)
            rest_weights(1, 0).then_inc(s_lo, 1)
            dve.wait_ge(s_sg, 1)
            V.tensor_tensor(hh[:, 0, :], bank(0)[:, DE:2 * DE], sg[:, 0, :], ALU.mult).then_inc(s_h, 1)
            dve.wait_ge(s_hi, 4)
            rest_weights(1, 1).then_inc(s_lo, 1)
            dve.wait_ge(s_brow, 2)
            steps_n = nc.vector.value_load(nstep[0:1, 0:1], min_val=1, max_val=NPAIR_IT)
            with dve.Fori(0, NPAIR_IT) as i:
                with dve.If(i < steps_n):
                    for u in range(2):
                        dve.wait_ge(s_th, i * 2 + u + 1)
                        V.tensor_copy(hhT[:, u], bank(2)[:, 2 * u * P:(2 * u + 2) * P].rearrange(
                            "p (f n) -> p f n", f=2)).then_inc(s_hte, 1)
                        dve.wait_ge(s_hi, i * 4 + 2 * u + 5)
                        rest_weights(u, 0).then_inc(s_lo, 1)
                        dve.wait_ge(s_sg, i * 2 + u + 2)
                        V.tensor_tensor(hh[:, 1 - u, :], bank(1 - u)[:, DE:2 * DE], sg[:, 1 - u, :],
                                        ALU.mult).then_inc(s_h, 1)
                        dve.wait_ge(s_xea, i * 2 + u + 3)
                        rest_rows(u).then_inc(s_xeb, 1)
                        dve.wait_ge(s_hi, i * 4 + 2 * u + 6)
                        rest_weights(u, 1).then_inc(s_lo, 1)
                        dve.wait_ge(s_ym, i * 4 + 2 * u + 2)
                        dve.wait_ge(s_sca[u], i * 16)
                        V.tensor_copy(yo[:, u, 512:1024], bank(6)).then_inc(s_yeb, 1)
            dve.wait_ge(s_fl, 16)
            for t in range(LT_):
                a = acc2[:, t % 2]
                dve.wait_ge(s_cw, t + 1)
                for k in range(1, TOPK):
                    if k == 1:
                        dve.wait_ge(s_yl[2 * (t % 3)], 16 * (t // 3 + 1))
                    if k == 3:
                        dve.wait_ge(s_yl[2 * (t % 3) + 1], 16 * (t // 3 + 1))
                    last = V.scalar_tensor_tensor(a, y_in[:, t % 3, k, :], w_tok[:, t, k:k + 1], a, ALU.mult, ALU.add)
                    if k < TOPK - 1:
                        link(last)
                last.then_inc(s_cmb, 1)
                if t == LT_ - 1:
                    dve.wait_ge(s_cmb, LT_)
                    link(V.tensor_tensor(a, a, rows[:, 3], ALU.mult))
                    V.tensor_tensor(x1[:, t], x1[:, t], a, ALU.add).then_inc(s_cx3, 1)
                if t >= 1:
                    final_dve(dve, link, t - 1)
            final_dve(dve, link, LT_ - 1)


def kernel(**inputs):
    import numpy as np
    import concourse.bacc as bacc
    from concourse.bass_utils import run_bass_kernel_spmd

    arrays = host_arrays(inputs, np)
    nc = bacc.Bacc("TRN2", target_bir_lowering=False, num_devices=1)
    d = {n: nc.dram_tensor("in_" + n, a.shape, mybir.dt.from_np(a.dtype), kind="ExternalInput").ap()
         for n, a in arrays.items()}
    d["out"] = nc.dram_tensor("out_x", (L, D), F32, kind="ExternalOutput").ap()
    build(nc, d)
    r = run_bass_kernel_spmd(nc, [{"in_" + n: a for n, a in arrays.items()}], core_ids=[0])
    return r.results[0]["out_x"].reshape(1, L, D)


def host_arrays(inputs, np):
    x = {k: np.asarray(v) for k, v in inputs.items()}

    def chunks(w, n):
        k = w.shape[0] // P
        return np.ascontiguousarray(
            w.reshape(k, P, w.shape[1] // n, n).transpose(2, 1, 0, 3)).reshape(w.shape[1] // n, P, k, n)

    def columns(v):
        return np.ascontiguousarray(v.reshape(-1, P).T)

    w_in = x["w_in"][0]
    n_x, n_dt = D_XBC, 2 * HEADS
    pos = np.arange(L, dtype=np.float64)
    pos2 = np.concatenate([pos[0::2], pos[1::2]])
    mlp = np.zeros((P, 6), np.float32)
    for i, n in enumerate(("hy_b1", "hy_b2", "hy_b3")):
        mlp[0:64, i] = x[n][0]
    mlp[0:64, 3:6] = x["hy_freq"][0].T
    consts = {"neg_t": columns((-(pos2 / (L - 1))).astype(np.float32)),
              "not_t0": columns((pos2 > 0).astype(np.float32)),
              "mlp": mlp, "jcol": np.arange(P, dtype=np.float32)[:, None]}
    named = {"c": x["c"], "c_ctx": x["c_ctx"], "norm1_g": x["norm1_g"], "ada_b": x["ada_b"].reshape(-1)[0:2 * D],
             "ssm_norm_g": x["ssm_norm_g"], "ssm_w": x["ssm_conv_w"],
             "ssm_b": x["ssm_conv_b"], "hy_w": x["hy_conv_w"], "hy_b": x["hy_conv_b"]}
    cols = np.concatenate([consts[n] if n in consts else columns(named[n]) for n in COLS], axis=1)
    j, i = np.arange(P)[:, None], np.arange(P)[None, :]
    f32 = lambda a: np.ascontiguousarray(a, dtype=np.float32)
    omega = np.pi * (2 * pos[0:L // 2] + 1) / (2 * L)
    ang = pos2[:, None] * omega[None, :]
    fwd = np.stack([np.cos(ang), np.sin(ang)]).reshape(2, LT_, P, L // 2).transpose(2, 0, 1, 3)
    inv = (np.stack([np.cos(ang).T, np.sin(ang).T]) / L).reshape(2, 2, P, L).transpose(2, 0, 1, 3)
    bands = np.linspace(1e-4, 15, 16)
    pa = (2.0 * np.pi / L) * pos2[:, None] * bands[None, :]
    zpos = np.concatenate([(pos2 / (L - 1))[:, None], np.cos(pa), -np.sin(pa)], axis=-1)
    out = {
        "x": x["x"][0], "ctx": x["ctx"][0], "cols": cols,
        "ident": f32(j == i), "tri_le": f32(j <= i), "tri_gt": f32(j > i), "tri_ge": f32(j >= i),
        "tri_lt": f32(j < i),
        "ada": chunks(x["ada_w"][0], W_CHUNK),
        "w_in": chunks(np.concatenate([w_in[:, 0:n_x], w_in[:, n_x + n_dt:]], axis=1), W_CHUNK),
        "w_dt": chunks(w_in[:, n_x:n_x + n_dt], n_dt)[0],
        "rows_ssd": np.concatenate([x["ssm_dt_bias"].reshape(-1), x["ssm_a_log"].reshape(-1),
                                    x["ssm_d"].reshape(-1)]),
        "ada_b_late": x["ada_b"].reshape(-1)[2 * D:], "norm2_g": x["norm2_g"].reshape(-1),
        "w_hy_out": chunks(x["w_hy_out"][0], W_CHUNK), "w_ssm_out": chunks(x["w_ssm_out"][0], W_CHUNK),
        "w_o": chunks(x["w_o"][0], W_CHUNK),
        "dft_f": f32(fwd), "dft_i": f32(inv),
        "zpos": f32(zpos.T), "hy_w1": x["hy_w1"][0],
        "hy_w23": np.ascontiguousarray(np.stack([x["hy_w2"][0], x["hy_w3"][0]], axis=1)),
        "hy_w_out": x["hy_w_out"][0], "hy_decay": x["hy_decay"].reshape(-1), "hy_bias": x["hy_bias"].reshape(-1),
        "router_w": np.ascontiguousarray(x["router_w"][0].reshape(KD, P, E).transpose(1, 0, 2)),
        "router_bias": x["router_bias"][0], "final_g": x["final_g"],
        "w_gu": np.ascontiguousarray(
            np.stack([x["e_w_gate"][0], x["e_w_up"][0]], axis=2).reshape(E, KD, P, 2 * DE).transpose(0, 2, 1, 3)),
        "w_down": np.ascontiguousarray(x["e_w_down"][0].reshape(E, 2, P, D).transpose(0, 2, 1, 3)),
        "sh_gu": np.ascontiguousarray(
            np.stack([x["sh_w_gate"][0], x["sh_w_up"][0]], axis=1).reshape(KD, P, 2 * DE).transpose(1, 0, 2)),
        "sh_down": np.ascontiguousarray(x["sh_w_down"][0].reshape(2, P, D).transpose(1, 0, 2)),
        "pair_ids": ((np.arange(LT_)[None, :, None] * P + np.arange(P)[:, None, None]) * PAIR_STRIDE
                     + np.arange(TOPK)[None, None, :]).reshape(P, LT_ * TOPK).astype(np.int32),
        "iota64": np.tile(np.arange(E, dtype=np.float32), (P, 1)),
    }
    return {n: np.ascontiguousarray(a) for n, a in out.items()}
```
